# Optimizing a Trainium2 kernel written in Bass

```python
import math
import jax
import jax.numpy as jnp
from jax import lax
import numpy as np
import jax, jax.numpy as jnp

D_MODEL = 1024
BATCH = 1
SEQ = 256
DEPTH = 4

N_MIXERS = 4
HEAD_DIM = 64
RMS_EPS = 1e-6
NEG_INF = -1e30
TINY = 1e-30
Q_BLOCK = 128

A_HEADS = D_MODEL // HEAD_DIM
A_KV_HEADS = A_HEADS // 4
A_GROUP = A_HEADS // A_KV_HEADS
A_CMP_BLOCK = 32
A_CMP_STRIDE = 16
A_CMP_HIDDEN = 4 * HEAD_DIM
A_SEL_BLOCK = 64
A_SEL_TOPK = 16
A_WINDOW = 512
A_Q_BLOCK = 64
A_FORCE_BONUS = 1e3
A_SPLITS = (A_HEADS * HEAD_DIM,) + (A_KV_HEADS * HEAD_DIM,) * 6 + (3 * A_HEADS, D_MODEL)
A_IN = sum(A_SPLITS)

B_HEADS = D_MODEL // (2 * HEAD_DIM)
B_IN = 4 * D_MODEL

C_PATTERNS = ((128, 1), (512, 4), (2048, 16))
C_GROUPS = 3
C_HEADS = 4
C_V_DIM = D_MODEL // C_HEADS
C_Q_BLOCK = 64
C_IN = 2 * C_GROUPS * C_HEADS * HEAD_DIM + 2 * D_MODEL

D_HEADS = D_MODEL // HEAD_DIM
D_IN = 4 * D_MODEL


def rms_norm(x, gain):
    xf = x.astype(jnp.float32)
    y = xf * lax.rsqrt(jnp.mean(xf * xf, axis=-1, keepdims=True) + RMS_EPS)
    return (y * gain.astype(jnp.float32)).astype(x.dtype)

def alibi_slopes(n):
    return jnp.asarray(np.array([2.0 ** (-8.0 * (i + 1) / n) for i in range(n)], np.float32))

def split_cols(a, sizes):
    return jnp.split(a, [int(c) for c in np.cumsum(sizes)[:-1]], axis=-1)

def masked_softmax(s, mask):
    s = jnp.where(mask, s, NEG_INF)
    e = jnp.where(mask, jnp.exp(s - jnp.max(s, axis=-1, keepdims=True)), 0.0)
    return e / jnp.maximum(jnp.sum(e, axis=-1, keepdims=True), TINY)

def unblock(o):
    nq, b, h, t, d = o.shape
    return o.transpose(1, 0, 3, 2, 4).reshape(b, nq * t, h * d)

def nsa_mixer(u, w_in, w_out, pos_k, pos_v, w1_k, w2_k, w1_v, w2_v):
    B, S, _ = u.shape
    H, Hk, G, dh = A_HEADS, A_KV_HEADS, A_GROUP, HEAD_DIM
    L, st, SB, W, TQ = A_CMP_BLOCK, A_CMP_STRIDE, A_SEL_BLOCK, A_WINDOW, A_Q_BLOCK
    f32 = jnp.float32
    q, kc, vc, ks, vs, kw, vw, gl, z = split_cols(u @ w_in, A_SPLITS)
    q = q.reshape(B, S, Hk, G, dh).transpose(0, 2, 3, 1, 4).astype(f32) * dh ** -0.5

    def heads(a):
        return a.reshape(B, S, Hk, dh).transpose(0, 2, 1, 3).astype(f32)

    kc, vc, ks, vs, kw, vw = (heads(a) for a in (kc, vc, ks, vs, kw, vw))

    n_cmp = (S - L) // st + 1
    cidx = st * np.arange(n_cmp)[:, None] + np.arange(L)[None, :]
    cmp_end = jnp.asarray(cidx[:, -1])

    def compress(a, pos, w1, w2):
        blk = (a[:, :, cidx] + pos).reshape(B, Hk, n_cmp, L * dh)
        return jax.nn.gelu(blk @ w1) @ w2

    kcmp = compress(kc, pos_k, w1_k, w2_k).astype(f32)
    vcmp = compress(vc, pos_v, w1_v, w2_v).astype(f32)

    n_sel = S // SB
    ov = np.zeros((n_cmp, n_sel), np.float32)
    np.add.at(ov, (np.repeat(np.arange(n_cmp), L), (cidx // SB).ravel()), 1.0 / L)
    ov = jnp.asarray(ov)
    ks_blk = ks.reshape(B, Hk, n_sel, SB, dh)
    vs_blk = vs.reshape(B, Hk, n_sel, SB, dh)
    topk = min(A_SEL_TOPK, n_sel)
    bi = jnp.arange(B)[:, None, None, None]
    hi = jnp.arange(Hk)[None, :, None, None]

    kw_p = jnp.pad(kw, ((0, 0), (0, 0), (W, 0), (0, 0)))
    vw_p = jnp.pad(vw, ((0, 0), (0, 0), (W, 0), (0, 0)))
    slopes = alibi_slopes(H).reshape(1, Hk, G, 1, 1)

    def block(i):
        q0 = i * TQ
        t = q0 + jnp.arange(TQ)
        qb = lax.dynamic_slice_in_dim(q, q0, TQ, axis=3)
        dist = t[:, None] - cmp_end[None, :]
        p_c = masked_softmax(jnp.einsum('bhgqd,bhnd->bhgqn', qb, kcmp) - slopes * dist.astype(f32), dist >= 0)
        o_c = jnp.einsum('bhgqn,bhnd->bhgqd', p_c, vcmp)
        imp = jnp.einsum('bhgqn,nj->bhqj', p_c, ov)
        cur = (t // SB)[:, None]
        j = jnp.arange(n_sel)[None, :]
        forced = (j == 0) | (j == cur) | (j == cur - 1)
        imp = jnp.where(j > cur, -1.0, imp + jnp.where(forced, A_FORCE_BONUS, 0.0))
        _, sel = lax.top_k(imp, topk)
        ksel = ks_blk[bi, hi, sel].reshape(B, Hk, TQ, topk * SB, dh)
        vsel = vs_blk[bi, hi, sel].reshape(B, Hk, TQ, topk * SB, dh)
        pos = (sel[..., None] * SB + jnp.arange(SB)).reshape(B, Hk, TQ, topk * SB)
        dist = (t[:, None] - pos)[:, :, None]
        p_s = masked_softmax(jnp.einsum('bhgqd,bhqkd->bhgqk', qb, ksel) - slopes * dist.astype(f32), dist >= 0)
        o_s = jnp.einsum('bhgqk,bhqkd->bhgqd', p_s, vsel)
        kwin = lax.dynamic_slice_in_dim(kw_p, q0, TQ + W, axis=2)
        vwin = lax.dynamic_slice_in_dim(vw_p, q0, TQ + W, axis=2)
        spos = q0 - W + jnp.arange(TQ + W)
        dist = t[:, None] - spos[None, :]
        mask = (dist >= 0) & (dist < W) & (spos[None, :] >= 0)
        p_w = masked_softmax(jnp.einsum('bhgqd,bhkd->bhgqk', qb, kwin) - slopes * dist.astype(f32), mask)
        o_w = jnp.einsum('bhgqk,bhkd->bhgqd', p_w, vwin)
        return jnp.stack([o_c, o_s, o_w])

    outs = lax.map(block, jnp.arange(S // TQ))
    outs = outs.transpose(1, 2, 0, 5, 3, 4, 6).reshape(3, B, S, H, dh)
    gates = jax.nn.sigmoid(gl.astype(f32)).reshape(B, S, 3, H).transpose(2, 0, 1, 3)[..., None]
    o = jnp.sum(gates * outs, axis=0).reshape(B, S, H * dh)
    return (o.astype(u.dtype) * jax.nn.silu(z)) @ w_out

def diff_mixer(u, w_in, w_out, lam, sub_gain, lambda_init):
    B, S, _ = u.shape
    H, dh, TQ = B_HEADS, HEAD_DIM, Q_BLOCK
    f32 = jnp.float32
    q, k, v, z = split_cols(u @ w_in, (D_MODEL,) * 4)
    q = q.reshape(B, S, H, 2, dh).transpose(0, 2, 3, 1, 4).astype(f32) * dh ** -0.5
    k = k.reshape(B, S, H, 2, dh).transpose(0, 2, 3, 1, 4).astype(f32)
    v = v.reshape(B, S, H, 2 * dh).transpose(0, 2, 1, 3).astype(f32)
    lamf = lam.astype(f32)
    lam_full = jnp.exp(jnp.sum(lamf[0] * lamf[1])) - jnp.exp(jnp.sum(lamf[2] * lamf[3])) + lambda_init
    slopes = alibi_slopes(H).reshape(1, H, 1, 1, 1)
    kpos = jnp.arange(S)

    def block(i):
        q0 = i * TQ
        t = q0 + jnp.arange(TQ)
        qb = lax.dynamic_slice_in_dim(q, q0, TQ, axis=3)
        dist = t[:, None] - kpos[None, :]
        p = masked_softmax(jnp.einsum('bhmqd,bhmkd->bhmqk', qb, k) - slopes * dist.astype(f32), dist >= 0)
        a = p[:, :, 0] - lam_full * p[:, :, 1]
        return jnp.einsum('bhqk,bhkd->bhqd', a, v)

    o = lax.map(block, jnp.arange(S // TQ))
    o = o.transpose(1, 0, 3, 2, 4).reshape(B, S, H, 2 * dh)
    o = (rms_norm(o, sub_gain) * (1.0 - lambda_init)).reshape(B, S, H * 2 * dh)
    return (o.astype(u.dtype) * jax.nn.silu(z)) @ w_out

def dilated_mixer(u, w_in, w_out):
    B, S, _ = u.shape
    G, Hg, dh, dv, TQ = C_GROUPS, C_HEADS, HEAD_DIM, C_V_DIM, C_Q_BLOCK
    f32 = jnp.float32
    qk = G * Hg * dh
    q, k, v, z = split_cols(u @ w_in, (qk, qk, D_MODEL, D_MODEL))
    q = q.reshape(B, S, G, Hg, dh).transpose(2, 0, 3, 1, 4).astype(f32) * dh ** -0.5
    k = k.reshape(B, S, G, Hg, dh).transpose(2, 0, 3, 1, 4).astype(f32)
    v = v.reshape(B, S, Hg, dv).transpose(0, 2, 1, 3).astype(f32)
    slopes = alibi_slopes(G * Hg).reshape(G, Hg)

    def block(i):
        q0 = i * TQ
        t = q0 + jnp.arange(TQ)
        outs, lses = [], []
        for g, (w, d) in enumerate(C_PATTERNS):
            offs = d * np.arange(w // d + 1)
            p = t[:, None] - offs[None, :]
            valid = p >= 0
            pc = jnp.maximum(p, 0)
            kg = jnp.take(k[g], pc, axis=2)
            vg = jnp.take(v, pc, axis=2)
            qb = lax.dynamic_slice_in_dim(q[g], q0, TQ, axis=2)
            s = jnp.einsum('bhqd,bhqnd->bhqn', qb, kg) - slopes[g][None, :, None, None] * offs.astype(np.float32)
            s = jnp.where(valid, s, NEG_INF)
            m = jnp.max(s, axis=-1, keepdims=True)
            e = jnp.where(valid, jnp.exp(s - m), 0.0)
            l = jnp.sum(e, axis=-1, keepdims=True)
            outs.append(jnp.einsum('bhqn,bhqnd->bhqd', e / l, vg))
            lses.append(m[..., 0] + jnp.log(l[..., 0]))
        wts = jax.nn.softmax(jnp.stack(lses), axis=0)[..., None]
        return jnp.sum(wts * jnp.stack(outs), axis=0)

    o = unblock(lax.map(block, jnp.arange(S // TQ)))
    return (o.astype(u.dtype) * jax.nn.silu(z)) @ w_out

def stick_mixer(u, w_in, w_out):
    B, S, _ = u.shape
    H, dh, TQ = D_HEADS, HEAD_DIM, Q_BLOCK
    f32 = jnp.float32
    q, k, v, z = split_cols(u @ w_in, (D_MODEL,) * 4)
    q = q.reshape(B, S, H, dh).transpose(0, 2, 1, 3).astype(f32) * dh ** -0.5
    k = k.reshape(B, S, H, dh).transpose(0, 2, 1, 3).astype(f32)
    v = v.reshape(B, S, H, dh).transpose(0, 2, 1, 3).astype(f32)
    kpos = jnp.arange(S)

    def block(i):
        q0 = i * TQ
        t = q0 + jnp.arange(TQ)
        qb = lax.dynamic_slice_in_dim(q, q0, TQ, axis=2)
        logits = jnp.einsum('bhqd,bhkd->bhqk', qb, k)
        causal = kpos[None, :] < t[:, None]
        log_om = jnp.where(causal, jax.nn.log_sigmoid(-logits), 0.0)
        between = lax.cumsum(log_om, axis=3, reverse=True) - log_om
        a = jnp.where(causal, jnp.exp(jax.nn.log_sigmoid(logits) + between), 0.0)
        return jnp.einsum('bhqk,bhkd->bhqd', a, v)

    o = unblock(lax.map(block, jnp.arange(S // TQ)))
    return (o.astype(u.dtype) * jax.nn.silu(z)) @ w_out

def first_inputs(seed: int = 0) -> dict:
    key = jax.random.key(seed)
    ks = jax.random.split(key, 20)
    n_a = (DEPTH + 3) // 4
    n_b = (DEPTH + 2) // 4
    n_c = (DEPTH + 1) // 4
    n_d = DEPTH // 4
    L, dh = A_CMP_BLOCK, HEAD_DIM

    def dense(k, shape, fan_in):
        return jax.random.normal(k, shape, jnp.float32) * fan_in ** -0.5

    def gain(k, shape):
        return 1.0 + 0.02 * jax.random.normal(k, shape, jnp.float32)

    return {
        'x': jax.random.normal(ks[0], (BATCH, SEQ, D_MODEL), jnp.float32),
        'norm_pre': gain(ks[1], (DEPTH, D_MODEL)),
        'norm_post': gain(ks[2], (DEPTH, D_MODEL)),
        'a_w_in': dense(ks[3], (n_a, D_MODEL, A_IN), D_MODEL),
        'a_w_out': dense(ks[4], (n_a, D_MODEL, D_MODEL), D_MODEL),
        'a_cmp_pos_k': 0.1 * jax.random.normal(ks[5], (n_a, L, dh), jnp.float32),
        'a_cmp_pos_v': 0.1 * jax.random.normal(ks[6], (n_a, L, dh), jnp.float32),
        'a_cmp_w1_k': dense(ks[7], (n_a, L * dh, A_CMP_HIDDEN), L * dh),
        'a_cmp_w2_k': dense(ks[8], (n_a, A_CMP_HIDDEN, dh), A_CMP_HIDDEN),
        'a_cmp_w1_v': dense(ks[9], (n_a, L * dh, A_CMP_HIDDEN), L * dh),
        'a_cmp_w2_v': dense(ks[10], (n_a, A_CMP_HIDDEN, dh), A_CMP_HIDDEN),
        'b_w_in': dense(ks[11], (n_b, D_MODEL, B_IN), D_MODEL),
        'b_w_out': dense(ks[12], (n_b, D_MODEL, D_MODEL), D_MODEL),
        'b_lambda': 0.1 * jax.random.normal(ks[13], (n_b, 4, dh), jnp.float32),
        'b_sub_gain': gain(ks[14], (n_b, 2 * dh)),
        'c_w_in': dense(ks[15], (n_c, D_MODEL, C_IN), D_MODEL),
        'c_w_out': dense(ks[16], (n_c, D_MODEL, D_MODEL), D_MODEL),
        'd_w_in': dense(ks[17], (n_d, D_MODEL, D_IN), D_MODEL),
        'd_w_out': dense(ks[18], (n_d, D_MODEL, D_MODEL), D_MODEL),
    }

def first_block(x, norm_pre, norm_post, a_w_in, a_w_out, a_cmp_pos_k, a_cmp_pos_v, a_cmp_w1_k, a_cmp_w2_k,
              a_cmp_w1_v, a_cmp_w2_v, b_w_in, b_w_out, b_lambda, b_sub_gain, c_w_in, c_w_out, d_w_in, d_w_out):
    h = x
    for i in range(DEPTH):
        m, j = i % N_MIXERS, i // N_MIXERS
        u = rms_norm(h, norm_pre[i])
        if m == 0:
            y = nsa_mixer(u, a_w_in[j], a_w_out[j], a_cmp_pos_k[j], a_cmp_pos_v[j],
                          a_cmp_w1_k[j], a_cmp_w2_k[j], a_cmp_w1_v[j], a_cmp_w2_v[j])
        elif m == 1:
            lambda_init = 0.8 - 0.6 * math.exp(-0.3 * i)
            y = diff_mixer(u, b_w_in[j], b_w_out[j], b_lambda[j], b_sub_gain[j], lambda_init)
        elif m == 2:
            y = dilated_mixer(u, c_w_in[j], c_w_out[j])
        else:
            y = stick_mixer(u, d_w_in[j], d_w_out[j])
        h = h + rms_norm(y, norm_post[i])
    return h


DEPTH_2 = 1

GRID_W = 64
NA_HEADS = 8
NA_HEAD_DIM = 64
NA_WIN_ROWS_MAX = 8
NA_WIN_COLS = 16
NA_WIDTH = NA_HEADS * NA_HEAD_DIM
MLA_HEADS = 8
MLA_Q_RANK = 256
MLA_KV_RANK = 128
MLA_NOPE_DIM = 64
MLA_ROPE_DIM = 32
MLA_V_DIM = 64
MLA_QK_DIM = MLA_NOPE_DIM + MLA_ROPE_DIM
MLA_WIDTH = MLA_HEADS * MLA_V_DIM
ROPE_THETA = 10000.0
ATTN_BLOCK = 128
IN_SPLITS = (NA_WIDTH, NA_WIDTH, NA_WIDTH, MLA_Q_RANK, MLA_KV_RANK, MLA_ROPE_DIM, D_MODEL, D_MODEL)
IN_COLS = 3 * NA_WIDTH + MLA_Q_RANK + MLA_KV_RANK + MLA_ROPE_DIM + 2 * D_MODEL
N_EXPERTS = 64
TOP_K = 8
N_GROUPS = 8
TOPK_GROUPS = 4
EXPERT_FF = 256
SHARED_FF = 256
ROUTED_SCALE = 2.5
MOE_CHUNK = 128
EPS = 1e-6
NEG_BIG = -1e30


def rms_norm_2(x, g):
    xf = x.astype(jnp.float32)
    y = xf * lax.rsqrt(jnp.mean(xf * xf, axis=-1, keepdims=True) + EPS)
    return (y * g.astype(jnp.float32)).astype(x.dtype)

def apply_rope(x, positions):
    half = x.shape[-1] // 2
    inv_freq = ROPE_THETA ** (-jnp.arange(half, dtype=jnp.float32) / half)
    ang = positions.astype(jnp.float32)[:, :, None, None] * inv_freq
    cos, sin = jnp.cos(ang), jnp.sin(ang)
    xf = x.astype(jnp.float32)
    x1, x2 = xf[..., :half], xf[..., half:]
    return jnp.concatenate([x1 * cos - x2 * sin, x2 * cos + x1 * sin], axis=-1).astype(x.dtype)

def neighbourhood_attention(q, k, v, rpb):
    B, S, H, Dh = q.shape
    R = S // GRID_W
    kh = min(NA_WIN_ROWS_MAX, R)
    to_grid = lambda t: t.reshape(B, R, GRID_W, H, Dh).transpose(0, 3, 1, 2, 4)
    qg, kg, vg = to_grid(q), to_grid(k), to_grid(v)
    rows = jnp.arange(R)
    row_start = jnp.clip(rows - kh // 2, 0, R - kh)
    key_rows = row_start[:, None] + jnp.arange(kh)[None, :]
    kb = kg[:, :, key_rows]
    vb = vg[:, :, key_rows]
    s = jnp.einsum('bhrqd,bhrjkd->bhrqjk', qg, kb).astype(jnp.float32) * (Dh ** -0.5)
    cols = jnp.arange(GRID_W)
    col_start = jnp.clip(cols - NA_WIN_COLS // 2, 0, GRID_W - NA_WIN_COLS)
    in_win = (cols[None, :] >= col_start[:, None]) & (cols[None, :] < col_start[:, None] + NA_WIN_COLS)
    dr = key_rows - rows[:, None]
    dc = jnp.clip(cols[None, :] - cols[:, None], -(NA_WIN_COLS - 1), NA_WIN_COLS - 1)
    bias = rpb[:, dr[:, None, :, None] + (NA_WIN_ROWS_MAX - 1),
               dc[None, :, None, :] + (NA_WIN_COLS - 1)]
    s = s + bias.astype(jnp.float32)[None]
    s = jnp.where(in_win[:, None, :], s, NEG_BIG)
    p = jax.nn.softmax(s.reshape(B, H, R, GRID_W, kh * GRID_W), axis=-1)
    p = p.reshape(B, H, R, GRID_W, kh, GRID_W).astype(v.dtype)
    o = jnp.einsum('bhrqjk,bhrjkd->bhrqd', p, vb)
    return o.transpose(0, 2, 3, 1, 4).reshape(B, S, H * Dh)

def blocked_full_attention(q, k, v):
    B, S, H, Dqk = q.shape
    Dv = v.shape[-1]
    nb = S // ATTN_BLOCK
    qb = q.reshape(B, nb, ATTN_BLOCK, H, Dqk).transpose(1, 0, 2, 3, 4)
    scale = Dqk ** -0.5

    def one_block(q_blk):
        s = jnp.einsum('bqhd,bkhd->bhqk', q_blk, k).astype(jnp.float32) * scale
        p = jax.nn.softmax(s, axis=-1).astype(v.dtype)
        return jnp.einsum('bhqk,bkhd->bqhd', p, v)

    o = lax.map(one_block, qb)
    return o.transpose(1, 0, 2, 3, 4).reshape(B, S, H * Dv)

def moe_ffn(h, w_router, e_bias, w_eg, w_eu, w_ed, w_sg, w_su, w_sd):
    B, S, D = h.shape
    t = h.reshape(-1, D)
    T = t.shape[0]
    scores = jax.nn.sigmoid((t @ w_router).astype(jnp.float32))
    sel = scores + e_bias.astype(jnp.float32)
    grp = sel.reshape(T, N_GROUPS, N_EXPERTS // N_GROUPS)
    grp_score = jnp.sum(lax.top_k(grp, 2)[0], axis=-1)
    _, gidx = lax.top_k(grp_score, TOPK_GROUPS)
    gmask = jnp.sum(jax.nn.one_hot(gidx, N_GROUPS, dtype=jnp.float32), axis=-2)
    emask = jnp.repeat(gmask, N_EXPERTS // N_GROUPS, axis=-1)
    sel = jnp.where(emask > 0, sel, -jnp.inf)
    _, eidx = lax.top_k(sel, TOP_K)
    w = jnp.take_along_axis(scores, eidx, axis=-1)
    w = w / jnp.sum(w, axis=-1, keepdims=True) * ROUTED_SCALE
    gates = jnp.sum(jax.nn.one_hot(eidx, N_EXPERTS, dtype=jnp.float32) * w[..., None], axis=-2)
    tc = t.reshape(-1, MOE_CHUNK, D)
    gc = gates.reshape(-1, MOE_CHUNK, N_EXPERTS).astype(t.dtype)

    def expert_chunk(args):
        xc, gch = args
        hg = jnp.einsum('cd,edf->cef', xc, w_eg)
        hu = jnp.einsum('cd,edf->cef', xc, w_eu)
        a = jax.nn.silu(hg) * hu * gch[..., None]
        return jnp.einsum('cef,efd->cd', a, w_ed)

    routed = lax.map(expert_chunk, (tc, gc)).reshape(T, D)
    shared = (jax.nn.silu(t @ w_sg) * (t @ w_su)) @ w_sd
    return (routed + shared).reshape(B, S, D)

def second_inputs(seed: int = 0) -> dict:
    key = jax.random.key(seed)
    ks = iter(jax.random.split(key, 32))
    f32 = jnp.float32
    nrm = lambda shape, s: jax.random.normal(next(ks), shape, f32) * s
    gain = lambda shape: 1.0 + 0.05 * jax.random.normal(next(ks), shape, f32)
    L, D, E, F = DEPTH_2, D_MODEL, N_EXPERTS, EXPERT_FF
    x = jax.random.normal(next(ks), (BATCH, SEQ, D), f32)
    c = jax.random.normal(next(ks), (BATCH, D), f32)
    positions = jnp.broadcast_to(jnp.arange(SEQ, dtype=jnp.int32)[None, :], (BATCH, SEQ))
    return {
        "x": x,
        "c": c,
        "positions": positions,
        "w_ada": nrm((L, D, 6 * D), 0.3 * D ** -0.5),
        "b_ada": nrm((L, 6 * D), 0.02),
        "g_norm1": gain((L, D)),
        "w_in": nrm((L, D, IN_COLS), D ** -0.5),
        "g_na_q": gain((L, NA_HEAD_DIM)),
        "g_na_k": gain((L, NA_HEAD_DIM)),
        "na_rpb": nrm((L, NA_HEADS, 2 * NA_WIN_ROWS_MAX - 1, 2 * NA_WIN_COLS - 1), 0.1),
        "g_q_lat": gain((L, MLA_Q_RANK)),
        "w_uq": nrm((L, MLA_Q_RANK, MLA_HEADS * MLA_QK_DIM), MLA_Q_RANK ** -0.5),
        "g_kv_lat": gain((L, MLA_KV_RANK)),
        "w_ukv": nrm((L, MLA_KV_RANK, MLA_HEADS * (MLA_NOPE_DIM + MLA_V_DIM)), MLA_KV_RANK ** -0.5),
        "g_mla_q": gain((L, MLA_QK_DIM)),
        "g_mla_k": gain((L, MLA_QK_DIM)),
        "w_proj_na": nrm((L, NA_WIDTH, D), NA_WIDTH ** -0.5),
        "w_proj_mla": nrm((L, MLA_WIDTH, D), MLA_WIDTH ** -0.5),
        "w_out": nrm((L, D, D), D ** -0.5),
        "g_norm2": gain((L, D)),
        "w_router": nrm((L, D, E), D ** -0.5),
        "e_bias": nrm((L, E), 0.01),
        "w_exp_gate": nrm((L, E, D, F), D ** -0.5),
        "w_exp_up": nrm((L, E, D, F), D ** -0.5),
        "w_exp_down": nrm((L, E, F, D), F ** -0.5),
        "w_sh_gate": nrm((L, D, SHARED_FF), D ** -0.5),
        "w_sh_up": nrm((L, D, SHARED_FF), D ** -0.5),
        "w_sh_down": nrm((L, SHARED_FF, D), SHARED_FF ** -0.5),
    }

def second_block(x, c, positions, w_ada, b_ada, g_norm1, w_in, g_na_q, g_na_k, na_rpb,
              g_q_lat, w_uq, g_kv_lat, w_ukv, g_mla_q, g_mla_k, w_proj_na, w_proj_mla,
              w_out, g_norm2, w_router, e_bias, w_exp_gate, w_exp_up, w_exp_down,
              w_sh_gate, w_sh_up, w_sh_down):
    B, S, D = x.shape
    split_at = list(np.cumsum(IN_SPLITS)[:-1])
    for l in range(DEPTH_2):
        mod = jax.nn.silu(c) @ w_ada[l] + b_ada[l]
        shift1, scale1, gate1, shift2, scale2, gate2 = jnp.split(mod[:, None, :], 6, axis=-1)

        h = rms_norm_2(x, g_norm1[l]) * (1.0 + scale1) + shift1
        proj = h @ w_in[l]
        na_q, na_k, na_v, q_lat, kv_lat, k_rot, gate_na, gate_mla = jnp.split(proj, split_at, axis=-1)

        qa = rms_norm_2(na_q.reshape(B, S, NA_HEADS, NA_HEAD_DIM), g_na_q[l])
        ka = rms_norm_2(na_k.reshape(B, S, NA_HEADS, NA_HEAD_DIM), g_na_k[l])
        va = na_v.reshape(B, S, NA_HEADS, NA_HEAD_DIM)
        y_na = neighbourhood_attention(qa, ka, va, na_rpb[l])

        qm = (rms_norm_2(q_lat, g_q_lat[l]) @ w_uq[l]).reshape(B, S, MLA_HEADS, MLA_QK_DIM)
        q_nope, q_rope = qm[..., :MLA_NOPE_DIM], apply_rope(qm[..., MLA_NOPE_DIM:], positions)
        kvm = (rms_norm_2(kv_lat, g_kv_lat[l]) @ w_ukv[l]).reshape(B, S, MLA_HEADS, MLA_NOPE_DIM + MLA_V_DIM)
        k_nope, vm = kvm[..., :MLA_NOPE_DIM], kvm[..., MLA_NOPE_DIM:]
        k_rope = jnp.broadcast_to(apply_rope(k_rot[:, :, None, :], positions), (B, S, MLA_HEADS, MLA_ROPE_DIM))
        qm = rms_norm_2(jnp.concatenate([q_nope, q_rope], axis=-1), g_mla_q[l])
        km = rms_norm_2(jnp.concatenate([k_nope, k_rope], axis=-1), g_mla_k[l])
        y_mla = blocked_full_attention(qm, km, vm)

        merged = (jax.nn.sigmoid(gate_na) * (y_na @ w_proj_na[l])
                  + jax.nn.sigmoid(gate_mla) * (y_mla @ w_proj_mla[l]))
        x = x + gate1 * (merged @ w_out[l])

        h2 = rms_norm_2(x, g_norm2[l]) * (1.0 + scale2) + shift2
        y_ffn = moe_ffn(h2, w_router[l], e_bias[l], w_exp_gate[l], w_exp_up[l], w_exp_down[l],
                        w_sh_gate[l], w_sh_up[l], w_sh_down[l])
        x = x + gate2 * y_ffn
    return x


def setup_inputs(seed=0):
    out = dict(first_inputs(seed))
    for name, value in second_inputs(seed + 1).items():
        if name != "x":
            out[name + "_2"] = value
    return out


def reference(
    x, norm_pre, norm_post, a_w_in, a_w_out, a_cmp_pos_k, a_cmp_pos_v, a_cmp_w1_k, a_cmp_w2_k,
    a_cmp_w1_v, a_cmp_w2_v, b_w_in, b_w_out, b_lambda, b_sub_gain, c_w_in, c_w_out, d_w_in,
    d_w_out, c_2, positions_2, w_ada_2, b_ada_2, g_norm1_2, w_in_2, g_na_q_2, g_na_k_2,
    na_rpb_2, g_q_lat_2, w_uq_2, g_kv_lat_2, w_ukv_2, g_mla_q_2, g_mla_k_2, w_proj_na_2,
    w_proj_mla_2, w_out_2, g_norm2_2, w_router_2, e_bias_2, w_exp_gate_2, w_exp_up_2,
    w_exp_down_2, w_sh_gate_2, w_sh_up_2, w_sh_down_2,
):
    x = first_block(
        x, norm_pre, norm_post, a_w_in, a_w_out, a_cmp_pos_k, a_cmp_pos_v, a_cmp_w1_k,
        a_cmp_w2_k, a_cmp_w1_v, a_cmp_w2_v, b_w_in, b_w_out, b_lambda, b_sub_gain, c_w_in,
        c_w_out, d_w_in, d_w_out,
    )
    return second_block(
        x, c_2, positions_2, w_ada_2, b_ada_2, g_norm1_2, w_in_2, g_na_q_2, g_na_k_2, na_rpb_2,
        g_q_lat_2, w_uq_2, g_kv_lat_2, w_ukv_2, g_mla_q_2, g_mla_k_2, w_proj_na_2, w_proj_mla_2,
        w_out_2, g_norm2_2, w_router_2, e_bias_2, w_exp_gate_2, w_exp_up_2, w_exp_down_2,
        w_sh_gate_2, w_sh_up_2, w_sh_down_2,
    )


_drawn_inputs = setup_inputs


def setup_inputs(seed=0):
    import zlib

    import numpy as np

    out = dict(_drawn_inputs(seed))
    spreads = {}
    factors = {'a_cmp_pos_k': 3.764,
     'b_lambda': 3.749,
     'b_sub_gain': 3.378,
     'b_ada_2': 4.562,
     'g_norm1_2': 8.0,
     'w_in_2': 3.036,
     'g_na_q_2': 8.0,
     'g_na_k_2': 8.0,
     'na_rpb_2': 8.0,
     'g_q_lat_2': 8.0,
     'w_uq_2': 8.0,
     'g_kv_lat_2': 8.0,
     'w_ukv_2': 4.933,
     'g_mla_q_2': 8.0,
     'g_mla_k_2': 8.0,
     'w_proj_na_2': 4.07,
     'w_proj_mla_2': 4.943,
     'w_out_2': 3.256,
     'g_norm2_2': 32.714,
     'e_bias_2': 12.843}
    for name, (base, spread) in spreads.items():
        noise = np.random.default_rng([zlib.crc32(name.encode()), seed]).standard_normal(out[name].shape)
        drawn = base * np.exp(spread * noise) if base else spread * noise
        out[name] = jnp.asarray(drawn.astype(out[name].dtype))
    for name, factor in factors.items():
        out[name] = (out[name] * factor).astype(out[name].dtype)
    return out
```

```python
import math
import numpy as np
import concourse.bass as bass
from concourse import mybir
from contextlib import ExitStack

S, D, P, T = 256, 1024, 128, 2
DC = D // P
HD = 64
RING = 3
SLOT = 4096
N_CMP, CMP_L, CMP_ST = 15, 32, 16
A_COLS = dict(q=0, kc=1024, vc=1280, ks=1536, vs=1792, kw=2048, vw=2304, gl=2560, z=2608)
EXPERTS, FF, TOPK, GROUPS = 64, 256, 8, 8
ROUTED_SCALE = 2.5
EPS = 1e-6
BIG = 1e30
MOE_SLOTS = 2

PC = {}
_at = 0
for _n, _w in (("pre", 4 * DC), ("g1", DC), ("g2", DC), ("c", DC), ("naq", 1), ("nak", 1), ("qlat", 2),
               ("kvlat", 1), ("mlaq", 1), ("mlak", 1), ("posk", 16), ("posv", 16)):
    PC[_n] = (_at, _at + _w)
    _at += _w
PC_N = _at

CC = {}
_at = 0
for _n, _w in (("dist", 4 * 256), ("win", 256), ("cbias", 480), ("cmask", 30), ("strict", 256),
               ("tri", 128), ("lower", 64), ("freq", 16), ("negiota", 64), ("row", 1)):
    CC[_n] = (_at, _at + _w)
    _at += _w
CC_N = _at


def slopes(n):
    return [2.0 ** (-8.0 * (i + 1) / n) for i in range(n)]


def shape_constants():
    a = np.zeros((P, CC_N), np.float32)
    p = np.arange(P)[:, None]
    dist = P + p - np.arange(2 * P)[None, :]
    ok = dist >= 0
    pats = [ok, ok & (dist <= 128), ok & (dist % 4 == 0), ok & (dist % 16 == 0)]
    a[:, CC["dist"][0]:CC["dist"][1]] = np.stack([np.where(m, dist, BIG) for m in pats], 1).reshape(P, -1)
    col = p % 64
    kcol = 63 - np.arange(256)[None, :] % 64
    start = np.clip(col - 8, 0, 48)
    a[:, CC["win"][0]:CC["win"][1]] = np.where((kcol >= start) & (kcol < start + 16), 0.0, -BIG)
    end = CMP_ST * np.arange(N_CMP) + CMP_L - 1
    tok = np.arange(2)[None, :, None] * P + np.arange(P)[:, None, None]
    cd = tok - end[None, None, :]
    sl = np.array(slopes(16), np.float32)
    cb = np.where(cd[:, :, None, :] >= 0, -sl[None, None, :, None] * cd[:, :, None, :].astype(np.float32), -BIG)
    a[:, CC["cbias"][0]:CC["cbias"][1]] = cb.reshape(P, -1)
    a[:, CC["cmask"][0]:CC["cmask"][1]] = (cd >= 0).reshape(P, -1)
    q = np.arange(P)[None, :]
    neg = -(p < q).astype(np.float32)
    a[:, CC["strict"][0]:CC["strict"][1]] = np.concatenate([neg, neg], 1)
    a[:, CC["tri"][0]:CC["tri"][1]] = (p >= q)
    i, j = np.arange(8)[:, None], np.arange(8)[None, :]
    a[:, CC["lower"][0]:CC["lower"][1]] = (j < i).reshape(1, 64)
    a[:, CC["freq"][0]:CC["freq"][1]] = (np.float32(10000.0) ** (-np.arange(16, dtype=np.float32) / np.float32(16)))[None, :]
    a[:, CC["negiota"][0]:CC["negiota"][1]] = -np.arange(64)[None, :]
    a[:, CC["row"][0]:CC["row"][1]] = p
    return a


def build(nc, A, out):
    f32 = mybir.dt.float32
    i32 = mybir.dt.int32
    ALU = mybir.AluOpType
    ACT = mybir.ActivationFunctionType
    AX = mybir.AxisListType
    ctx = ExitStack()
    with ctx:
        def sb(name, *shape, dt=f32):
            return ctx.enter_context(nc.sbuf_tensor(name, [shape[0], int(np.prod(shape[1:]))], dt))

        def sem(name):
            return ctx.enter_context(nc.semaphore(name))

        ident = sb("ident", P, 128)
        cst = sb("shape_consts", P, CC_N)
        par = sb("params", P, PC_N)
        h_ = sb("h", P, T * D)
        u_ = sb("u", P, T * D)
        uT_ = sb("uT", P, DC * S)
        QK_ = sb("QK", P, 16 * S)
        V_ = sb("V", P, T * D)
        z_ = sb("z", P, T * D)
        ob = sb("oraw", P, 6144)
        bias_ = sb("bias", P, 16 * 256)
        mod = sb("mod", P, 6 * D)
        pb_ = sb("probs", P, 2 * 1024)
        pT_ = sb("probsT", P, 4 * 512)
        ring = [sb(f"ring{i}", P, SLOT) for i in range(RING)]
        gpost = sb("gpost", P, D)
        w2_ = sb("w2", P, 4 * 64)
        kcT = sb("kcmpT", P, 64)
        ones = sb("ones", P, 128)
        lam_ = sb("lambda_subgain", P, 384)
        sm = sb("small", P, 1120)
        posn = sb("positions", P, 2, dt=i32)
        todo = sb("expert_list", 1, 66, dt=i32)

        h = h_[:, :].rearrange("p (t n) -> p t n", t=T)
        u = u_[:, :].rearrange("p (t n) -> p t n", t=T)
        uT = uT_[:, :].rearrange("p (c s) -> p c s", s=S)
        QK = QK_[:, :].rearrange("p (c s) -> p c s", s=S)
        V = V_[:, :].rearrange("p (t n) -> p t n", t=T)
        z = z_[:, :].rearrange("p (t n) -> p t n", t=T)
        bias = bias_[:, :].rearrange("p (h k) -> p h k", k=256)
        probs = pb_[:, :].rearrange("p (u t i k) -> p u t i k", u=2, t=2, i=2)
        probsT = pT_[:, :].rearrange("p (b n) -> p b n", n=512)
        w2 = w2_[:, :].rearrange("p (v c n) -> p v c n", v=2, c=2)

        def small(a, n):
            return sm[:, a:a + n]
        ssq, lnv, rstd = small(0, 16), small(16, 16), small(32, 16)
        rs = small(64, 96).rearrange("p (t j) -> p t j", t=2)
        nm = small(160, 96).rearrange("p (t j) -> p t j", t=2)
        cf = small(256, 96).rearrange("p (t j) -> p t j", t=2)
        gate = small(352, 132).rearrange("p (t j) -> p t j", t=2)
        epsc, onec, zeroc = small(484, 1), small(485, 1), small(486, 1)
        lamc = small(488, 8)
        gcur = small(496, 8).rearrange("p (t j) -> p t j", t=2)
        cosr = small(512, 32)
        sinr = small(544, 32)
        modc = small(576, 32)
        gs = small(608, 16)
        siluc = small(624, 16)
        gelu_x, gelu_t = small(640, 240), small(880, 240)
        rank = small(640, 256)

        psum = ctx.enter_context(nc.psum_tensor("psum", [P, 8 * 512], f32))
        banks = [psum[:, 512 * i:512 * i + 512] for i in range(8)]

        s_const, s_h, s_gpost, s_small = sem("consts_in"), sem("h_in"), sem("gpost_in"), sem("smalls_in")
        s_rpb, s_lam, s_row, s_rt, s_out = sem("rpb_in"), sem("lambda_in"), sem("b_ada_in"), sem("router_in"), sem("out_done")
        w_in = [sem(f"weights_in{i}") for i in range(RING)]
        acc_done = sem("acc_done")
        free = {("d", 0): sem("acc0_free_dve"), ("d", 1): sem("acc1_free_dve"),
                ("a", 0): sem("acc0_free_act"), ("a", 1): sem("acc1_free_act"),
                ("td", 0): sem("tr0_free_dve"), ("td", 1): sem("tr1_free_dve"),
                ("ta", 0): sem("tr0_free_act"), ("ta", 1): sem("tr1_free_act"),
                ("o", 0): sem("o0_free"), ("o", 1): sem("o1_free")}
        tr_done = sem("transposes_done")
        o_done = sem("o_done")
        dch, ach, pch, pech = sem("dve_chain"), sem("act_chain"), sem("pool_chain"), sem("pe_chain")
        s_sq = sem("ready_for_rstd")
        s_rstd = sem("act_result")
        s_u = sem("u_ready")
        s_uT = sem("uT_ready")
        s_qkv = sem("qkv_ready")
        s_mx = sem("max_ready")
        s_p = sem("probs_ready")
        s_bias = sem("bias_ready")
        s_attn = sem("attn_done")
        s_x = sem("cmp_in_ready")
        s_xp = sem("cmp_windows_ready")
        s_hid = sem("cmp_hidden_ready")
        s_cum = sem("cumsum_done")
        s_lom = sem("log_om_ready")
        s_abs = sem("softplus_parts_ready")
        s_am = sem("stick_weights_ready")
        s_id = sem("ident_ready")
        gu_in = [sem(f"gate_up_in{i}") for i in range(MOE_SLOTS)]
        dn_in = [sem(f"down_in{i}") for i in range(MOE_SLOTS)]
        s_gu, s_dn = sem("gate_up_done"), sem("down_done")
        s_ge, s_ga, s_gat, s_aT = sem("moe_exp"), sem("moe_act"), sem("moe_act_transposed"), sem("moe_actT")
        s_moe = sem("moe_gates_ready")
        s_fin = sem("final_ready")
        s_r1, s_r2, s_aux = sem("expert_masks_ready"), sem("expert_ranks_ready"), sem("expert_sums_done")
        s_all = sem("experts_done")
        s_gc, s_mc = sem("moe_weights_copied"), sem("moe_chain")

        guv = [ring[j][:, :].rearrange("p (c n) -> p c n", n=2 * FF) for j in range(MOE_SLOTS)]
        dnv = [ring[2][:, 2048 * j:2048 * j + 2048].rearrange("p (c n) -> p c n", n=D) for j in range(MOE_SLOTS)]

        class Count:
            def __init__(self):
                self.acc = self.tr = self.o = self.w = 0
                self.win = [0] * RING
                self.n = {}

            def up(self, name, by=1):
                self.n[name] = self.n.get(name, 0) + by
                return self.n[name]

        class Own:
            def __init__(self, eng, s):
                self.eng, self.s, self.n = eng, s, 0

            def tick(self, ins):
                self.n += 1
                ins.then_inc(self.s, 1)

            def own(self):
                self.eng.wait_ge(self.s, self.n)

            def link(self, ins):
                self.tick(ins)
                self.own()

        def pc(name, i=0, p=P):
            a = PC[name][0] + i
            return par[0:p, a:a + 1]

        def cc(name):
            return cst[:, CC[name][0]:CC[name][1]]

        dist = cc("dist").rearrange("p (m k) -> p m k", k=256)
        tri = cc("tri")

        def cols(ap, a, n):
            return [(0, 8 * n, ap[:, a:a + n].rearrange("(c p) n -> p c n", p=P), n)]
        aw, bw, cw, dw, ew = A["a_w_in"][0], A["b_w_in"][0], A["c_w_in"][0], A["d_w_in"][0], A["w_in_2"][0]
        MOD = [cols(A["w_ada_2"][0], 512 * j, 512) for j in range(12)]
        LA = [cols(aw, c, 512) for c in (0, 512, 1024, 1536, 2048, 2608, 3120)] + [cols(aw, 2560, 48)]
        LA_CMP = [[(0, SLOT, A[n][0].rearrange("(c p) n -> p c n", p=P), 256)] for n in ("a_cmp_w1_k", "a_cmp_w1_v")]
        LB = [cols(bw, 512 * j, 512) for j in range(8)]
        LC = [cols(cw, 512 * j, 512) for j in range(7)]
        LD = [cols(dw, 512 * j, 512) for j in range(8)]
        LE = [cols(ew, 512 * j, 512) for j in range(3)] + [cols(ew, 1536, 416)] + [cols(ew, 1952 + 512 * j, 512) for j in range(4)]
        LE_UP = [[(0, 1536, A["w_uq_2"][0].rearrange("(c p) n -> p c n", p=P), 768),
                  (1536, 1024, A["w_ukv_2"][0].rearrange("(c p) n -> p c n", p=P), 1024)]]
        LE_PROJ = [[(0, SLOT, A[n][0].rearrange("(c p) n -> p c n", p=P), 1024)] for n in ("w_proj_na_2", "w_proj_mla_2")]

        def outw(ap):
            return [cols(ap, 512 * j, 512) for j in range(2)]

        def stream():
            yield from ((w, 1) for w in MOD)
            yield (None, 1)
            yield from ((w, 1) for w in LA)
            yield (LA_CMP[0], 0)
            yield (LA_CMP[1], 1)
            yield (None, 2)
            yield (None, 16)
            yield from ((w, 1) for w in outw(A["a_w_out"][0]))
            yield from ((w, 1) for w in LB)
            yield (None, 8)
            yield from ((w, 1) for w in outw(A["b_w_out"][0]))
            yield from ((w, 1) for w in LC)
            yield (None, 6)
            yield from ((w, 1) for w in outw(A["c_w_out"][0]))
            yield from ((w, 1) for w in LD)
            yield (None, 16)
            yield from ((w, 1) for w in outw(A["d_w_out"][0]))
            yield from ((w, 1) for w in LE)
            yield (LE_UP[0], 4)
            yield (None, 8)
            yield from ((w, 2) for w in LE_PROJ)
            yield from ((w, 1) for w in outw(A["w_out_2"][0]))

        block = ctx.enter_context(nc.Block())

        @block.sync
        def _(sp):
            sp.dma_start(h[:, :, :], A["x"][0].rearrange("(t p) n -> p t n", p=P)).then_inc(s_h, 16)
            n, fills, done_at = 0, 0, []
            for loads, f in stream():
                fills += f
                if loads is None:
                    continue
                if n >= RING:
                    sp.wait_ge(acc_done, done_at[n - RING])
                for off, size, src, width in loads:
                    dst = ring[n % RING][:, off:off + size].rearrange("p (c n) -> p c n", n=width)
                    sp.dma_start(dst, src).then_inc(w_in[n % RING], 16)
                done_at.append(fills if f else fills + 1)
                n += 1
            def gate_up(j, g, up):
                sp.dma_start(guv[j][:, :, 0:FF], g.rearrange("(c p) n -> p c n", p=P)).then_inc(gu_in[j], 16)
                sp.dma_start(guv[j][:, :, FF:2 * FF], up.rearrange("(c p) n -> p c n", p=P)).then_inc(gu_in[j], 16)

            def down(j, dn):
                sp.dma_start(dnv[j], dn.rearrange("(c p) n -> p c n", p=P)).then_inc(dn_in[j], 16)

            def chosen(name, e):
                return A[name][0][bass.ds(e, 1)].rearrange("e k n -> (e k) n")

            def expert_id(k):
                return sp.value_load(todo[0:1, bass.ds(k, 1)], min_val=0, max_val=EXPERTS - 1)

            sp.wait_ge(acc_done, done_at[n - RING])
            gate_up(0, A["w_sh_gate_2"][0], A["w_sh_up_2"][0])
            sp.wait_ge(acc_done, fills)
            down(0, A["w_sh_down_2"][0])
            sp.wait_ge(s_moe, 1)
            pairs = sp.value_load(todo[0:1, 64:65], min_val=TOPK // 2, max_val=EXPERTS // 2)
            for g in (1, 2):
                e = expert_id(g - 1)
                if g > 1:
                    sp.wait_ge(s_gu, 2 * g - 2)
                gate_up(g % 2, chosen("w_exp_gate_2", e), chosen("w_exp_up_2", e))
                if g > 1:
                    sp.wait_ge(s_dn, 2 * g - 2)
                down(g % 2, chosen("w_exp_down_2", e))
            with sp.Fori(1, pairs) as it:
                for j in range(MOE_SLOTS):
                    g = it * 2 + 1 + j
                    e = expert_id(it * 2 + j)
                    sp.wait_ge(s_gu, 2 * g - 2)
                    gate_up((1 + j) % 2, chosen("w_exp_gate_2", e), chosen("w_exp_up_2", e))
                    sp.wait_ge(s_dn, 2 * g - 2)
                    down((1 + j) % 2, chosen("w_exp_down_2", e))
            sp.wait_ge(s_fin, 1)
            sp.dma_start(out[0].rearrange("(t p) n -> p t n", p=P), u[:, :, :]).then_inc(s_out, 16)
            sp.wait_ge(s_out, 16)


        def last_bc(ap, n):
            return bass.AP(ap.tensor, ap.offset, [*ap.ap, [0, n]])

        def mid_bc(ap, n):
            return bass.AP(ap.tensor, ap.offset, [ap.ap[0], [0, n], *ap.ap[1:]])

        def row_bc(ap, n):
            return bass.AP(ap.tensor, ap.offset, [[0, P], [1, n]])

        def head(q, k, job, v, bidx):
            return dict(q=q, k=k, job=job, v=v, b=bidx)

        def o_view(n, dv):
            return ob[:, 0:2 * n * dv].rearrange("p (t j d) -> p t j d", t=2, j=n)

        UA, UB, UC, UN, UM = [], [], [], [], []
        for br in range(2):
            for hp in range(8):
                UA.append([head(QK[64 * i:64 * i + 64, hp, :], QK[64 * i:64 * i + 64, 8 + 4 * br + hp // 2, :],
                                16 + 16 * br + 2 * hp + i, (256 * br + 64 * (hp // 2), 64), 2 * hp + i) for i in range(2)])
        for hh in range(8):
            UB.append([head(QK[64 * i:64 * i + 64, hh, :], QK[64 * i:64 * i + 64, 8 + hh, :],
                            2 * hh + i, (128 * hh, 128), 2 * hh + i) for i in range(2)])
        for x in range(6):
            UC.append([head(QK[64 * i:64 * i + 64, x, :], QK[64 * i:64 * i + 64, 6 + x, :],
                            2 * x + i, (256 * ((2 * x + i) % 4), 256), 2 * x + i) for i in range(2)])
        for x in range(4):
            UN.append([head(QK[64 * i:64 * i + 64, x, :], QK[64 * i:64 * i + 64, 4 + x, :],
                            2 * x + i, (64 * (2 * x + i), 64), 2 * x + i) for i in range(2)])
            UM.append([head(QK[0:96, 8 + 2 * x + i, :], uT[0:96, 2 * x + i, :],
                            8 + 2 * x + i, (512 + 64 * (2 * x + i), 64), None) for i in range(2)])
        CAUSAL, FULL = [(1, 0), (1, 1), (0, 0)], [(1, 0), (1, 1), (0, 0), (0, 1)]
        LAYERS = ((UA, CAUSAL, 48, 64), (UB, CAUSAL, 16, 128), (UC, CAUSAL, 12, 256))

        Xc = ob[:, 0:2048].rearrange("p (v g s) -> p v g s", v=2, g=4)
        Xp = ob[:, 2048:2048 + 1920].rearrange("p (v l n) -> p v l n", v=2, l=16)
        hid = gelu_x.rearrange("p (f n) -> p f n", n=60)
        vd = ob[:, 4096:5120].rearrange("p (g n) -> p g n", g=4)
        pc_ = pb_[:, 1024:2048].rearrange("p (t h n) -> p t h n", t=2, n=32)
        pcT = u_[:, 0:1024].rearrange("p (b q) -> p b q", q=128)
        sp_ = [bias_[:, 384 * i:384 * i + 384] for i in range(2)]
        lom = [bias_[:, 768 + 384 * i:1152 + 384 * i] for i in range(2)]
        am = [bias_[:, 1536 + 384 * i:1920 + 384 * i] for i in range(2)]
        SH = [(QK[64 * (i % 2):64 * (i % 2) + 64, i // 2, :], QK[64 * (i % 2):64 * (i % 2) + 64, 8 + i // 2, :]) for i in range(16)]
        NQ = ob[:, 0:1024].rearrange("p (t n) -> p t n", t=2)
        NK = ob[:, 1024:2048].rearrange("p (t n) -> p t n", t=2)
        LAT = ob[:, 2048:2880].rearrange("p (t n) -> p t n", t=2)
        MQ = ob[:, 0:1536].rearrange("p (t n) -> p t n", t=2)
        MK = ob[:, 2880:4416].rearrange("p (t n) -> p t n", t=2)
        KR = ob[:, 4416:4480].rearrange("p (t n) -> p t n", t=2)
        TMP = pb_[:, 0:1536]
        MG = ob[:, 2048:4096].rearrange("p (t n) -> p t n", t=2)
        MG2 = ob[:, 4096:6144].rearrange("p (t n) -> p t n", t=2)
        ym = bias_[:, 0:2048].rearrange("p (t n) -> p t n", t=2)
        ge = [V_[:, 256 * t:256 * t + 256] for t in range(2)]
        ma = [V_[:, 512 + 256 * t:768 + 256 * t] for t in range(2)]
        maT = [pT_[:, 256 * t:256 * t + 256] for t in range(2)]
        wr = pT_[:, 1024:1536].rearrange("p (c n) -> p c n", n=64)
        ebias = pT_[:, 1536:1600]
        rt = [pb_[:, 128 * i:128 * i + 128] for i in range(8)]
        brow = ob[0:1, 0:6144]
        active, rankc = small(896, 1)[0:64, :], small(897, 1)[0:64, :]
        order, gT = pb_[0:64, 1024:1088], pb_[0:64, 1280:1536]
        cb = uT_[:, 0:1024].rearrange("p (c n) -> p c n", n=128)
        zeros_ = pT_[:, 0:512]
        ones_, ones_row = ones[:, :], ones[0:1, :]
        lamb, subg = lam_[:, 0:256], lam_[:, 256:384]
        acc_before_D = 83
        acc_router = 127

        @block.tensor
        def _(pe):
            c, me = Count(), Own(pe, pech)
            prev = {}

            def take(kind, i, releaser):
                if (kind, i) in prev:
                    pe.wait_ge(*prev[kind, i])
                prev[kind, i] = (free[releaser, i], c.up((releaser, i)))

            def acc(releaser):
                i = c.acc % 2
                take("acc", i, releaser)
                c.acc += 1
                return banks[2 * i], banks[2 * i + 1]

            def tr(releaser):
                i = c.tr % 2
                take("tr", i, releaser)
                c.tr += 1
                return banks[4 + i]

            def obank():
                i = c.o % 2
                take("o", i, "o")
                c.o += 1
                return banks[6 + i]

            def slot():
                i = c.w % RING
                c.w += 1
                c.win[i] += 16
                pe.wait_ge(w_in[i], c.win[i])
                return ring[i]

            def transposes(src, chunks, releaser="td"):
                for k in range(0, len(chunks), 2):
                    b = tr(releaser)
                    for j, (a, w) in enumerate(chunks[k:k + 2]):
                        for t in range(T):
                            last = nc.tensor.transpose(b[0:w, 256 * j + 128 * t:256 * j + 128 * t + 128],
                                                       src[:, t, a:a + w], ident[:, :])
                    last.then_inc(tr_done, 1)

            CH = [(128 * k, 128) for k in range(DC)]

            def mm_T(bank, w, col, n=256):
                for f in range(n // 128):
                    for d in range(DC):
                        last = nc.tensor.matmul(bank[:, 256 * f:256 * f + 256], w[:, d, col + 128 * f:col + 128 * f + 128],
                                                uT[:, d, :], start=(d == 0), stop=(d == DC - 1))
                return last

            def mm_R(out_, w, t, col, n, lhs=None, kc=DC):
                for d in range(kc):
                    last = nc.tensor.matmul(out_, uT[:, (lhs or 0) + d, 128 * t:128 * t + 128], w[:, d, col:col + n],
                                            start=(d == 0), stop=(d == kc - 1))
                return last

            def proj(kind, n=512):
                s = slot()
                w = s[:, 0:8 * n].rearrange("p (c n) -> p c n", n=n)
                a, b = acc("d")
                if kind == "TT":
                    mm_T(a, w, 0)
                    last = mm_T(b, w, 256)
                elif kind == "TR":
                    mm_T(a, w, 0)
                    mm_R(b[:, 0:256], w, 0, 256, 256)
                    last = mm_R(b[:, 256:512], w, 1, 256, 256)
                else:
                    mm_R(a[:, 0:n], w, 0, 0, n)
                    last = mm_R(b[:, 0:n], w, 1, 0, n)
                last.then_inc(acc_done, 1)

            def norm_in():
                pe.wait_ge(s_u, c.up("u"))
                transposes(u, CH)
                pe.wait_ge(s_uT, c.up("uT"))

            def attention(units, blocks, dv):
                nk0 = 128 if blocks is CAUSAL else 256
                pe.wait_ge(s_qkv, c.up("qkv"))

                def scores(un):
                    a, b = acc("d")
                    for x, bk in ((un[0], a), (un[1], b)):
                        nc.tensor.matmul(bk[:, 0:256], x["q"][:, 128:256], x["k"][:, 0:256], start=True, stop=True)
                        last = nc.tensor.matmul(bk[:, 256:256 + nk0], x["q"][:, 0:128], x["k"][:, 0:nk0],
                                                start=True, stop=True)
                    last.then_inc(acc_done, 1)

                def values(n, un):
                    pe.wait_ge(s_p, c.up("p"))
                    ready = []
                    for i in range(2):
                        rel = "ta" if i == 0 else "td"
                        at = c.tr % 2
                        b = tr(rel)
                        for k, (qt, kb) in enumerate(blocks):
                            last = nc.tensor.transpose(b[:, 128 * k:128 * k + 128],
                                                       probs[:, n % 2, qt, i, 128 * kb:128 * kb + 128], ident[:, :])
                        last.then_inc(tr_done, 1)
                        ready.append(prev["tr", at])
                    for i, x in enumerate(un):
                        ob_ = obank()
                        pe.wait_ge(*ready[i])
                        for qt in (1, 0):
                            ks = [(k, kb) for k, (q_, kb) in enumerate(blocks) if q_ == qt]
                            for j, (k, kb) in enumerate(ks):
                                last = nc.tensor.matmul(ob_[:, dv * qt:dv * qt + dv],
                                                        probsT[:, 2 * (n % 2) + i, 128 * k:128 * k + 128],
                                                        V[:, kb, x["v"][0]:x["v"][0] + dv],
                                                        start=(j == 0), stop=(j == len(ks) - 1))
                        last.then_inc(o_done, 1)

                scores(units[0])
                for n in range(len(units)):
                    if n + 1 < len(units):
                        scores(units[n + 1])
                    values(n, units[n])

            def project_out():
                norm_in()
                for _ in range(2):
                    proj("RR")

            pe.wait_ge(s_id, 2)
            pe.wait_ge(s_u, c.up("u"))
            pe.wait_ge(s_row, 16)
            for j in range(12):
                w = slot()[:, :].rearrange("p (c n) -> p c n", n=512)
                a, _b = acc("d")
                for d in range(DC):
                    nc.tensor.matmul(a[:, :], cb[:, d, :], w[:, d, :], start=(d == 0), stop=False)
                nc.tensor.matmul(a[:, :], ones_row, brow[0:1, 512 * j:512 * j + 512], start=False, stop=True)\
                    .then_inc(acc_done, 1)
            a, _b = acc("d")
            pe.wait_ge(free["d", 0], c.n["d", 0] - 1)
            pe.wait_ge(free["d", 1], c.n["d", 1])
            for k, base in enumerate((0, D, 3 * D, 4 * D)):
                for d in range(DC):
                    last = nc.tensor.matmul(a[:, 8 * k + d:8 * k + d + 1], mod[0:1, base + 128 * d:base + 128 * d + 128],
                                            ones_row[0:1, 0:1], start=True, stop=True)
            last.then_inc(acc_done, 1)

            norm_in()
            for kind, n in (("TT", 512), ("TT", 512), ("TT", 512), ("TR", 512), ("TR", 512), ("RR", 512), ("RR", 512), ("RR", 48)):
                proj(kind, n)
            wk, wv = slot(), slot()
            a, b = acc("d")
            pe.wait_ge(s_xp, 1)
            for v, (w, bk) in enumerate(((wk, a), (wv, b))):
                w = w[:, :].rearrange("p (c n) -> p c n", n=256)
                for f in range(2):
                    for l in range(16):
                        last = nc.tensor.matmul(bk[:, 64 * f:64 * f + 60], w[:, l, 128 * f:128 * f + 128], Xp[:, v, l, :],
                                                start=(l == 0), stop=(l == 15))
            last.then_inc(acc_done, 1)
            pe.wait_ge(s_hid, 1)
            pe.wait_ge(s_small, 32)
            a, b = acc("d")
            for f in range(2):
                nc.tensor.matmul(a[0:64, 0:60], w2[:, 0, f, :], hid[:, f, :], start=(f == 0), stop=(f == 1))
            for g in range(4):
                for f in range(2):
                    last = nc.tensor.matmul(b[0:15, 64 * g:64 * g + 64], hid[:, 2 + f, 15 * g:15 * g + 15], w2[:, 1, f, :],
                                            start=(f == 0), stop=(f == 1))
            last.then_inc(acc_done, 1)
            pe.wait_ge(s_hid, 2)
            a, b = acc("d")
            for qt in range(2):
                for i in range(16):
                    r, bk = 64 * (i % 2), (a, b)[i % 2]
                    at = 128 * qt + 16 * (i // 2)
                    last = nc.tensor.matmul(bk[:, at:at + 15], QK[r:r + 64, i // 2, 128 * qt:128 * qt + 128],
                                            kcT[r:r + 64, 15 * (i // 4):15 * (i // 4) + 15], start=True, stop=True)
            last.then_inc(acc_done, 1)
            pe.wait_ge(s_hid, 3)
            for g2 in range(2):
                bk = tr("td")
                for k in range(4):
                    g, qt = 2 * g2 + k // 2, k % 2
                    last = nc.tensor.transpose(bk[:, 128 * k:128 * k + 128],
                                               pb_[:, 1024 + 512 * qt + 128 * g:1024 + 512 * qt + 128 * g + 128], ident[:, :])
                last.then_inc(tr_done, 1)
            for g in range(4):
                bk = obank()
                pe.wait_ge(free["td", (c.tr - 2 + g // 2) % 2], c.n["td", (c.tr - 2 + g // 2) % 2])
                for qt in range(2):
                    last = nc.tensor.matmul(bk[:, 256 * qt:256 * qt + 256], pcT[:, 2 * g + qt, :], vd[:, g, :],
                                            start=True, stop=True)
                last.then_inc(o_done, 1)
            attention(UA, CAUSAL, 64)
            project_out()
            norm_in()
            for kind in ("TT",) * 4 + ("RR",) * 4:
                proj(kind)
            attention(UB, CAUSAL, 128)
            project_out()
            norm_in()
            for kind in ("TT",) * 3 + ("RR",) * 4:
                proj(kind)
            attention(UC, CAUSAL, 256)
            project_out()
            norm_in()
            for kind in ("TT",) * 4 + ("RR",) * 4:
                proj(kind)
            pe.wait_ge(s_qkv, c.up("qkv"))
            bk = {}

            def stick_scores(i):
                bk[i], _b = acc("a")
                q, k = SH[i]
                nc.tensor.matmul(bk[i][:, 0:128], k[:, 128:256], q[:, 128:256], start=True, stop=False, skip_group_check=True)
                nc.tensor.matmul(bk[i][:, 128:384], k[:, 0:128], q[:, 0:256], start=False, stop=False, skip_group_check=True)\
                    .then_inc(acc_done, 1)

            def stick_values(i):
                b = obank()
                pe.wait_ge(s_am, i + 1)
                nc.tensor.matmul(b[:, 64:128], am[i % 2][:, 0:128], V[:, 1, 64 * i:64 * i + 64], start=True, stop=False)
                nc.tensor.matmul(b[:, 64:128], am[i % 2][:, 256:384], V[:, 0, 64 * i:64 * i + 64], start=False, stop=True)
                nc.tensor.matmul(b[:, 0:64], am[i % 2][:, 128:256], V[:, 0, 64 * i:64 * i + 64], start=True, stop=True)\
                    .then_inc(o_done, 1)

            stick_scores(0)
            stick_scores(1)
            for i in range(16):
                pe.wait_ge(s_lom, i + 1)
                l_ = lom[i % 2]
                nc.tensor.matmul(bk[i][:, 0:128], tri, l_[:, 0:128], start=False, stop=False, skip_group_check=True)
                nc.tensor.matmul(bk[i][:, 128:384], tri, l_[:, 128:384], start=False, stop=False, skip_group_check=True)
                nc.tensor.matmul(bk[i][:, 256:384], ones_, l_[:, 0:128], start=False, stop=True, skip_group_check=True)\
                    .then_inc(s_cum, 1)
                if i >= 1:
                    stick_values(i - 1)
                if i + 2 < 16:
                    stick_scores(i + 2)
            stick_values(15)
            project_out()

            norm_in()
            for n in (512, 512, 512, 416, 512, 512, 512, 512):
                proj("RR", n)
            pe.wait_ge(s_u, c.up("u"))
            transposes(NQ, CH[0:4])
            transposes(NK, CH[0:4])
            transposes(LAT, CH[0:3])
            pe.wait_ge(s_uT, c.up("uT"))
            s = slot()
            i = (c.w - 1) % RING
            c.win[i] += 16
            pe.wait_ge(w_in[i], c.win[i])
            wq = s[:, 0:1536].rearrange("p (c n) -> p c n", n=768)
            wkv = s[:, 1536:2560].rearrange("p (c n) -> p c n", n=1024)
            for t in range(T):
                a, b = acc("d")
                mm_R(a[:, 0:384], wq, t, 0, 384, kc=2)
                mm_R(b[:, 0:384], wq, t, 384, 384, kc=2).then_inc(acc_done, 1)
            for t in range(T):
                a, b = acc("d")
                mm_R(a[:, :], wkv, t, 0, 512, lhs=2, kc=1)
                mm_R(b[:, :], wkv, t, 512, 512, lhs=2, kc=1).then_inc(acc_done, 1)
            pe.wait_ge(s_u, c.up("u"))
            transposes(MQ, [(96 * k, 96) for k in range(8)])
            transposes(MK, [(96 * k, 96) for k in range(8)])
            attention(UN, FULL, 64)
            attention(UM, FULL, 64)
            pe.wait_ge(s_u, c.up("u"))
            transposes(ym, CH)
            pe.wait_ge(s_uT, c.up("uT"))
            for k in range(2):
                w = slot()[:, :].rearrange("p (c n) -> p c n", n=1024)
                for t in range(T):
                    a, b = acc("d")
                    mm_R(a[:, :], w, t, 0, 512, lhs=4 * k, kc=4)
                    mm_R(b[:, :], w, t, 512, 512, lhs=4 * k, kc=4).then_inc(acc_done, 1)
            pe.wait_ge(s_u, c.up("u"))
            transposes(MG, CH)
            pe.wait_ge(s_uT, c.up("uT"))
            for _ in range(2):
                proj("RR")
            norm_in()
            a, b = acc("a")
            pe.wait_ge(s_rt, 32)
            mm_R(a[:, 0:64], wr, 0, 0, 64)
            mm_R(b[:, 0:64], wr, 1, 0, 64).then_inc(acc_done, 1)
            for k in ("tr", "o"):
                for i in range(2):
                    pe.wait_ge(*prev[k, i])
            pe.wait_ge(*prev["acc", 0])

            def gate_up(t, j):
                for d in range(DC):
                    last = nc.tensor.matmul(banks[t][:, :], uT[:, d, 128 * t:128 * t + 128], guv[j][:, d, :],
                                            start=(d == 0), stop=(d == DC - 1))
                last.then_inc(s_gu, 1)

            def act_T(e, t):
                pe.wait_ge(s_ga, 2 * e + t + 1)
                for f in range(2):
                    last = nc.tensor.transpose(banks[2 + t][:, 128 * f:128 * f + 128], ma[t][:, 128 * f:128 * f + 128], ident[:, :])
                last.then_inc(s_gat, 1)

            def down(e, t, j, stop=False, done=None):
                pe.wait_ge(s_aT, 2 * e + t + 1)
                for f in range(2):
                    for n in range(2):
                        last = nc.tensor.matmul(banks[4 + 2 * t + n][:, :], maT[t][:, 128 * f:128 * f + 128],
                                                dnv[j][:, f, 512 * n:512 * n + 512], start=False,
                                                stop=(stop and f == 1), skip_group_check=True)
                last.then_inc(done or s_dn, 1)

            pe.wait_ge(gu_in[0], 32)
            gate_up(0, 0)
            gate_up(1, 0)
            pe.wait_ge(*prev["acc", 1])
            pe.wait_ge(s_r1, 1)
            for t in range(T):
                nc.tensor.matmul(banks[2][0:64, 0:1], rt[1][:, 64 * t:64 * t + 64], ones_[:, 0:1], start=(t == 0), stop=(t == 1))
            for t in range(T):
                last = nc.tensor.transpose(banks[3][0:64, 128 * t:128 * t + 128], gate[:, t, 0:64], ident[:, :])
            last.then_inc(s_aux, 1)
            pe.wait_ge(s_r2, 1)
            nc.tensor.matmul(banks[2][0:64, 1:2], cc("strict")[0:64, 0:64], active, start=True, stop=True)
            nc.tensor.matmul(banks[2][0:1, 2:3], active, ones_[0:64, 0:1], start=True, stop=True).then_inc(s_aux, 1)
            pe.wait_ge(s_r2, 2)
            nc.tensor.matmul(banks[2][0:1, 8:72], cc("row")[0:64, :], order, start=True, stop=True)
            for t in range(T):
                last = nc.tensor.matmul(banks[3][:, 64 * t:64 * t + 64], gT[:, 128 * t:128 * t + 128], order, start=True, stop=True)
            last.then_inc(s_aux, 1)
            pe.wait_ge(s_moe, 1)
            pairs = pe.value_load(todo[0:1, 64:65], min_val=TOPK // 2, max_val=EXPERTS // 2)
            for k in range(4):
                nc.tensor.matmul(banks[4 + k][:, :], zeros_[:, 0:128], zeros_[:, :], start=True, stop=False, skip_group_check=True)
            with pe.Fori(0, pairs) as it:
                for j in range(MOE_SLOTS):
                    g, nj = it * 2 + j, (j + 1) % 2
                    act_T(g, 0)
                    pe.wait_ge(gu_in[nj], 32 * it + (32 if j == 0 else 64))
                    gate_up(0, nj)
                    pe.wait_ge(dn_in[j], 16 * it + 16)
                    down(g, 0, j)
                    act_T(g, 1)
                    gate_up(1, nj)
                    down(g, 1, j)
            g = pairs * 2
            act_T(g, 0)
            pe.wait_ge(dn_in[0], 16 * pairs + 16)
            down(g, 0, 0, stop=True)
            act_T(g, 1)
            down(g, 1, 0, stop=True, done=s_all)

        @block.scalar
        def _(act):
            c, me = Count(), Own(act, ach)
            act.dma_start(cst[:, :], A["shape_consts"]).then_inc(s_const, 16)
            act.dma_start(par[:, :], A["params"]).then_inc(s_const, 16)
            act.dma_start(posn[:, :], A["pos_cols"]).then_inc(s_const, 16)
            act.dma_start(brow, A["b_ada_2"][0:1, :]).then_inc(s_row, 16)
            for v, n in enumerate(("a_cmp_w2_k", "a_cmp_w2_v")):
                act.dma_start(w2[:, v, :, :], A[n][0].rearrange("(c p) n -> p c n", p=P)).then_inc(s_small, 16)

            act.dma_start(lamb, row_bc(A["b_lambda"][0].rearrange("a b -> (a b)"), 256)).then_inc(s_lam, 16)
            act.dma_start(subg, row_bc(A["b_sub_gain"][0], 128)).then_inc(s_lam, 16)

            def gp(i):
                act.dma_start(gpost[:, :], row_bc(A["norm_post"][i], D)).then_inc(s_gpost, 16)

            def funcs(kind, *args):
                act.wait_ge(s_sq, c.up("sq"))
                kind(*args)

            def do_rstd(n, width):
                me.link(nc.scalar.activation(lnv[:, 0:n], ssq[:, 0:n], ACT.Ln, bias=epsc, scale=1.0 / width))
                nc.scalar.activation(rstd[:, 0:n], lnv[:, 0:n], ACT.Exp, scale=-0.5).then_inc(s_rstd, 1)

            def do_exp(dst, src, scale):
                nc.scalar.activation(dst, src, ACT.Exp, scale=scale).then_inc(s_rstd, 1)

            def do_sigmoid(dst, src, scale=1.0):
                nc.scalar.activation(dst, src, ACT.Sigmoid, scale=scale).then_inc(s_rstd, 1)

            def squares(src):
                act.wait_ge(s_sq, c.up("sq"))
                for t in range(T):
                    me.link(nc.scalar.activation(pT_[:, 0:D], src[:, t, :], ACT.Square, accum_out=ssq[:, t:t + 1]))
                do_rstd(2, D)

            def skip_proj(n):
                c.acc += n

            def attention(units, blocks, dv):
                nb = 128 * len(blocks)

                def exps(n, un):
                    act.wait_ge(s_mx, c.up("mx"))
                    job = un[0]["job"]
                    for qt in (1, 0):
                        nk = 256 if (qt or blocks is FULL) else 128
                        for i in range(2):
                            x = probs[:, n % 2, qt, i, 0:nk]
                            last = nc.scalar.activation(x, x, ACT.Exp, bias=nm[:, qt, job + i:job + i + 1],
                                                        accum_out=rs[:, qt, job + i:job + i + 1])
                    last.then_inc(s_p, 1)

                def evac(n):
                    act.wait_ge(tr_done, c.tr + 1)
                    if c.o - 2 > 0:
                        act.wait_ge(o_done, c.o - 2)
                    nc.scalar.activation(probsT[:, 2 * (n % 2), 0:nb], banks[4 + c.tr % 2][:, 0:nb], ACT.Copy)\
                        .then_inc(free["ta", c.tr % 2], 1)
                    c.tr += 2
                    c.o += 2
                exps(0, units[0])
                for n in range(len(units)):
                    evac(n)
                    if n + 1 < len(units):
                        exps(n + 1, units[n + 1])

            gp(0)
            funcs(do_sigmoid, siluc[:, 0:8], siluc[:, 8:16])
            act.wait_ge(s_sq, c.up("sq"))
            me.link(nc.scalar.activation(sinr, sinr, ACT.Sin))
            nc.scalar.activation(cosr, cosr, ACT.Sin).then_inc(s_rstd, 1)
            squares(h)
            c.tr += 4
            funcs(do_sigmoid, u[:, :, :], z[:, :, :])
            funcs(do_sigmoid, gate[:, :, 0:48], gate[:, :, 0:48])
            funcs(do_sigmoid, gelu_t, gelu_t, 1.5957691216057308)
            for qt in range(2):
                funcs(do_exp, pc_[:, qt, :, 0:15], pc_[:, qt, :, 0:15], 1.0)
            c.tr += 2
            c.o += 4
            attention(UA, CAUSAL, 64)
            squares(u)
            c.tr += 4
            squares(h)
            gp(1)
            c.tr += 4
            funcs(do_sigmoid, u[:, :, :], z[:, :, :])
            funcs(do_exp, lamc[:, 0:2], lamc[:, 0:2], 1.0)
            attention(UB, CAUSAL, 128)
            funcs(do_rstd, 16, 128)
            squares(u)
            c.tr += 4
            squares(h)
            gp(2)
            c.tr += 4
            funcs(do_sigmoid, u[:, :, :], z[:, :, :])
            attention(UC, CAUSAL, 256)
            funcs(do_exp, cf[:, :, 0:12], cf[:, :, 0:12], 1.0)
            squares(u)
            c.tr += 4
            squares(h)
            gp(3)
            c.tr += 4
            c.acc = acc_before_D
            funcs(do_sigmoid, u[:, :, :], z[:, :, :])

            def softplus_parts(i):
                act.wait_ge(acc_done, acc_before_D + i + 1)
                bk = banks[2 * ((acc_before_D + i) % 2)]
                me.link(nc.scalar.activation(sp_[i % 2], bk[:, 0:384], ACT.Abs))
                me.link(nc.scalar.activation(sp_[i % 2], sp_[i % 2], ACT.Exp, scale=-1.0))
                nc.scalar.activation(sp_[i % 2], sp_[i % 2], ACT.Ln, bias=onec).then_inc(s_abs, 1)

            softplus_parts(0)
            softplus_parts(1)
            for i in range(16):
                act.wait_ge(s_cum, i + 1)
                if i >= 2:
                    act.wait_ge(o_done, c.o + i - 1)
                pair = (acc_before_D + i) % 2
                nc.scalar.activation(am[i % 2], banks[2 * pair][:, 0:384], ACT.Exp).then_inc(free["a", pair], 1)
                if i + 2 < 16:
                    softplus_parts(i + 2)
            c.o += 16
            squares(u)
            c.tr += 4
            squares(h)
            c.tr += 4
            act.wait_ge(s_attn, 4)
            rp = A["na_rpb_2"]
            for i in range(8):
                for r in range(4):
                    src = bass.AP(rp.tensor, rp.offset + 465 * i + 31 * (7 - r) - 48, [[1, 64], [31, 4], [1, 64]])
                    act.dma_start(bias[64 * (r % 2):64 * (r % 2) + 64, 8 * (r // 2) + i, :].rearrange("p (a b) -> p a b", a=4),
                                  src).then_inc(s_rpb, 16)
            funcs(do_sigmoid, z[:, :, :], z[:, :, :])
            funcs(do_sigmoid, u[:, :, :], u[:, :, :])
            funcs(do_rstd, 16, 64)
            funcs(do_rstd, 16, 64)
            act.wait_ge(s_sq, c.up("sq"))
            for width, a in ((256, 0), (128, 2)):
                me.link(nc.scalar.activation(lnv[:, a:a + 2], ssq[:, a:a + 2], ACT.Ln, bias=epsc, scale=1.0 / width))
            nc.scalar.activation(rstd[:, 0:4], lnv[:, 0:4], ACT.Exp, scale=-0.5).then_inc(s_rstd, 1)
            c.tr += 6
            funcs(do_rstd, 16, 96)
            funcs(do_rstd, 16, 96)
            c.tr += 8
            attention(UN, FULL, 64)
            attention(UM, FULL, 64)
            act.wait_ge(s_attn, 5)
            act.dma_start(wr, A["w_router_2"][0].rearrange("(c p) n -> p c n", p=P)).then_inc(s_rt, 16)
            act.dma_start(ebias, row_bc(A["e_bias_2"][0], 64)).then_inc(s_rt, 16)
            c.tr += 8
            squares(h)
            c.acc = acc_router
            act.wait_ge(acc_done, acc_router + 1)
            pair = acc_router % 2
            for t in range(T):
                last = nc.scalar.activation(gate[:, t, 0:64], banks[2 * pair + t][:, 0:64], ACT.Sigmoid)
            last.then_inc(free["a", pair], 1)

            def moe_exp(e, t):
                act.wait_ge(s_gu, 2 * e + t + 1)
                nc.scalar.activation(ge[t], banks[t][:, 0:FF], ACT.Sigmoid).then_inc(s_ge, 1)

            def moe_evac(e, t):
                act.wait_ge(s_gat, 2 * e + t + 1)
                nc.scalar.activation(maT[t], banks[2 + t][:, 0:FF], ACT.Copy).then_inc(s_aT, 1)

            moe_exp(0, 0)
            moe_exp(0, 1)
            act.wait_ge(s_moe, 1)
            pairs = act.value_load(todo[0:1, 64:65], min_val=TOPK // 2, max_val=EXPERTS // 2)
            with act.Fori(0, pairs) as it:
                for j in range(MOE_SLOTS):
                    g = it * 2 + j
                    for t in range(T):
                        moe_evac(g, t)
                        moe_exp(g + 1, t)
            moe_evac(pairs * 2, 0)
            moe_evac(pairs * 2, 1)

        @block.gpsimd
        def _(pool):
            c, me = Count(), Own(pool, pch)
            me.link(nc.gpsimd.memset(ident[:, :], 0.0))
            nc.gpsimd.affine_select(out=ident[:, :], in_=ident[:, :], compare_op=ALU.not_equal, fill=1.0, base=0,
                                    pattern=[[-1, P]], channel_multiplier=1).then_inc(s_id, 1)
            nc.gpsimd.memset(ones[:, :], 1.0).then_inc(s_id, 1)
            pool.wait_ge(s_const, 48)

            def alibi(sl, pattern):
                for i, x in enumerate(sl):
                    last = nc.gpsimd.tensor_scalar(bias[:, i, :], dist[:, pattern[i], :], -x, None, ALU.mult)
                last.then_inc(s_bias, 1)

            alibi(slopes(16), [0] * 16)
            pool.wait_ge(s_x, 1)
            for v, n in enumerate(("posk", "posv")):
                for l in range(16):
                    last = nc.gpsimd.tensor_scalar(Xp[:, v, l, :].rearrange("p (g n) -> p g n", g=4),
                                                   Xc[:, v, :, 2 * l:2 * l + 225:16], pc(n, l), None, ALU.add)
            last.then_inc(s_xp, 1)
            pool.wait_ge(s_attn, 1)
            alibi([x for x in slopes(8) for _ in range(2)], [0] * 16)
            pool.wait_ge(s_attn, 2)
            alibi(slopes(12), [1 + i // 4 for i in range(12)])
            for i in range(16):
                pair = (acc_before_D + i) % 2
                pool.wait_ge(free["a", pair], c.up(pair))
                x = am[i % 2][:, 0:256].rearrange("p (a b) -> p a b", a=2)
                nc.gpsimd.affine_select(out=x, in_=x, compare_op=ALU.is_ge, fill=0.0, base=-1,
                                        pattern=[[0, 2], [1, P]], channel_multiplier=-1).then_inc(s_am, 1)
            pool.wait_ge(s_rpb, 32 * 16)
            nc.gpsimd.tensor_tensor(bias[:, :, :], bias[:, :, :], mid_bc(cc("win"), 16), ALU.add).then_inc(s_bias, 1)

        @block.vector
        def _(dve):
            c, me = Count(), Own(dve, dch)
            v = nc.vector
            tick, own, link = me.tick, me.own, me.link

            def acc_in():
                i = c.acc % 2
                c.acc += 1
                dve.wait_ge(acc_done, c.acc)
                c.up(("d", i))
                return banks[2 * i], banks[2 * i + 1], free["d", i]

            def own_acc():
                i = (c.acc - 1) % 2
                dve.wait_ge(free["d", i], c.n["d", i])

            def act_does():
                dve.wait_ge(s_rstd, c.up("rstd"))

            def tr_in(dst, n, gains):
                for k in range(0, n, 2):
                    dve.wait_ge(tr_done, c.tr + 1)
                    b = banks[4 + c.tr % 2]
                    for j in range(min(2, n - k)):
                        w, s1, s2, op = gains(k + j)
                        last = v.tensor_scalar(dst[0:w, k + j, :], b[0:w, 256 * j:256 * j + 256], s1, s2, ALU.mult, op) \
                            if s2 is not None else v.tensor_scalar(dst[0:w, k + j, :], b[0:w, 256 * j:256 * j + 256], s1, None, ALU.mult)
                    last.then_inc(free["td", c.tr % 2], 1)
                    c.up(("td", c.tr % 2))
                    c.tr += 1

            def tr_own():
                i = (c.tr - 1) % 2
                dve.wait_ge(free["td", i], c.n["td", i])

            def uT_ready():
                tr_own()
                dve.sem_inc(s_uT, 1)

            def plain(k):
                return P, 1.0, None, None

            def norm_in(gains):
                act_does()
                for t in range(T):
                    last = v.tensor_scalar(u[:, t, :], h[:, t, :], rstd[:, t:t + 1], None, ALU.mult)
                last.then_inc(s_u, 1)
                tr_in(uT, DC, gains)
                uT_ready()

            def both(a, b, n):
                return [(0, a[:, 0:n]), (1, b[:, 0:n])]

            def evac(dst0, dst1, n=512, scale=None):
                a, b, f = acc_in()
                for dst, x in ((dst0, a), (dst1, b)):
                    last = v.tensor_copy(dst, x[:, 0:n]) if scale is None else \
                        v.tensor_scalar(dst, x[:, 0:n], scale, None, ALU.mult)
                last.then_inc(f, 1)

            def flat(ap):
                return ap.rearrange("p a b -> p (a b)")

            def silu_z():
                own_acc()
                dve.sem_inc(s_sq, 1)

            def silu_end():
                act_does()
                link(v.tensor_tensor(z_[:, :], z_[:, :], u_[:, :], ALU.mult))

            def attention(units, blocks, dv, njobs, qkv=True):
                o = o_view(njobs, dv)
                nb = 128 * len(blocks)
                nk0 = 128 if blocks is CAUSAL else 256
                if qkv:
                    dve.sem_inc(s_qkv, 1)

                def soft(n, un):
                    a, b, f = acc_in()
                    if c.tr > 0:
                        dve.wait_ge(tr_done, c.tr)
                    job, bi = un[0]["job"], un[0]["b"]
                    d1 = probs[:, n % 2, 1, :, :]
                    d0 = probs[:, n % 2, 0, :, 0:nk0]
                    pair = psum[:, 1024 * ((c.acc - 1) % 2):1024 * ((c.acc - 1) % 2) + 1024].rearrange("p (i k) -> p i k", i=2)
                    a_, b_ = pair[:, :, 0:256], pair[:, :, 256:256 + nk0]
                    if bi is None:
                        v.tensor_copy(d1, a_)
                        v.tensor_copy(d0, b_).then_inc(f, 1)
                    else:
                        if blocks is CAUSAL:
                            v.tensor_tensor(d1, a_, bias[:, bi:bi + 2, :], ALU.add)
                            v.tensor_tensor(d0, b_, bias[:, bi:bi + 2, 128:256], ALU.add).then_inc(f, 1)
                        else:
                            for x, y, k in ((d1, a_, 8 + bi), (d0, b_, bi)):
                                for i in range(2):
                                    r3 = bias[:, k + i, :].rearrange("p (r c) -> p r c", c=64)
                                    rev = bass.AP(r3.tensor, r3.offset + 63, [r3.ap[0], [64, 4], [-1, 64]])
                                    last = v.tensor_tensor(x[:, i, :].rearrange("p (r c) -> p r c", c=64),
                                                           y[:, i, :].rearrange("p (r c) -> p r c", c=64), rev, ALU.add)
                            last.then_inc(f, 1)
                    own_acc()
                    v.tensor_reduce(nm[:, 1, job:job + 2], d1, AX.X, ALU.max, negate=True)
                    v.tensor_reduce(nm[:, 0, job:job + 2], d0, AX.X, ALU.max, negate=True).then_inc(s_mx, 1)

                def values(n, un):
                    dve.wait_ge(tr_done, c.tr + 2)
                    if c.o - 2 > 0:
                        dve.wait_ge(o_done, c.o - 2)
                    i = (c.tr + 1) % 2
                    v.tensor_copy(probsT[:, 2 * (n % 2) + 1, 0:nb], banks[4 + i][:, 0:nb]).then_inc(free["td", i], 1)
                    c.up(("td", i))
                    c.tr += 2
                    for i in range(2):
                        dve.wait_ge(o_done, c.o + 1)
                        ob_in(o[:, :, un[i]["job"], :], dv)
                soft(0, units[0])
                for n in range(len(units)):
                    if n + 1 < len(units):
                        soft(n + 1, units[n + 1])
                    values(n, units[n])
                own_o()

            def ob_in(dst, dv):
                i = c.o % 2
                v.tensor_copy(dst, banks[6 + i][:, 0:2 * dv].rearrange("p (t d) -> p t d", t=2)).then_inc(free["o", i], 1)
                c.up(("o", i))
                c.o += 1

            def own_o():
                for i in range(2):
                    dve.wait_ge(free["o", i], c.n["o", i])

            def scaled(o, n, dv):
                for t in range(T):
                    tick(v.tensor_tensor(o[:, t, :, :], o[:, t, :, :], last_bc(cf[:, t, 0:n], dv), ALU.mult))
                own()

            def attn_end():
                own()
                dve.sem_inc(s_attn, 1)
                dve.sem_inc(s_u, 1)

            def project_out(i):
                tr_in(uT, DC, plain)
                uT_ready()
                for j in range(2):
                    evac(u[:, 0, 512 * j:512 * j + 512], u[:, 1, 512 * j:512 * j + 512])
                own_acc()
                dve.sem_inc(s_sq, 1)
                act_does()
                dve.wait_ge(s_gpost, 16 * (i + 1))
                for t in range(T):
                    tick(v.scalar_tensor_tensor(u[:, t, :], u[:, t, :], rstd[:, t:t + 1], gpost[:, :], ALU.mult, ALU.mult))
                own()
                for t in range(T):
                    last = v.tensor_tensor(h[:, t, :], h[:, t, :], u[:, t, :], ALU.add)
                last.then_inc(s_sq, 1)

            def head_norms(x, nh, width, src=None):
                m = nh * width
                for t in range(T):
                    xt = x[:, t, 0:m]
                    link(v.tensor_tensor(TMP[:, 0:m], xt, xt, ALU.mult))
                    link(v.tensor_reduce(ssq[:, nh * t:nh * t + nh], TMP[:, 0:m].rearrange("p (a b) -> p a b", a=nh), AX.X, ALU.add))
                dve.sem_inc(s_sq, 1)
                act_does()
                for t in range(T):
                    xt = x[:, t, 0:m].rearrange("p (a b) -> p a b", a=nh)
                    tick(v.tensor_tensor(xt, xt, last_bc(rstd[:, nh * t:nh * t + nh], width), ALU.mult))
                own()

            for x, val in ((epsc, EPS), (onec, 1.0), (rs[:, :, 0:16], 1.0)):
                tick(v.memset(x, val))
            dve.wait_ge(s_const, 48)
            own()
            cpar = par[:, PC["c"][0]:PC["c"][1]]
            v.tensor_copy(siluc[:, 8:16], cpar).then_inc(s_sq, 1)
            act_does()
            link(v.tensor_tensor(siluc[:, 0:8], siluc[:, 0:8], cpar, ALU.mult))
            v.tensor_copy(cb, last_bc(siluc[:, 0:8], P)).then_inc(s_u, 1)
            posf = lamc[:, 0:2]
            link(v.tensor_copy(posf, posn[:, :]))
            magic = 1.5 * 2.0 ** 23
            two_pi = 2.0 * math.pi
            c1 = float(np.float32(np.round(two_pi * 2 ** 7) / 2 ** 7))
            c2 = float(np.float32(np.round((two_pi - c1) * 2 ** 20) / 2 ** 20))
            c3 = float(np.float32(two_pi - c1 - c2))
            turn = gelu_x[:, 0:32]
            ang = gelu_x[:, 32:64]
            for t in range(T):
                tick(v.tensor_scalar(ang[:, 16 * t:16 * t + 16], cc("freq"), posf[:, t:t + 1], None, ALU.mult))
            own()
            for dst, shift in ((sinr, 0.0), (cosr, 0.25)):
                link(v.tensor_scalar(turn, ang, 1.0 / two_pi, shift, ALU.mult, ALU.add))
                link(v.tensor_scalar(turn, turn, magic, None, ALU.add))
                link(v.tensor_scalar(turn, turn, magic, None, ALU.subtract))
                link(v.scalar_tensor_tensor(dst, turn, -c1, ang, ALU.mult, ALU.add))
                link(v.scalar_tensor_tensor(dst, turn, -c2, dst, ALU.mult, ALU.add))
                link(v.scalar_tensor_tensor(dst, turn, -c3, dst, ALU.mult, ALU.add))
                if shift:
                    link(v.tensor_scalar(dst, dst, math.pi / 2, None, ALU.add))
                link(v.tensor_scalar(dst, dst, 3.1415925, -3.1415925, ALU.min, ALU.max))
            dve.sem_inc(s_sq, 1)
            act_does()
            for j in range(12):
                a, b, f = acc_in()
                v.tensor_copy(mod[:, 512 * j:512 * j + 512], a[:, :]).then_inc(f, 1)
            a, b, f = acc_in()
            v.tensor_copy(modc, a[:, 0:32]).then_inc(f, 1)
            own_acc()
            for k, n in ((0, "g1"), (1, "g2")):
                link(v.tensor_scalar(gs[:, 8 * k:8 * k + 8], modc[:, 16 * k + 8:16 * k + 16], 1.0, None, ALU.add))
                link(v.tensor_tensor(gs[:, 8 * k:8 * k + 8], gs[:, 8 * k:8 * k + 8], par[:, PC[n][0]:PC[n][1]], ALU.mult))
            dve.wait_ge(s_h, 16)
            dve.sem_inc(s_sq, 1)

            norm_in(lambda k: (P, pc("pre", k), None, None))
            for j in range(2):
                evac(flat(QK[:, 4 * j:4 * j + 2, :]), flat(QK[:, 4 * j + 2:4 * j + 4, :]), scale=0.125)
            a, b, f = acc_in()
            for vi, bk in ((0, a), (1, b)):
                y = bk[:, :].rearrange("p (f s) -> p f s", f=2)
                for r in range(2):
                    v.tensor_copy(Xc[0:64, vi, r:r + 3:2, :], y[64 * r:64 * r + 64, :, :])
                    last = v.tensor_copy(Xc[64:128, vi, r:r + 3:2, 0:255], y[64 * r:64 * r + 64, :, 1:256])
            last.then_inc(f, 1)
            own_acc()
            dve.sem_inc(s_x, 1)
            for br in range(2):
                a, b, f = acc_in()
                y = a[:, :].rearrange("p (f s) -> p f s", f=2)
                for r in range(2):
                    for r2 in range(2):
                        g0 = 8 + 4 * br + r
                        v.tensor_copy(QK[64 * r2:64 * r2 + 64, g0:g0 + 3:2, :], y[64 * r:64 * r + 64, :, :])
                v.tensor_copy(V[:, :, 256 * br:256 * br + 256], b[:, :].rearrange("p (t n) -> p t n", t=2)).then_inc(f, 1)
            for j in range(2):
                evac(z[:, 0, 512 * j:512 * j + 512], z[:, 1, 512 * j:512 * j + 512])
            silu_z()
            evac(gate[:, 0, 0:48], gate[:, 1, 0:48], n=48)
            own_acc()
            dve.sem_inc(s_sq, 1)
            silu_end()
            act_does()
            a, b, f = acc_in()
            for vi, bk in ((0, a), (1, b)):
                last = v.tensor_copy(hid[:, 2 * vi:2 * vi + 2, :], bk[:, 0:128].rearrange("p (f n) -> p f n", f=2)[:, :, 0:60])
            last.then_inc(f, 1)
            own_acc()
            link(v.tensor_tensor(gelu_t, gelu_x, gelu_x, ALU.mult))
            link(v.tensor_scalar(gelu_t, gelu_t, 0.044715, 1.0, ALU.mult, ALU.add))
            v.tensor_tensor(gelu_t, gelu_t, gelu_x, ALU.mult).then_inc(s_sq, 1)
            act_does()
            v.tensor_tensor(gelu_x, gelu_x, gelu_t, ALU.mult).then_inc(s_hid, 1)
            tick(v.memset(ob[:, 4096:5120], 0.0))
            tick(v.memset(pb_[:, 1024:2048], 0.0))
            own()
            a, b, f = acc_in()
            for r in range(2):
                v.tensor_copy(kcT[64 * r:64 * r + 64, 0:60], a[0:64, 0:60])
            for r in range(4):
                last = v.tensor_copy(vd[32 * r:32 * r + 15, :, 64 * r:64 * r + 64], b[0:15, 0:256].rearrange("p (g n) -> p g n", g=4))
            last.then_inc(f, 1)
            own_acc()
            dve.sem_inc(s_hid, 1)
            a, b, f = acc_in()
            cbias = cc("cbias").rearrange("p (t h n) -> p t h n", t=2, n=15)
            cmask = cc("cmask").rearrange("p (t n) -> p t n", t=2)
            for t in range(T):
                for r, bk in ((0, a), (1, b)):
                    last = v.tensor_tensor(pc_[:, t, r:16:2, 0:15],
                                           bk[:, 128 * t:128 * t + 128].rearrange("p (h n) -> p h n", n=16)[:, :, 0:15],
                                           cbias[:, t, r:16:2, :], ALU.add)
            last.then_inc(f, 1)
            own_acc()
            for t in range(T):
                link(v.tensor_reduce(ssq, pc_[:, t, :, 0:15], AX.X, ALU.max))
                v.tensor_tensor(pc_[:, t, :, 0:15], pc_[:, t, :, 0:15], last_bc(ssq, 15), ALU.subtract).then_inc(s_sq, 1)
                act_does()
                link(v.tensor_tensor(pc_[:, t, :, 0:15], pc_[:, t, :, 0:15], mid_bc(cmask[:, t, :], 16), ALU.mult))
                link(v.tensor_reduce(ssq, pc_[:, t, :, 0:15], AX.X, ALU.add))
                link(v.tensor_scalar(ssq, ssq, 1e-30, None, ALU.max))
                link(v.reciprocal(ssq, ssq))
                link(v.tensor_tensor(pc_[:, t, :, 0:15], pc_[:, t, :, 0:15], last_bc(ssq, 15), ALU.mult))
            dve.sem_inc(s_hid, 1)
            for _ in range(2):
                dve.wait_ge(tr_done, c.tr + 1)
                i = c.tr % 2
                v.tensor_copy(flat(pcT[:, 4 * (c.tr % 2 if False else _):4 * _ + 4, :]), banks[4 + i][:, :]).then_inc(free["td", i], 1)
                c.up(("td", i))
                c.tr += 1
            oA = o_view(48, 64)
            for g in range(4):
                dve.wait_ge(o_done, c.o + 1)
                i = c.o % 2
                v.tensor_copy(oA[:, :, 4 * g:4 * g + 4, :], banks[6 + i][:, :].rearrange("p (t j d) -> p t j d", t=2, j=4))\
                    .then_inc(free["o", i], 1)
                c.up(("o", i))
                c.o += 1
            dve.wait_ge(s_bias, 1)
            attention(UA, CAUSAL, 64, 48)
            for t in range(T):
                link(v.reciprocal(cf[:, t, 0:48], rs[:, t, 0:48]))
                link(v.tensor_tensor(cf[:, t, 0:48], cf[:, t, 0:48], gate[:, t, 0:48], ALU.mult))
            scaled(oA, 48, 64)

            def osum(o, t, j, n):
                return o[:, t, j:j + n, :].rearrange("p j d -> p (j d)")
            for t in range(T):
                link(v.tensor_tensor(u[:, t, :], osum(oA, t, 0, 16), osum(oA, t, 16, 16), ALU.add))
                link(v.tensor_tensor(u[:, t, :], u[:, t, :], osum(oA, t, 32, 16), ALU.add))
                link(v.tensor_tensor(u[:, t, :], u[:, t, :], z[:, t, :], ALU.mult))
            attn_end()
            project_out(0)

            def qkv(nq, nk):
                for j in range(nq + nk):
                    a, b, f = acc_in()
                    for x, t0 in ((a, 4 * j), (b, 4 * j + 2)):
                        for y in range(2):
                            last = v.tensor_scalar(QK[:, t0 + y, :], x[:, 256 * y:256 * y + 256],
                                                   0.125 if t0 + y < 2 * (nq + nk) else 1.0, None, ALU.mult)
                    last.then_inc(f, 1)
                for dst in (V, z):
                    for j in range(2):
                        evac(dst[:, 0, 512 * j:512 * j + 512], dst[:, 1, 512 * j:512 * j + 512])
                silu_z()
                silu_end()

            norm_in(lambda k: (P, pc("pre", DC + k), None, None))
            qkv(2, 2)
            lam_init = 0.8 - 0.6 * math.exp(-0.3 * 1)
            dve.wait_ge(s_lam, 32)
            l4 = lamb.rearrange("p (a b) -> p a b", b=64)
            link(v.tensor_tensor(TMP[:, 0:128].rearrange("p (a b) -> p a b", a=2), l4[:, 0:3:2, :], l4[:, 1:4:2, :], ALU.mult))
            link(v.tensor_reduce(lamc[:, 0:2], TMP[:, 0:128].rearrange("p (a b) -> p a b", a=2), AX.X, ALU.add))
            dve.sem_inc(s_sq, 1)
            act_does()
            link(v.tensor_tensor(lamc[:, 2:3], lamc[:, 1:2], lamc[:, 0:1], ALU.subtract))
            link(v.tensor_scalar(lamc[:, 2:3], lamc[:, 2:3], -lam_init, None, ALU.add))
            dve.wait_ge(s_bias, 2)
            attention(UB, CAUSAL, 128, 16)
            for t in range(T):
                link(v.reciprocal(cf[:, t, 0:16], rs[:, t, 0:16]))
                odd = cf[:, t, 1:16:2]
                link(v.tensor_scalar(odd, odd, lamc[:, 2:3], None, ALU.mult))
            oB = o_view(16, 128)
            scaled(oB, 16, 128)
            for t in range(T):
                pairs = oB[:, t, :, :].rearrange("p (a m) d -> p m a d", m=2)
                ut = u[:, t, :].rearrange("p (a d) -> p a d", d=128)
                link(v.tensor_tensor(ut, pairs[:, 0, :, :], pairs[:, 1, :, :], ALU.add))
            head_norms(u, 8, 128)
            for t in range(T):
                ut = u[:, t, :].rearrange("p (a d) -> p a d", d=128)
                link(v.scalar_tensor_tensor(ut, ut, 1.0 - lam_init, mid_bc(subg, 8), ALU.mult, ALU.mult))
                link(v.tensor_tensor(u[:, t, :], u[:, t, :], z[:, t, :], ALU.mult))
            attn_end()
            project_out(1)

            norm_in(lambda k: (P, pc("pre", 2 * DC + k), None, None))
            qkv(1, 2)
            dve.wait_ge(s_bias, 3)
            attention(UC, CAUSAL, 256, 12)
            M4 = ssq[:, 0:8].rearrange("p (t h) -> p t h", t=2)
            link(v.tensor_tensor(M4, nm[:, :, 0:4], nm[:, :, 4:8], ALU.min))
            link(v.tensor_tensor(M4, M4, nm[:, :, 8:12], ALU.min))
            for g in range(3):
                tick(v.tensor_tensor(cf[:, :, 4 * g:4 * g + 4], M4, nm[:, :, 4 * g:4 * g + 4], ALU.subtract))
            own()
            dve.sem_inc(s_sq, 1)
            act_does()
            link(v.tensor_tensor(rs[:, :, 0:12], rs[:, :, 0:12], cf[:, :, 0:12], ALU.mult))
            link(v.tensor_tensor(M4, rs[:, :, 0:4], rs[:, :, 4:8], ALU.add))
            link(v.tensor_tensor(M4, M4, rs[:, :, 8:12], ALU.add))
            link(v.reciprocal(M4, M4))
            for g in range(3):
                tick(v.tensor_tensor(cf[:, :, 4 * g:4 * g + 4], cf[:, :, 4 * g:4 * g + 4], M4, ALU.mult))
            own()
            oC = o_view(12, 256)
            scaled(oC, 12, 256)
            for t in range(T):
                link(v.tensor_tensor(u[:, t, :], osum(oC, t, 0, 4), osum(oC, t, 4, 4), ALU.add))
                link(v.tensor_tensor(u[:, t, :], u[:, t, :], osum(oC, t, 8, 4), ALU.add))
                link(v.tensor_tensor(u[:, t, :], u[:, t, :], z[:, t, :], ALU.mult))
            attn_end()
            project_out(2)

            norm_in(lambda k: (P, pc("pre", 3 * DC + k), None, None))
            qkv(2, 2)
            dve.sem_inc(s_qkv, 1)
            oD = o_view(16, 64)
            for i in range(17):
                if i < 16:
                    bk = banks[2 * ((acc_before_D + i) % 2)]
                    dve.wait_ge(s_abs, i + 1)
                    link(v.scalar_tensor_tensor(lom[i % 2], bk[:, 0:384], 0.0, sp_[i % 2], ALU.max, ALU.add))
                    v.tensor_tensor(lom[i % 2][:, 0:256], lom[i % 2][:, 0:256], cc("strict"), ALU.mult)
                    v.tensor_scalar(lom[i % 2][:, 256:384], lom[i % 2][:, 256:384], -1.0, None, ALU.mult).then_inc(s_lom, 1)
                if i >= 1:
                    dve.wait_ge(o_done, c.o + 1)
                    ob_in(oD[:, :, i - 1, :], 64)
            own_o()
            c.acc += 16
            for t in range(T):
                link(v.tensor_tensor(u[:, t, :], osum(oD, t, 0, 16), z[:, t, :], ALU.mult))
            attn_end()
            project_out(3)

            norm_in(lambda k: (P, gs[:, k:k + 1], modc[:, k:k + 1], ALU.add))
            for dst in (NQ, NK):
                evac(dst[:, 0, :], dst[:, 1, :])
            evac(V[:, 0, 0:512], V[:, 1, 0:512])
            evac(LAT[:, 0, :], LAT[:, 1, :], n=416)
            for dst in (z, u):
                for j in range(2):
                    evac(dst[:, 0, 512 * j:512 * j + 512], dst[:, 1, 512 * j:512 * j + 512])
            own_acc()
            for _ in range(2):
                dve.sem_inc(s_sq, 1)
            act_does()
            act_does()
            head_norms(NQ, 8, 64)
            head_norms(NK, 8, 64)
            for a, n, at in ((0, 256, 0), (256, 128, 2)):
                for t in range(T):
                    x = LAT[:, t, a:a + n]
                    link(v.tensor_tensor(TMP[:, 0:n], x, x, ALU.mult))
                    link(v.tensor_reduce(ssq[:, at + t:at + t + 1], TMP[:, 0:n], AX.X, ALU.add))
            dve.sem_inc(s_sq, 1)
            act_does()
            for a, n, at in ((0, 256, 0), (256, 128, 2)):
                for t in range(T):
                    tick(v.tensor_scalar(LAT[:, t, a:a + n], LAT[:, t, a:a + n], rstd[:, at + t:at + t + 1], None, ALU.mult))
            own()
            dve.sem_inc(s_u, 1)
            tr_in(QK[:, 0:4, :], 4, lambda k: (P, pc("naq"), 0.125, ALU.mult))
            tr_in(QK[:, 4:8, :], 4, lambda k: (P, pc("nak"), None, None))
            tr_in(uT, 3, lambda k: (P, pc("qlat", k) if k < 2 else pc("kvlat"), None, None))
            uT_ready()
            cos2 = cosr.rearrange("p (t n) -> p t n", t=2)
            sin2 = sinr.rearrange("p (t n) -> p t n", t=2)

            def rope(dst, x, nh):
                for t in range(T):
                    x1, x2 = x[t][:, :, 0:16], x[t][:, :, 16:32]
                    co, si = mid_bc(cos2[:, t, :], nh), mid_bc(sin2[:, t, :], nh)
                    y = [TMP[:, 128 * k:128 * k + 16 * nh].rearrange("p (h n) -> p h n", h=nh) for k in range(4)]
                    for d, p_, q_ in ((0, x1, co), (1, x2, si), (2, x2, co), (3, x1, si)):
                        tick(v.tensor_tensor(y[d], p_, q_, ALU.mult))
                    own()
                    tick(v.tensor_tensor(dst[t][:, :, 0:16], y[0], y[1], ALU.subtract))
                    tick(v.tensor_tensor(dst[t][:, :, 16:32], y[2], y[3], ALU.add))
                    own()
            rope([KR[:, t:t + 1, :] for t in range(T)],
                 [LAT[:, t, 384:416].rearrange("p (h n) -> p h n", h=1) for t in range(T)], 1)
            for t in range(T):
                evac(MQ[:, t, 0:384], MQ[:, t, 384:768], n=384)
            for t in range(T):
                a, b, f = acc_in()
                for j, bk in ((0, a), (1, b)):
                    y = bk[:, :].rearrange("p (h n) -> p h n", n=128)
                    v.tensor_copy(MK[:, t, 384 * j:384 * j + 384].rearrange("p (h n) -> p h n", n=96)[:, :, 0:64], y[:, :, 0:64])
                    last = v.tensor_copy(V[:, t, 512 + 256 * j:768 + 256 * j].rearrange("p (h n) -> p h n", n=64), y[:, :, 64:128])
                last.then_inc(f, 1)
            own_acc()
            for t in range(T):
                tick(v.tensor_copy(MK[:, t, :].rearrange("p (h n) -> p h n", n=96)[:, :, 64:96], mid_bc(KR[:, t, :], 8)))
            qr = [MQ[:, t, :].rearrange("p (h n) -> p h n", n=96)[:, :, 64:96] for t in range(T)]
            rope(qr, qr, 8)
            head_norms(MQ, 8, 96)
            head_norms(MK, 8, 96)
            dve.sem_inc(s_u, 1)
            tr_in(QK[:, 8:16, :], 8, lambda k: (96, pc("mlaq", 0, 96), 96 ** -0.5, ALU.mult))
            tr_in(uT, 8, lambda k: (96, pc("mlak", 0, 96), None, None))
            tr_own()
            dve.wait_ge(s_bias, 4)
            attention(UN, FULL, 64, 16)
            attention(UM, FULL, 64, 16)
            oN = o_view(16, 64)
            for t in range(T):
                link(v.reciprocal(cf[:, t, 0:16], rs[:, t, 0:16]))
            for t in range(T):
                tick(v.tensor_tensor(ym[:, t, :].rearrange("p (j d) -> p j d", d=64), oN[:, t, :, :], last_bc(cf[:, t, 0:16], 64), ALU.mult))
            attn_end()
            tr_in(uT, DC, plain)
            uT_ready()
            for t in range(T):
                a, b, f = acc_in()
                v.tensor_tensor(MG[:, t, 0:512], a[:, :], z[:, t, 0:512], ALU.mult)
                v.tensor_tensor(MG[:, t, 512:1024], b[:, :], z[:, t, 512:1024], ALU.mult).then_inc(f, 1)
            for t in range(T):
                a, b, f = acc_in()
                v.tensor_tensor(MG2[:, t, 0:512], a[:, :], u[:, t, 0:512], ALU.mult)
                v.tensor_tensor(MG2[:, t, 512:1024], b[:, :], u[:, t, 512:1024], ALU.mult).then_inc(f, 1)
            own_acc()
            v.tensor_tensor(ob[:, 2048:4096], ob[:, 2048:4096], ob[:, 4096:6144], ALU.add).then_inc(s_u, 1)
            tr_in(uT, DC, plain)
            uT_ready()
            for j in range(2):
                a, b, f = acc_in()
                g1 = mod[:, 2 * D + 512 * j:2 * D + 512 * j + 512]
                v.tensor_tensor(u[:, 0, 512 * j:512 * j + 512], a[:, :], g1, ALU.mult)
                v.tensor_tensor(u[:, 1, 512 * j:512 * j + 512], b[:, :], g1, ALU.mult).then_inc(f, 1)
            own_acc()
            v.tensor_tensor(h_[:, :], h_[:, :], u_[:, :], ALU.add).then_inc(s_sq, 1)
            norm_in(lambda k: (P, gs[:, 8 + k:9 + k], modc[:, 16 + k:17 + k], ALU.add))

            pair = acc_router % 2
            dve.wait_ge(free["a", pair], 8 + 1)
            sc = gate[:, :, 0:64]
            sel, rep, m8, tmp = rt[0], rt[1], rt[2], rt[3]
            for t in range(T):
                tick(v.tensor_tensor(sel[:, 64 * t:64 * t + 64], sc[:, t, :], ebias, ALU.add))
            own()
            for g in range(16):
                tick(v.max(m8[:, 8 * g:8 * g + 8], sel[:, 8 * g:8 * g + 8]))
            own()
            m83 = m8.rearrange("p (g k) -> p g k", k=8)
            gsc, rk, wsum = rt[4][:, 0:16], rt[4][:, 16:32], rt[4][:, 32:34]
            link(v.tensor_tensor(gsc, m83[:, :, 0], m83[:, :, 1], ALU.add))
            for t in range(T):
                gi = last_bc(gsc[:, 8 * t:8 * t + 8], 8)
                gj = mid_bc(gsc[:, 8 * t:8 * t + 8], 8)
                x, y = rank[:, 0:64].rearrange("p (i j) -> p i j", i=8), rank[:, 64:128].rearrange("p (i j) -> p i j", i=8)
                tick(v.tensor_tensor(x, gj, gi, ALU.is_gt))
                link(v.tensor_tensor(y, gj, gi, ALU.is_equal))
                link(v.tensor_tensor(y, y, cc("lower").rearrange("p (i j) -> p i j", i=8), ALU.mult))
                link(v.tensor_tensor(x, x, y, ALU.add))
                link(v.tensor_reduce(rk[:, 8 * t:8 * t + 8], x, AX.X, ALU.add))
            link(v.tensor_scalar(rk, rk, 3.5, None, ALU.is_lt))
            s3 = sel.rearrange("p (g k) -> p g k", k=8)
            link(v.tensor_tensor(s3, s3, last_bc(rk, 8), ALU.mult))
            link(v.tensor_scalar(rk, rk, 1.0, BIG, ALU.subtract, ALU.mult))
            link(v.tensor_tensor(s3, s3, last_bc(rk, 8), ALU.add))
            for t in range(T):
                link(v.max(m8[:, 8 * t:8 * t + 8], sel[:, 64 * t:64 * t + 64]))
                link(v.match_replace(rep[:, 64 * t:64 * t + 64], m8[:, 8 * t:8 * t + 8], sel[:, 64 * t:64 * t + 64], -2 * BIG))
            link(v.tensor_scalar(rep, rep, -1.5 * BIG, None, ALU.is_lt))
            for t in range(T):
                link(v.tensor_tensor(sc[:, t, :], sc[:, t, :], rep[:, 64 * t:64 * t + 64], ALU.mult))
                link(v.tensor_reduce(wsum[:, t:t + 1], sc[:, t, :], AX.X, ALU.add))
            link(v.reciprocal(wsum, wsum))
            for t in range(T):
                link(v.tensor_scalar(sc[:, t, :], sc[:, t, :], wsum[:, t:t + 1], ROUTED_SCALE, ALU.mult, ALU.mult))
            dve.sem_inc(s_r1, 1)
            dve.wait_ge(s_aux, 1)
            link(v.tensor_scalar(active, banks[2][0:64, 0:1], 0.5, None, ALU.is_gt))
            link(v.tensor_copy(gT, banks[3][0:64, 0:256]))
            dve.sem_inc(s_r2, 1)
            dve.wait_ge(s_aux, 2)
            link(v.tensor_copy(rankc, banks[2][0:64, 1:2]))
            link(v.tensor_scalar(order, cc("negiota")[0:64, :], rankc, active, ALU.is_equal, ALU.mult))
            link(v.tensor_scalar(todo[0:1, 64:65], banks[2][0:1, 2:3], 0.5, 0.25, ALU.mult, ALU.add))
            dve.sem_inc(s_r2, 1)
            dve.wait_ge(s_aux, 3)
            tick(v.tensor_copy(todo[0:1, 0:64], banks[2][0:1, 8:72]))
            tick(v.tensor_copy(gate[:, :, 1:65], banks[3][:, 0:128].rearrange("p (t n) -> p t n", t=2)))
            tick(v.memset(zeros_, 0.0))
            own()
            tick(v.memset(gate[:, :, 0:1], 1.0))
            own()
            dve.sem_inc(s_moe, 1)

            for t in range(T):
                dve.wait_ge(s_ge, t + 1)
                link(v.tensor_tensor(ge[t], ge[t], banks[t][:, 0:FF], ALU.mult))
                v.scalar_tensor_tensor(ma[t], ge[t], gate[:, t, 0:1], banks[t][:, FF:2 * FF], ALU.mult, ALU.mult).then_inc(s_ga, 1)
            pairs = dve.value_load(todo[0:1, 64:65], min_val=TOPK // 2, max_val=EXPERTS // 2)
            with dve.Fori(0, pairs) as it:
                dve.wait_ge(s_ga, 4 * it + 2)
                v.tensor_copy(gcur[:, :, 0:2], gate[:, :, bass.ds(it * 2 + 1, 2)]).then_inc(s_gc, 1)
                dve.wait_ge(s_gc, it + 1)
                for j in range(MOE_SLOTS):
                    for t in range(T):
                        n0 = it * 4 + 2 * j + t
                        dve.wait_ge(s_ge, n0 + 3)
                        v.tensor_tensor(ge[t], ge[t], banks[t][:, 0:FF], ALU.mult).then_inc(s_mc, 1)
                        dve.wait_ge(s_mc, n0 + 1)
                        dve.wait_ge(s_gat, n0 + 1)
                        v.scalar_tensor_tensor(ma[t], ge[t], gcur[:, t, j:j + 1], banks[t][:, FF:2 * FF],
                                               ALU.mult, ALU.mult).then_inc(s_ga, 1)
            dve.wait_ge(s_all, 1)
            for t in range(T):
                for n in range(2):
                    tick(v.tensor_tensor(u[:, t, 512 * n:512 * n + 512], banks[4 + 2 * t + n][:, :],
                                         mod[:, 5 * D + 512 * n:5 * D + 512 * n + 512], ALU.mult))
            own()
            v.tensor_tensor(u_[:, :], u_[:, :], h_[:, :], ALU.add).then_inc(s_fin, 1)


_WEIGHTS = ["x", "norm_post", "a_w_in", "a_w_out", "a_cmp_w1_k", "a_cmp_w2_k", "a_cmp_w1_v", "a_cmp_w2_v", "b_w_in",
            "b_w_out", "b_lambda", "b_sub_gain", "c_w_in", "c_w_out", "d_w_in", "d_w_out", "w_ada_2", "b_ada_2",
            "w_in_2", "na_rpb_2", "w_uq_2", "w_ukv_2", "w_proj_na_2", "w_proj_mla_2", "w_out_2", "w_router_2",
            "e_bias_2", "w_exp_gate_2", "w_exp_up_2", "w_exp_down_2", "w_sh_gate_2", "w_sh_up_2", "w_sh_down_2"]


def kernel(**inputs):
    import concourse.bacc as _bacc
    from concourse import mybir as _mybir
    from concourse.bass_utils import run_bass_kernel_spmd as _run

    def cols(a, k):
        return np.asarray(a).reshape(k, P).T

    f = {k: np.asarray(x) for k, x in inputs.items()}
    par = np.zeros((P, PC_N), np.float32)

    def put(name, a):
        par[0:a.shape[0], PC[name][0]:PC[name][1]] = a
    put("pre", cols(f["norm_pre"].reshape(-1), 4 * DC))
    put("g1", cols(f["g_norm1_2"], DC))
    put("g2", cols(f["g_norm2_2"], DC))
    put("c", cols(f["c_2"], DC))
    put("naq", np.concatenate([f["g_na_q_2"][0]] * 2)[:, None])
    put("nak", np.concatenate([f["g_na_k_2"][0]] * 2)[:, None])
    put("qlat", cols(f["g_q_lat_2"], 2))
    put("kvlat", cols(f["g_kv_lat_2"], 1))
    put("mlaq", f["g_mla_q_2"][0][:, None])
    put("mlak", f["g_mla_k_2"][0][:, None])
    put("posk", cols(f["a_cmp_pos_k"], 16))
    put("posv", cols(f["a_cmp_pos_v"], 16))
    nc = _bacc.Bacc("TRN2", target_bir_lowering=False, num_devices=1)
    given = {n: f[n] for n in _WEIGHTS}
    given["params"] = par
    given["shape_consts"] = shape_constants()
    given["na_rpb_2"] = f["na_rpb_2"][..., ::-1]
    given["pos_cols"] = f["positions_2"].reshape(T, P).T
    arrays, aps = {}, {}
    for n, a in given.items():
        a = np.ascontiguousarray(a)
        arrays[f"in_{n}"] = a
        aps[n] = nc.dram_tensor(f"in_{n}", a.shape, _mybir.dt.from_np(a.dtype), kind="ExternalInput").ap()
    out = nc.dram_tensor("out_x", (1, S, D), _mybir.dt.float32, kind="ExternalOutput").ap()
    build(nc, aps, out)
    r = _run(nc, [arrays], core_ids=[0])
    return r.results[0]["out_x"]
```

```python
import math
import numpy as np
import concourse.bass as bass
from concourse import mybir
from contextlib import ExitStack

S, D, P, T = 256, 1024, 128, 2
DC = D // P
HD = 64
RING = 3
SLOT = 4096
N_CMP, CMP_L, CMP_ST = 15, 32, 16
A_COLS = dict(q=0, kc=1024, vc=1280, ks=1536, vs=1792, kw=2048, vw=2304, gl=2560, z=2608)
EXPERTS, FF, TOPK, GROUPS = 64, 256, 8, 8
ROUTED_SCALE = 2.5
EPS = 1e-6
BIG = 1e30
MOE_SLOTS = 2

PC = {}
_at = 0
for _n, _w in (("pre", 4 * DC), ("g1", DC), ("g2", DC), ("c", DC), ("naq", 1), ("nak", 1), ("qlat", 2),
               ("kvlat", 1), ("mlaq", 1), ("mlak", 1), ("posk", 16), ("posv", 16)):
    PC[_n] = (_at, _at + _w)
    _at += _w
PC_N = _at

CC = {}
_at = 0
for _n, _w in (("dist", 4 * 256), ("win", 256), ("cbias", 480), ("cmask", 30), ("strict", 256),
               ("tri", 128), ("lower", 64), ("freq", 16), ("negiota", 64), ("row", 1)):
    CC[_n] = (_at, _at + _w)
    _at += _w
CC_N = _at


def slopes(n):
    return [2.0 ** (-8.0 * (i + 1) / n) for i in range(n)]


def shape_constants():
    a = np.zeros((P, CC_N), np.float32)
    p = np.arange(P)[:, None]
    dist = P + p - np.arange(2 * P)[None, :]
    ok = dist >= 0
    pats = [ok, ok & (dist <= 128), ok & (dist % 4 == 0), ok & (dist % 16 == 0)]
    a[:, CC["dist"][0]:CC["dist"][1]] = np.stack([np.where(m, dist, BIG) for m in pats], 1).reshape(P, -1)
    col = p % 64
    kcol = 63 - np.arange(256)[None, :] % 64
    start = np.clip(col - 8, 0, 48)
    a[:, CC["win"][0]:CC["win"][1]] = np.where((kcol >= start) & (kcol < start + 16), 0.0, -BIG)
    end = CMP_ST * np.arange(N_CMP) + CMP_L - 1
    tok = np.arange(2)[None, :, None] * P + np.arange(P)[:, None, None]
    cd = tok - end[None, None, :]
    sl = np.array(slopes(16), np.float32)
    cb = np.where(cd[:, :, None, :] >= 0, -sl[None, None, :, None] * cd[:, :, None, :].astype(np.float32), -BIG)
    a[:, CC["cbias"][0]:CC["cbias"][1]] = cb.reshape(P, -1)
    a[:, CC["cmask"][0]:CC["cmask"][1]] = (cd >= 0).reshape(P, -1)
    q = np.arange(P)[None, :]
    neg = -(p < q).astype(np.float32)
    a[:, CC["strict"][0]:CC["strict"][1]] = np.concatenate([neg, neg], 1)
    a[:, CC["tri"][0]:CC["tri"][1]] = (p >= q)
    i, j = np.arange(8)[:, None], np.arange(8)[None, :]
    a[:, CC["lower"][0]:CC["lower"][1]] = (j < i).reshape(1, 64)
    a[:, CC["freq"][0]:CC["freq"][1]] = (np.float32(10000.0) ** (-np.arange(16, dtype=np.float32) / np.float32(16)))[None, :]
    a[:, CC["negiota"][0]:CC["negiota"][1]] = -np.arange(64)[None, :]
    a[:, CC["row"][0]:CC["row"][1]] = p
    return a


def build(nc, A, out):
    f32 = mybir.dt.float32
    f32r = mybir.dt.float32r
    i32 = mybir.dt.int32
    ALU = mybir.AluOpType
    ACT = mybir.ActivationFunctionType
    AX = mybir.AxisListType
    ctx = ExitStack()
    with ctx:
        def sb(name, *shape, dt=f32, stack=ctx):
            return stack.enter_context(nc.sbuf_tensor(name, [shape[0], int(np.prod(shape[1:]))], dt))

        def sem(name):
            return ctx.enter_context(nc.semaphore(name))

        ident = sb("ident", P, 128)
        cst = sb("shape_consts", P, CC_N)
        par = sb("params", P, PC_N)
        h_ = sb("h", P, T * D)
        u_ = sb("u", P, T * D)
        uT_ = sb("uT", P, DC * S)
        V_ = sb("V", P, T * D)
        mod = sb("mod", P, 6 * D)
        pb_ = sb("probs", P, 2 * 1024)
        pT_ = sb("probsT", P, 4 * 512)
        w2_ = sb("w2", P, 4 * 64)
        kcT = sb("kcmpT", P, 64)
        ones = sb("ones", P, 128)
        lam_ = sb("lambda_subgain", P, 384)
        sm = sb("small", P, 1120)
        posn = sb("positions", P, 2, dt=i32)
        todo = sb("expert_list", 1, 66, dt=i32)

        with ExitStack() as layers:
            ring = [sb(f"ring{i}", P, SLOT, stack=layers) for i in range(RING)]
            QK_ = sb("QK", P, 16 * S, stack=layers)
            ob = sb("oraw", P, 6144, stack=layers)
            bias_ = sb("bias", P, 16 * 256, stack=layers)
            z_ = sb("z", P, T * D, stack=layers)
            gpost = sb("gpost", P, D, stack=layers)
        gu_lo = [sb(f"gate_up_low{j}", P, SLOT, dt=f32r) for j in range(MOE_SLOTS)]
        dn_lo = sb("down_low", P, SLOT, dt=f32r)
        gu_hi = [sb(f"gate_up_high{j}", P, SLOT, dt=f32r) for j in range(MOE_SLOTS)]
        dn_hi = sb("down_high", P, SLOT, dt=f32r)
        uT_hi = sb("uT_high", P, DC * S, dt=f32r)
        uT_lo = sb("uT_low", P, DC * S, dt=f32r)
        ma_hi = sb("act_high", P, 2 * 256, dt=f32r)
        ma_lo = sb("act_low", P, 2 * 256, dt=f32r)

        h = h_[:, :].rearrange("p (t n) -> p t n", t=T)
        u = u_[:, :].rearrange("p (t n) -> p t n", t=T)
        uT = uT_[:, :].rearrange("p (c s) -> p c s", s=S)
        QK = QK_[:, :].rearrange("p (c s) -> p c s", s=S)
        V = V_[:, :].rearrange("p (t n) -> p t n", t=T)
        z = z_[:, :].rearrange("p (t n) -> p t n", t=T)
        bias = bias_[:, :].rearrange("p (h k) -> p h k", k=256)
        probs = pb_[:, :].rearrange("p (u t i k) -> p u t i k", u=2, t=2, i=2)
        probsT = pT_[:, :].rearrange("p (b n) -> p b n", n=512)
        w2 = w2_[:, :].rearrange("p (v c n) -> p v c n", v=2, c=2)

        def small(a, n):
            return sm[:, a:a + n]
        ssq, lnv, rstd = small(0, 16), small(16, 16), small(32, 16)
        rs = small(64, 96).rearrange("p (t j) -> p t j", t=2)
        nm = small(160, 96).rearrange("p (t j) -> p t j", t=2)
        cf = small(256, 96).rearrange("p (t j) -> p t j", t=2)
        gate = small(352, 132).rearrange("p (t j) -> p t j", t=2)
        epsc, onec, zeroc = small(484, 1), small(485, 1), small(486, 1)
        lamc = small(488, 8)
        gcur = small(496, 8).rearrange("p (t j) -> p t j", t=2)
        cosr = small(512, 32)
        sinr = small(544, 32)
        modc = small(576, 32)
        gs = small(608, 16)
        siluc = small(624, 16)
        gelu_x, gelu_t = small(640, 240), small(880, 240)
        rank = small(640, 256)

        psum = ctx.enter_context(nc.psum_tensor("psum", [P, 8 * 512], f32))
        banks = [psum[:, 512 * i:512 * i + 512] for i in range(8)]

        s_const, s_h, s_gpost, s_small = sem("consts_in"), sem("h_in"), sem("gpost_in"), sem("smalls_in")
        s_rpb, s_lam, s_row, s_rt, s_out = sem("rpb_in"), sem("lambda_in"), sem("b_ada_in"), sem("router_in"), sem("out_done")
        w_in = [sem(f"weights_in{i}") for i in range(RING)]
        acc_done = sem("acc_done")
        free = {("d", 0): sem("acc0_free_dve"), ("d", 1): sem("acc1_free_dve"),
                ("a", 0): sem("acc0_free_act"), ("a", 1): sem("acc1_free_act"),
                ("td", 0): sem("tr0_free_dve"), ("td", 1): sem("tr1_free_dve"),
                ("ta", 0): sem("tr0_free_act"), ("ta", 1): sem("tr1_free_act"),
                ("o", 0): sem("o0_free"), ("o", 1): sem("o1_free")}
        tr_done = sem("transposes_done")
        o_done = sem("o_done")
        dch, ach, pch, pech = sem("dve_chain"), sem("act_chain"), sem("pool_chain"), sem("pe_chain")
        s_sq = sem("ready_for_rstd")
        s_rstd = sem("act_result")
        s_u = sem("u_ready")
        s_uT = sem("uT_ready")
        s_qkv = sem("qkv_ready")
        s_mx = sem("max_ready")
        s_p = sem("probs_ready")
        s_bias = sem("bias_ready")
        s_attn = sem("attn_done")
        s_x = sem("cmp_in_ready")
        s_xp = sem("cmp_windows_ready")
        s_hid = sem("cmp_hidden_ready")
        s_cum = sem("cumsum_done")
        s_lom = sem("log_om_ready")
        s_abs = sem("softplus_parts_ready")
        s_am = sem("stick_weights_ready")
        s_id = sem("ident_ready")
        gu_in = [sem(f"gate_up_in{i}") for i in range(MOE_SLOTS)]
        dn_in = [sem(f"down_in{i}") for i in range(MOE_SLOTS)]
        s_gu, s_dn = sem("gate_up_done"), sem("down_done")
        s_ge, s_ga, s_gat = sem("moe_exp"), sem("moe_act"), sem("moe_act_transposed")
        s_ah, s_al = sem("moe_actT_high"), sem("moe_actT_low")
        s_gh, s_gl = sem("gate_up_high_ready"), sem("gate_up_low_ready")
        s_dh, s_dl = sem("down_high_ready"), sem("down_low_ready")
        s_uh, s_ul = sem("uT_high_ready"), sem("uT_low_ready")
        s_moe = sem("moe_gates_ready")
        s_fin = sem("final_ready")
        s_r1, s_r2, s_aux = sem("expert_masks_ready"), sem("expert_ranks_ready"), sem("expert_sums_done")
        s_all = sem("experts_done")
        s_gc, s_mc = sem("moe_weights_copied"), sem("moe_chain")

        guv = [ring[j][:, :].rearrange("p (c n) -> p c n", n=2 * FF) for j in range(MOE_SLOTS)]
        dnv = [ring[2][:, 2048 * j:2048 * j + 2048].rearrange("p (c n) -> p c n", n=D) for j in range(MOE_SLOTS)]
        gu_ = [[x[j][:, :].rearrange("p (c n) -> p c n", n=2 * FF) for x in (gu_hi, gu_lo)] for j in range(MOE_SLOTS)]
        dn_ = [[x[:, 2048 * j:2048 * j + 2048].rearrange("p (c n) -> p c n", n=D) for x in (dn_hi, dn_lo)] for j in range(MOE_SLOTS)]
        uT2 = [x[:, :].rearrange("p (c s) -> p c s", s=S) for x in (uT_hi, uT_lo)]
        ma2 = [[x[:, 256 * t:256 * t + 256] for x in (ma_hi, ma_lo)] for t in range(T)]
        PARTS = ((0, 0), (0, 1), (1, 0))

        class Count:
            def __init__(self):
                self.acc = self.tr = self.o = self.w = 0
                self.win = [0] * RING
                self.n = {}

            def up(self, name, by=1):
                self.n[name] = self.n.get(name, 0) + by
                return self.n[name]

        class Own:
            def __init__(self, eng, s):
                self.eng, self.s, self.n = eng, s, 0

            def tick(self, ins):
                self.n += 1
                ins.then_inc(self.s, 1)

            def own(self):
                self.eng.wait_ge(self.s, self.n)

            def link(self, ins):
                self.tick(ins)
                self.own()

        def pc(name, i=0, p=P):
            a = PC[name][0] + i
            return par[0:p, a:a + 1]

        def cc(name):
            return cst[:, CC[name][0]:CC[name][1]]

        dist = cc("dist").rearrange("p (m k) -> p m k", k=256)
        tri = cc("tri")

        def last_bc(ap, n):
            return bass.AP(ap.tensor, ap.offset, [*ap.ap, [0, n]])

        def mid_bc(ap, n):
            return bass.AP(ap.tensor, ap.offset, [ap.ap[0], [0, n], *ap.ap[1:]])

        def row_bc(ap, n):
            return bass.AP(ap.tensor, ap.offset, [[0, P], [1, n]])

        def head(q, k, job, v, bidx):
            return dict(q=q, k=k, job=job, v=v, b=bidx)

        def o_view(n, dv):
            return ob[:, 0:2 * n * dv].rearrange("p (t j d) -> p t j d", t=2, j=n)

        UA, UB, UC, UN, UM = [], [], [], [], []
        for br in range(2):
            for hp in range(8):
                UA.append([head(QK[64 * i:64 * i + 64, hp, :], QK[64 * i:64 * i + 64, 8 + 4 * br + hp // 2, :],
                                16 + 16 * br + 2 * hp + i, (256 * br + 64 * (hp // 2), 64), 2 * hp + i) for i in range(2)])
        for hh in range(8):
            UB.append([head(QK[64 * i:64 * i + 64, hh, :], QK[64 * i:64 * i + 64, 8 + hh, :],
                            2 * hh + i, (128 * hh, 128), 2 * hh + i) for i in range(2)])
        for x in range(6):
            UC.append([head(QK[64 * i:64 * i + 64, x, :], QK[64 * i:64 * i + 64, 6 + x, :],
                            2 * x + i, (256 * ((2 * x + i) % 4), 256), 2 * x + i) for i in range(2)])
        for x in range(4):
            UN.append([head(QK[64 * i:64 * i + 64, x, :], QK[64 * i:64 * i + 64, 4 + x, :],
                            2 * x + i, (64 * (2 * x + i), 64), 2 * x + i) for i in range(2)])
            UM.append([head(QK[0:96, 8 + 2 * x + i, :], uT[0:96, 2 * x + i, :],
                            8 + 2 * x + i, (512 + 64 * (2 * x + i), 64), None) for i in range(2)])
        CAUSAL, FULL = [(1, 0), (1, 1), (0, 0)], [(1, 0), (1, 1), (0, 0), (0, 1)]
        LAYERS = ((UA, CAUSAL, 48, 64), (UB, CAUSAL, 16, 128), (UC, CAUSAL, 12, 256))

        Xc = ob[:, 0:2048].rearrange("p (v g s) -> p v g s", v=2, g=4)
        Xp = ob[:, 2048:2048 + 1920].rearrange("p (v l n) -> p v l n", v=2, l=16)
        hid = gelu_x.rearrange("p (f n) -> p f n", n=60)
        vd = ob[:, 4096:5120].rearrange("p (g n) -> p g n", g=4)
        pc_ = pb_[:, 1024:2048].rearrange("p (t h n) -> p t h n", t=2, n=32)
        pcT = u_[:, 0:1024].rearrange("p (b q) -> p b q", q=128)
        sp_ = [bias_[:, 384 * i:384 * i + 384] for i in range(2)]
        lom = [bias_[:, 768 + 384 * i:1152 + 384 * i] for i in range(2)]
        am = [bias_[:, 1536 + 384 * i:1920 + 384 * i] for i in range(2)]
        SH = [(QK[64 * (i % 2):64 * (i % 2) + 64, i // 2, :], QK[64 * (i % 2):64 * (i % 2) + 64, 8 + i // 2, :]) for i in range(16)]
        NQ = ob[:, 0:1024].rearrange("p (t n) -> p t n", t=2)
        NK = ob[:, 1024:2048].rearrange("p (t n) -> p t n", t=2)
        LAT = ob[:, 2048:2880].rearrange("p (t n) -> p t n", t=2)
        MQ = ob[:, 0:1536].rearrange("p (t n) -> p t n", t=2)
        MK = ob[:, 2880:4416].rearrange("p (t n) -> p t n", t=2)
        KR = ob[:, 4416:4480].rearrange("p (t n) -> p t n", t=2)
        TMP = pb_[:, 0:1536]
        MG = ob[:, 2048:4096].rearrange("p (t n) -> p t n", t=2)
        MG2 = ob[:, 4096:6144].rearrange("p (t n) -> p t n", t=2)
        ym = bias_[:, 0:2048].rearrange("p (t n) -> p t n", t=2)
        ge = [V_[:, 256 * t:256 * t + 256] for t in range(2)]
        ma = [V_[:, 512 + 256 * t:768 + 256 * t] for t in range(2)]
        wr = pT_[:, 1024:1536].rearrange("p (c n) -> p c n", n=64)
        ebias = pT_[:, 1536:1600]
        rt = [pb_[:, 128 * i:128 * i + 128] for i in range(8)]
        active, rankc = small(896, 1)[0:64, :], small(897, 1)[0:64, :]
        order, gT = pb_[0:64, 1024:1088], pb_[0:64, 1280:1536]
        zeros_ = pT_[:, 0:512]
        ones_, ones_row = ones[:, :], ones[0:1, :]
        lamb, subg = lam_[:, 0:256], lam_[:, 256:384]

        def cols(ap, a, n):
            return [(0, 8 * n, ap[:, a:a + n].rearrange("(c p) n -> p c n", p=P), n)]
        aw, bw, cw, dw, ew = A["a_w_in"][0], A["b_w_in"][0], A["c_w_in"][0], A["d_w_in"][0], A["w_in_2"][0]
        MOD = [cols(A["w_ada_2"][0], 512 * j, 512) for j in range(12)]
        LA = [cols(aw, c, 512) for c in (0, 512, 1024, 1536, 2048, 2608, 3120)] + [cols(aw, 2560, 48)]
        LA_CMP = [[(0, SLOT, A[n][0].rearrange("(c p) n -> p c n", p=P), 256)] for n in ("a_cmp_w1_k", "a_cmp_w1_v")]
        LB = [cols(bw, 512 * j, 512) for j in range(8)]
        LC = [cols(cw, 512 * j, 512) for j in range(7)]
        LD = [cols(dw, 512 * j, 512) for j in range(8)]
        LE = [cols(ew, 512 * j, 512) for j in range(3)] + [cols(ew, 1536, 416)] + [cols(ew, 1952 + 512 * j, 512) for j in range(4)]
        LE_UP = [[(0, 1536, A["w_uq_2"][0].rearrange("(c p) n -> p c n", p=P), 768),
                  (1536, 1024, A["w_ukv_2"][0].rearrange("(c p) n -> p c n", p=P), 1024)]]
        LE_PROJ = [[(0, SLOT, A[n][0].rearrange("(c p) n -> p c n", p=P), 1024)] for n in ("w_proj_na_2", "w_proj_mla_2")]

        def outw(ap):
            return [cols(ap, 512 * j, 512) for j in range(2)]

        def one(loads, fills=1):
            return [(w, fills, 0) for w in loads]

        def closing(w_out, mods):
            a, b = outw(w_out)
            return one(MOD[mods:mods + 2]) + [(a, 0, 2), (b, 2, 0)] + one(MOD[mods + 2:mods + 3])

        STREAM = one(LA) + [(LA_CMP[0], 0, 1), (LA_CMP[1], 1, 0), (None, 2 + len(UA), 0)] + closing(A["a_w_out"][0], 0)
        STREAM += one(LB) + [(None, len(UB), 0)] + closing(A["b_w_out"][0], 3)
        STREAM += one(LC) + [(None, len(UC), 0)] + closing(A["c_w_out"][0], 6)
        STREAM += one(LD)
        acc_B = len(LA) + 3 + len(UA) + 5
        acc_C = acc_B + len(LB) + len(UB) + 5
        acc_before_D = sum(f for _, f, _ in STREAM)
        STREAM += [(None, 16, 0)] + closing(A["d_w_out"][0], 9) + [(None, 1, 0)]
        STREAM += one(LE) + one(LE_UP, 4) + [(None, 8, 0)] + one(LE_PROJ, 2)
        a_, b_ = outw(A["w_out_2"][0])
        STREAM += [(a_, 0, 2), (b_, 2, 0)]
        acc_router = sum(f for _, f, _ in STREAM)
        assert sum(w is not None for w, _, _ in STREAM) % RING == 0

        block = ctx.enter_context(nc.Block())

        @block.sync
        def _(sp):
            sp.dma_start(h[:, :, :], A["x"][0].rearrange("(t p) n -> p t n", p=P)).then_inc(s_h, 16)
            n, fills, done_at = 0, 0, []
            for loads, f, ahead in STREAM:
                fills += f
                if loads is None:
                    continue
                if n >= RING:
                    sp.wait_ge(acc_done, done_at[n - RING])
                for off, size, src, width in loads:
                    dst = ring[n % RING][:, off:off + size].rearrange("p (c n) -> p c n", n=width)
                    sp.dma_start(dst, src).then_inc(w_in[n % RING], 16)
                done_at.append(fills + ahead)
                n += 1
            def gate_up(j, g, up):
                sp.dma_start(guv[j][:, :, 0:FF], g.rearrange("(c p) n -> p c n", p=P)).then_inc(gu_in[j], 16)
                sp.dma_start(guv[j][:, :, FF:2 * FF], up.rearrange("(c p) n -> p c n", p=P)).then_inc(gu_in[j], 16)

            def down(j, dn):
                sp.dma_start(dnv[j], dn.rearrange("(c p) n -> p c n", p=P)).then_inc(dn_in[j], 16)

            def chosen(name, e):
                return A[name][0][bass.ds(e, 1)].rearrange("e k n -> (e k) n")

            def expert_id(k):
                return sp.value_load(todo[0:1, bass.ds(k, 1)], min_val=0, max_val=EXPERTS - 1)

            sp.wait_ge(acc_done, done_at[n - RING])
            gate_up(0, A["w_sh_gate_2"][0], A["w_sh_up_2"][0])
            sp.wait_ge(acc_done, fills)
            down(0, A["w_sh_down_2"][0])
            sp.wait_ge(s_moe, 1)
            pairs = sp.value_load(todo[0:1, 64:65], min_val=TOPK // 2, max_val=EXPERTS // 2)

            def step(g, j, first=False):
                e2, e1 = expert_id(g + 1), expert_id(g)
                sp.wait_ge(s_gu, 2 * g + 2)
                gate_up(j, chosen("w_exp_gate_2", e2), chosen("w_exp_up_2", e2))
                if not first:
                    sp.wait_ge(s_dn, 2 * g)
                down(1 - j, chosen("w_exp_down_2", e1))

            e = expert_id(0)
            gate_up(1, chosen("w_exp_gate_2", e), chosen("w_exp_up_2", e))
            step(0, 0, first=True)
            step(1, 1)
            with sp.Fori(1, pairs) as it:
                for j in range(MOE_SLOTS):
                    step(it * 2 + j, j)
            sp.wait_ge(s_fin, 1)
            sp.dma_start(out[0].rearrange("(t p) n -> p t n", p=P), u[:, :, :]).then_inc(s_out, 16)
            sp.wait_ge(s_out, 16)


        @block.tensor
        def _(pe):
            c, me = Count(), Own(pe, pech)
            prev = {}

            def take(kind, i, releaser):
                if (kind, i) in prev:
                    pe.wait_ge(*prev[kind, i])
                prev[kind, i] = (free[releaser, i], c.up((releaser, i)))

            def acc(releaser):
                i = c.acc % 2
                take("acc", i, releaser)
                c.acc += 1
                return banks[2 * i], banks[2 * i + 1]

            def tr(releaser):
                i = c.tr % 2
                take("tr", i, releaser)
                c.tr += 1
                return banks[4 + i]

            def obank():
                i = c.o % 2
                take("o", i, "o")
                c.o += 1
                return banks[6 + i]

            def slot():
                i = c.w % RING
                c.w += 1
                c.win[i] += 16
                pe.wait_ge(w_in[i], c.win[i])
                return ring[i]

            def transposes(src, chunks, releaser="td"):
                for k in range(0, len(chunks), 2):
                    b = tr(releaser)
                    for j, (a, w) in enumerate(chunks[k:k + 2]):
                        for t in range(T):
                            last = nc.tensor.transpose(b[0:w, 256 * j + 128 * t:256 * j + 128 * t + 128],
                                                       src[:, t, a:a + w], ident[:, :])
                    last.then_inc(tr_done, 1)

            CH = [(128 * k, 128) for k in range(DC)]

            def tile_transposes(src, releaser="td"):
                for t in range(T):
                    pe.wait_ge(s_u, c.up("u"))
                    for k in range(0, DC, 4):
                        b = tr(releaser)
                        for j in range(4):
                            last = nc.tensor.transpose(b[:, 128 * j:128 * j + 128],
                                                       src[:, t, 128 * (k + j):128 * (k + j) + 128], ident[:, :])
                        last.then_inc(tr_done, 1)
                    yield t

            def mm_T(bank, w, col, n=256):
                for f in range(n // 128):
                    for d in range(DC):
                        last = nc.tensor.matmul(bank[:, 256 * f:256 * f + 256], w[:, d, col + 128 * f:col + 128 * f + 128],
                                                uT[:, d, :], start=(d == 0), stop=(d == DC - 1))
                return last

            def mm_R(out_, w, t, col, n, lhs=None, kc=DC):
                for d in range(kc):
                    last = nc.tensor.matmul(out_, uT[:, (lhs or 0) + d, 128 * t:128 * t + 128], w[:, d, col:col + n],
                                            start=(d == 0), stop=(d == kc - 1))
                return last

            def proj(kind, n=512):
                s = slot()
                w = s[:, 0:8 * n].rearrange("p (c n) -> p c n", n=n)
                a, b = acc("d")
                if kind == "TT":
                    mm_T(a, w, 0)
                    last = mm_T(b, w, 256)
                elif kind == "TR":
                    mm_T(a, w, 0)
                    mm_R(b[:, 0:256], w, 0, 256, 256)
                    last = mm_R(b[:, 256:512], w, 1, 256, 256)
                else:
                    mm_R(a[:, 0:n], w, 0, 0, n)
                    last = mm_R(b[:, 0:n], w, 1, 0, n)
                last.then_inc(acc_done, 1)

            def norm_in():
                for t in tile_transposes(u):
                    pass
                pe.wait_ge(s_uT, c.up("uT", 2))

            def modulation():
                w = slot()[:, :].rearrange("p (c n) -> p c n", n=512)
                a, _b = acc("d")
                for d in range(DC):
                    last = nc.tensor.matmul(a[:, :], last_bc(siluc[:, d:d + 1], P)[:, 0, :], w[:, d, :],
                                            start=(d == 0), stop=(d == DC - 1))
                last.then_inc(acc_done, 1)

            def attention(units, blocks, dv):
                nk0 = 128 if blocks is CAUSAL else 256
                pe.wait_ge(s_qkv, c.up("qkv"))

                def scores(un):
                    a, b = acc("d")
                    for x, bk in ((un[0], a), (un[1], b)):
                        nc.tensor.matmul(bk[:, 0:256], x["q"][:, 128:256], x["k"][:, 0:256], start=True, stop=True)
                        last = nc.tensor.matmul(bk[:, 256:256 + nk0], x["q"][:, 0:128], x["k"][:, 0:nk0],
                                                start=True, stop=True)
                    last.then_inc(acc_done, 1)

                def values(n, un):
                    pe.wait_ge(s_p, c.up("p"))
                    ready = []
                    for i in range(2):
                        rel = "ta" if i == 0 else "td"
                        at = c.tr % 2
                        b = tr(rel)
                        for k, (qt, kb) in enumerate(blocks):
                            last = nc.tensor.transpose(b[:, 128 * k:128 * k + 128],
                                                       probs[:, n % 2, qt, i, 128 * kb:128 * kb + 128], ident[:, :])
                        last.then_inc(tr_done, 1)
                        ready.append(prev["tr", at])
                    for i, x in enumerate(un):
                        ob_ = obank()
                        pe.wait_ge(*ready[i])
                        for qt in (1, 0):
                            ks = [(k, kb) for k, (q_, kb) in enumerate(blocks) if q_ == qt]
                            for j, (k, kb) in enumerate(ks):
                                last = nc.tensor.matmul(ob_[:, dv * qt:dv * qt + dv],
                                                        probsT[:, 2 * (n % 2) + i, 128 * k:128 * k + 128],
                                                        V[:, kb, x["v"][0]:x["v"][0] + dv],
                                                        start=(j == 0), stop=(j == len(ks) - 1))
                        last.then_inc(o_done, 1)

                scores(units[0])
                for n in range(len(units)):
                    if n + 1 < len(units):
                        scores(units[n + 1])
                    values(n, units[n])

            def project_out(src, mods=True):
                if mods:
                    modulation()
                    modulation()
                w = [slot()[:, :].rearrange("p (c n) -> p c n", n=512) for _ in range(2)]
                for t in tile_transposes(src):
                    pe.wait_ge(s_uT, c.up("uT"))
                    a, b = acc("d")
                    mm_R(a[:, :], w[0], t, 0, 512)
                    mm_R(b[:, :], w[1], t, 0, 512).then_inc(acc_done, 1)
                if mods:
                    modulation()

            pe.wait_ge(s_id, 2)
            pe.wait_ge(s_u, c.up("u"))
            norm_in()
            for kind, n in (("TT", 512), ("TT", 512), ("TT", 512), ("TR", 512), ("TR", 512), ("RR", 512), ("RR", 512), ("RR", 48)):
                proj(kind, n)
            wk, wv = slot(), slot()
            a, b = acc("d")
            pe.wait_ge(s_xp, 1)
            for v, (w, bk) in enumerate(((wk, a), (wv, b))):
                w = w[:, :].rearrange("p (c n) -> p c n", n=256)
                for f in range(2):
                    for l in range(16):
                        last = nc.tensor.matmul(bk[:, 64 * f:64 * f + 60], w[:, l, 128 * f:128 * f + 128], Xp[:, v, l, :],
                                                start=(l == 0), stop=(l == 15))
            last.then_inc(acc_done, 1)
            pe.wait_ge(s_hid, 1)
            pe.wait_ge(s_small, 32)
            a, b = acc("d")
            for f in range(2):
                nc.tensor.matmul(a[0:64, 0:60], w2[:, 0, f, :], hid[:, f, :], start=(f == 0), stop=(f == 1))
            for g in range(4):
                for f in range(2):
                    last = nc.tensor.matmul(b[0:15, 64 * g:64 * g + 64], hid[:, 2 + f, 15 * g:15 * g + 15], w2[:, 1, f, :],
                                            start=(f == 0), stop=(f == 1))
            last.then_inc(acc_done, 1)
            pe.wait_ge(s_hid, 2)
            a, b = acc("d")
            for qt in range(2):
                for i in range(16):
                    r, bk = 64 * (i % 2), (a, b)[i % 2]
                    at = 128 * qt + 16 * (i // 2)
                    last = nc.tensor.matmul(bk[:, at:at + 15], QK[r:r + 64, i // 2, 128 * qt:128 * qt + 128],
                                            kcT[r:r + 64, 15 * (i // 4):15 * (i // 4) + 15], start=True, stop=True)
            last.then_inc(acc_done, 1)
            pe.wait_ge(s_hid, 3)
            for g2 in range(2):
                bk = tr("td")
                for k in range(4):
                    g, qt = 2 * g2 + k // 2, k % 2
                    last = nc.tensor.transpose(bk[:, 128 * k:128 * k + 128],
                                               pb_[:, 1024 + 512 * qt + 128 * g:1024 + 512 * qt + 128 * g + 128], ident[:, :])
                last.then_inc(tr_done, 1)
            for g in range(4):
                bk = obank()
                pe.wait_ge(free["td", (c.tr - 2 + g // 2) % 2], c.n["td", (c.tr - 2 + g // 2) % 2])
                for qt in range(2):
                    last = nc.tensor.matmul(bk[:, 256 * qt:256 * qt + 256], pcT[:, 2 * g + qt, :], vd[:, g, :],
                                            start=True, stop=True)
                last.then_inc(o_done, 1)
            attention(UA, CAUSAL, 64)
            project_out(u)
            norm_in()
            for kind in ("TT",) * 4 + ("RR",) * 4:
                proj(kind)
            attention(UB, CAUSAL, 128)
            project_out(u)
            norm_in()
            for kind in ("TT",) * 3 + ("RR",) * 4:
                proj(kind)
            attention(UC, CAUSAL, 256)
            project_out(u)
            norm_in()
            for kind in ("TT",) * 4 + ("RR",) * 4:
                proj(kind)
            pe.wait_ge(s_qkv, c.up("qkv"))
            bk = {}

            def stick_scores(i):
                bk[i], _b = acc("a")
                q, k = SH[i]
                nc.tensor.matmul(bk[i][:, 0:128], k[:, 128:256], q[:, 128:256], start=True, stop=False, skip_group_check=True)
                nc.tensor.matmul(bk[i][:, 128:384], k[:, 0:128], q[:, 0:256], start=False, stop=False, skip_group_check=True)\
                    .then_inc(acc_done, 1)

            def stick_values(i):
                b = obank()
                pe.wait_ge(s_am, i + 1)
                nc.tensor.matmul(b[:, 64:128], am[i % 2][:, 0:128], V[:, 1, 64 * i:64 * i + 64], start=True, stop=False)
                nc.tensor.matmul(b[:, 64:128], am[i % 2][:, 256:384], V[:, 0, 64 * i:64 * i + 64], start=False, stop=True)
                nc.tensor.matmul(b[:, 0:64], am[i % 2][:, 128:256], V[:, 0, 64 * i:64 * i + 64], start=True, stop=True)\
                    .then_inc(o_done, 1)

            stick_scores(0)
            stick_scores(1)
            for i in range(16):
                pe.wait_ge(s_lom, i + 1)
                l_ = lom[i % 2]
                nc.tensor.matmul(bk[i][:, 0:128], tri, l_[:, 0:128], start=False, stop=False, skip_group_check=True)
                nc.tensor.matmul(bk[i][:, 128:384], tri, l_[:, 128:384], start=False, stop=False, skip_group_check=True)
                nc.tensor.matmul(bk[i][:, 256:384], ones_, l_[:, 0:128], start=False, stop=True, skip_group_check=True)\
                    .then_inc(s_cum, 1)
                if i >= 1:
                    stick_values(i - 1)
                if i + 2 < 16:
                    stick_scores(i + 2)
            stick_values(15)
            project_out(u)

            a, _b = acc("d")
            for i in range(2):
                if c.n["d", i] > (i == (c.acc - 1) % 2):
                    pe.wait_ge(free["d", i], c.n["d", i] - (i == (c.acc - 1) % 2))
            for k, base in enumerate((0, D, 3 * D, 4 * D)):
                for d in range(DC):
                    last = nc.tensor.matmul(a[:, 8 * k + d:8 * k + d + 1], mod[0:1, base + 128 * d:base + 128 * d + 128],
                                            ones_row[0:1, 0:1], start=True, stop=True)
            last.then_inc(acc_done, 1)
            norm_in()
            for n in (512, 512, 512, 416, 512, 512, 512, 512):
                proj("RR", n)
            pe.wait_ge(s_u, c.up("u"))
            transposes(NQ, CH[0:4])
            transposes(NK, CH[0:4])
            transposes(LAT, CH[0:3])
            pe.wait_ge(s_uT, c.up("uT"))
            s = slot()
            i = (c.w - 1) % RING
            c.win[i] += 16
            pe.wait_ge(w_in[i], c.win[i])
            wq = s[:, 0:1536].rearrange("p (c n) -> p c n", n=768)
            wkv = s[:, 1536:2560].rearrange("p (c n) -> p c n", n=1024)
            for t in range(T):
                a, b = acc("d")
                mm_R(a[:, 0:384], wq, t, 0, 384, kc=2)
                mm_R(b[:, 0:384], wq, t, 384, 384, kc=2).then_inc(acc_done, 1)
            for t in range(T):
                a, b = acc("d")
                mm_R(a[:, :], wkv, t, 0, 512, lhs=2, kc=1)
                mm_R(b[:, :], wkv, t, 512, 512, lhs=2, kc=1).then_inc(acc_done, 1)
            pe.wait_ge(s_u, c.up("u"))
            transposes(MQ, [(96 * k, 96) for k in range(8)])
            transposes(MK, [(96 * k, 96) for k in range(8)])
            attention(UN, FULL, 64)
            attention(UM, FULL, 64)
            for t in tile_transposes(ym):
                pass
            pe.wait_ge(s_uT, c.up("uT", 2))
            for k in range(2):
                w = slot()[:, :].rearrange("p (c n) -> p c n", n=1024)
                for t in range(T):
                    a, b = acc("d")
                    mm_R(a[:, :], w, t, 0, 512, lhs=4 * k, kc=4)
                    mm_R(b[:, :], w, t, 512, 512, lhs=4 * k, kc=4).then_inc(acc_done, 1)
            project_out(MG, mods=False)
            norm_in()
            a, b = acc("a")
            pe.wait_ge(s_rt, 32)
            mm_R(a[:, 0:64], wr, 0, 0, 64)
            mm_R(b[:, 0:64], wr, 1, 0, 64).then_inc(acc_done, 1)
            for k in ("tr", "o"):
                for i in range(2):
                    pe.wait_ge(*prev[k, i])
            pe.wait_ge(*prev["acc", 0])

            def gate_up(t, j):
                n = 0
                for d in range(DC):
                    for x, y in PARTS:
                        last = nc.tensor.matmul(banks[t][:, :], uT2[x][:, d, 128 * t:128 * t + 128], gu_[j][y][:, d, :],
                                                start=(n == 0), stop=(n == 3 * DC - 1))
                        n += 1
                last.then_inc(s_gu, 1)

            def act_T(e, t):
                pe.wait_ge(s_ga, 2 * e + t + 1)
                for f in range(2):
                    last = nc.tensor.transpose(banks[2 + t][:, 128 * f:128 * f + 128], ma[t][:, 128 * f:128 * f + 128], ident[:, :])
                last.then_inc(s_gat, 1)

            def down(e, t, j, stop=False, done=None):
                pe.wait_ge(s_al, 2 * e + t + 1)
                for f in range(2):
                    for k, (x, y) in enumerate(PARTS):
                        for n in range(2):
                            last = nc.tensor.matmul(banks[4 + 2 * t + n][:, :], ma2[t][x][:, 128 * f:128 * f + 128],
                                                    dn_[j][y][:, f, 512 * n:512 * n + 512], start=False,
                                                    stop=(stop and f == 1 and k == 2), skip_group_check=True)
                last.then_inc(done or s_dn, 1)

            pe.wait_ge(s_gl, 2)
            pe.wait_ge(s_ul, 1)
            gate_up(0, 0)
            gate_up(1, 0)
            pe.wait_ge(*prev["acc", 1])
            pe.wait_ge(s_r1, 1)
            for t in range(T):
                nc.tensor.matmul(banks[2][0:64, 0:1], rt[1][:, 64 * t:64 * t + 64], ones_[:, 0:1], start=(t == 0), stop=(t == 1))
            for t in range(T):
                last = nc.tensor.transpose(banks[3][0:64, 128 * t:128 * t + 128], gate[:, t, 0:64], ident[:, :])
            last.then_inc(s_aux, 1)
            pe.wait_ge(s_r2, 1)
            nc.tensor.matmul(banks[2][0:64, 1:2], cc("strict")[0:64, 0:64], active, start=True, stop=True)
            nc.tensor.matmul(banks[2][0:1, 2:3], active, ones_[0:64, 0:1], start=True, stop=True).then_inc(s_aux, 1)
            pe.wait_ge(s_r2, 2)
            nc.tensor.matmul(banks[2][0:1, 8:72], cc("row")[0:64, :], order, start=True, stop=True)
            for t in range(T):
                last = nc.tensor.matmul(banks[3][:, 64 * t:64 * t + 64], gT[:, 128 * t:128 * t + 128], order, start=True, stop=True)
            last.then_inc(s_aux, 1)
            pe.wait_ge(s_moe, 1)
            pairs = pe.value_load(todo[0:1, 64:65], min_val=TOPK // 2, max_val=EXPERTS // 2)
            for k in range(4):
                nc.tensor.matmul(banks[4 + k][:, :], zeros_[:, 0:128], zeros_[:, :], start=True, stop=False, skip_group_check=True)
            with pe.Fori(0, pairs) as it:
                for j in range(MOE_SLOTS):
                    g, nj = it * 2 + j, (j + 1) % 2
                    act_T(g, 0)
                    pe.wait_ge(s_gl, 2 * g + 4)
                    gate_up(0, nj)
                    pe.wait_ge(s_dl, g + 1)
                    down(g, 0, j)
                    act_T(g, 1)
                    gate_up(1, nj)
                    down(g, 1, j)
            g = pairs * 2
            act_T(g, 0)
            pe.wait_ge(s_dl, g + 1)
            down(g, 0, 0, stop=True)
            act_T(g, 1)
            down(g, 1, 0, stop=True, done=s_all)

        @block.scalar
        def _(act):
            c, me = Count(), Own(act, ach)
            act.dma_start(cst[:, :], A["shape_consts"]).then_inc(s_const, 16)
            act.dma_start(par[:, :], A["params"]).then_inc(s_const, 16)
            act.dma_start(posn[:, :], A["pos_cols"]).then_inc(s_const, 16)
            for v, n in enumerate(("a_cmp_w2_k", "a_cmp_w2_v")):
                act.dma_start(w2[:, v, :, :], A[n][0].rearrange("(c p) n -> p c n", p=P)).then_inc(s_small, 16)

            act.dma_start(lamb, row_bc(A["b_lambda"][0].rearrange("a b -> (a b)"), 256)).then_inc(s_lam, 16)
            act.dma_start(subg, row_bc(A["b_sub_gain"][0], 128)).then_inc(s_lam, 16)

            def gp(i):
                act.dma_start(gpost[:, :], row_bc(A["norm_post"][i], D)).then_inc(s_gpost, 16)

            def funcs(kind, *args):
                act.wait_ge(s_sq, c.up("sq"))
                kind(*args)

            def do_rstd(n, width, at=0):
                me.link(nc.scalar.activation(lnv[:, at:at + n], ssq[:, at:at + n], ACT.Ln, bias=epsc, scale=1.0 / width))
                nc.scalar.activation(rstd[:, at:at + n], lnv[:, at:at + n], ACT.Exp, scale=-0.5).then_inc(s_rstd, 1)

            def do_exp(dst, src, scale):
                nc.scalar.activation(dst, src, ACT.Exp, scale=scale).then_inc(s_rstd, 1)

            def do_sigmoid(dst, src, scale=1.0):
                nc.scalar.activation(dst, src, ACT.Sigmoid, scale=scale).then_inc(s_rstd, 1)

            def squares(src=h):
                for t in range(T):
                    act.wait_ge(s_sq, c.up("sq"))
                    tile_rstd(t, src[:, t, :])

            def tile_rstd(t, x):
                me.link(nc.scalar.activation(pT_[:, 0:D], x, ACT.Square, accum_out=ssq[:, t:t + 1]))
                me.link(nc.scalar.activation(lnv[:, t:t + 1], ssq[:, t:t + 1], ACT.Ln, bias=epsc, scale=1.0 / D))
                nc.scalar.activation(rstd[:, t:t + 1], lnv[:, t:t + 1], ACT.Exp, scale=-0.5).then_inc(s_rstd, 1)

            def closing_norm():
                c.acc += 2
                for t in range(T):
                    act.wait_ge(acc_done, c.acc + 1)
                    pair = c.acc % 2
                    tile_rstd(t, psum[:, 1024 * pair:1024 * pair + 1024])
                    c.acc += 1
                c.acc += 1

            def attention(units, blocks, dv):
                nb = 128 * len(blocks)

                def exps(n, un):
                    act.wait_ge(s_mx, c.up("mx"))
                    job = un[0]["job"]
                    for qt in (1, 0):
                        nk = 256 if (qt or blocks is FULL) else 128
                        for i in range(2):
                            x = probs[:, n % 2, qt, i, 0:nk]
                            last = nc.scalar.activation(x, x, ACT.Exp, bias=nm[:, qt, job + i:job + i + 1],
                                                        accum_out=rs[:, qt, job + i:job + i + 1])
                    last.then_inc(s_p, 1)

                def evac(n):
                    act.wait_ge(tr_done, c.tr + 1)
                    if c.o - 2 > 0:
                        act.wait_ge(o_done, c.o - 2)
                    nc.scalar.activation(probsT[:, 2 * (n % 2), 0:nb], banks[4 + c.tr % 2][:, 0:nb], ACT.Copy)\
                        .then_inc(free["ta", c.tr % 2], 1)
                    c.tr += 2
                    c.o += 2
                exps(0, units[0])
                for n in range(len(units)):
                    evac(n)
                    if n + 1 < len(units):
                        exps(n + 1, units[n + 1])

            gp(0)
            funcs(do_sigmoid, siluc[:, 0:8], siluc[:, 8:16])
            act.wait_ge(s_sq, c.up("sq"))
            me.link(nc.scalar.activation(sinr, sinr, ACT.Sin))
            nc.scalar.activation(cosr, cosr, ACT.Sin).then_inc(s_rstd, 1)
            squares()
            act.dma_start(mod[:, :], row_bc(A["b_ada_2"][0], 6 * D)).then_inc(s_row, 16)
            c.tr += 4
            funcs(do_sigmoid, u[:, :, :], z[:, :, :])
            funcs(do_sigmoid, gate[:, :, 0:48], gate[:, :, 0:48])
            funcs(do_sigmoid, gelu_t, gelu_t, 1.5957691216057308)
            for qt in range(2):
                funcs(do_exp, pc_[:, qt, :, 0:15], pc_[:, qt, :, 0:15], 1.0)
            c.tr += 2
            c.o += 4
            attention(UA, CAUSAL, 64)
            c.acc = len(LA) + 3 + len(UA)
            closing_norm()
            c.tr += 4
            squares()
            gp(1)
            c.tr += 4
            funcs(do_sigmoid, u[:, :, :], z[:, :, :])
            funcs(do_exp, lamc[:, 0:2], lamc[:, 0:2], 1.0)
            attention(UB, CAUSAL, 128)
            for t in range(T):
                funcs(do_rstd, 8, 128, 8 * t)
            c.acc = acc_B + len(LB) + len(UB)
            closing_norm()
            c.tr += 4
            squares()
            gp(2)
            c.tr += 4
            funcs(do_sigmoid, u[:, :, :], z[:, :, :])
            attention(UC, CAUSAL, 256)
            funcs(do_exp, cf[:, :, 0:12], cf[:, :, 0:12], 1.0)
            c.acc = acc_C + len(LC) + len(UC)
            closing_norm()
            c.tr += 4
            squares()
            gp(3)
            c.tr += 4
            c.acc = acc_before_D
            funcs(do_sigmoid, u[:, :, :], z[:, :, :])

            def softplus_parts(i):
                act.wait_ge(acc_done, acc_before_D + i + 1)
                bk = banks[2 * ((acc_before_D + i) % 2)]
                me.link(nc.scalar.activation(sp_[i % 2], bk[:, 0:384], ACT.Abs))
                me.link(nc.scalar.activation(sp_[i % 2], sp_[i % 2], ACT.Exp, scale=-1.0))
                nc.scalar.activation(sp_[i % 2], sp_[i % 2], ACT.Ln, bias=onec).then_inc(s_abs, 1)

            softplus_parts(0)
            softplus_parts(1)
            for i in range(16):
                act.wait_ge(s_cum, i + 1)
                if i >= 2:
                    act.wait_ge(o_done, c.o + i - 1)
                pair = (acc_before_D + i) % 2
                nc.scalar.activation(am[i % 2], banks[2 * pair][:, 0:384], ACT.Exp).then_inc(free["a", pair], 1)
                if i + 2 < 16:
                    softplus_parts(i + 2)
            c.o += 16
            c.acc = acc_before_D + 16
            closing_norm()
            c.tr += 4
            squares()
            c.tr += 4
            act.wait_ge(s_attn, 4)
            rp = A["na_rpb_2"]
            for i in range(8):
                for r in range(4):
                    src = bass.AP(rp.tensor, rp.offset + 465 * i + 31 * (7 - r) - 48, [[1, 64], [31, 4], [1, 64]])
                    act.dma_start(bias[64 * (r % 2):64 * (r % 2) + 64, 8 * (r // 2) + i, :].rearrange("p (a b) -> p a b", a=4),
                                  src).then_inc(s_rpb, 16)
            funcs(do_sigmoid, z[:, :, :], z[:, :, :])
            funcs(do_sigmoid, u[:, :, :], u[:, :, :])
            funcs(do_rstd, 16, 64)
            funcs(do_rstd, 16, 64)
            act.wait_ge(s_sq, c.up("sq"))
            for width, a in ((256, 0), (128, 2)):
                me.link(nc.scalar.activation(lnv[:, a:a + 2], ssq[:, a:a + 2], ACT.Ln, bias=epsc, scale=1.0 / width))
            nc.scalar.activation(rstd[:, 0:4], lnv[:, 0:4], ACT.Exp, scale=-0.5).then_inc(s_rstd, 1)
            c.tr += 6
            funcs(do_rstd, 16, 96)
            funcs(do_rstd, 16, 96)
            c.tr += 8
            attention(UN, FULL, 64)
            attention(UM, FULL, 64)
            act.wait_ge(s_attn, 5)
            act.dma_start(wr, A["w_router_2"][0].rearrange("(c p) n -> p c n", p=P)).then_inc(s_rt, 16)
            act.dma_start(ebias, row_bc(A["e_bias_2"][0], 64)).then_inc(s_rt, 16)
            c.tr += 8

            def gu_high(j, half, loads):
                act.wait_ge(gu_in[j], loads)
                nc.scalar.activation(gu_[j][0][:, 4 * half:4 * half + 4, :], guv[j][:, 4 * half:4 * half + 4, :], ACT.Copy)\
                    .then_inc(s_gh, 1)

            def dn_high(j, loads):
                act.wait_ge(dn_in[j], loads)
                nc.scalar.activation(dn_[j][0], dnv[j], ACT.Copy).then_inc(s_dh, 1)

            gu_high(0, 0, 32)
            gu_high(0, 1, 32)
            squares()
            act.wait_ge(s_sq, c.up("sq"))
            nc.scalar.activation(uT2[0], uT[:, :, :], ACT.Copy).then_inc(s_uh, 1)
            c.acc = acc_router
            act.wait_ge(acc_done, acc_router + 1)
            pair = acc_router % 2
            for t in range(T):
                last = nc.scalar.activation(gate[:, t, 0:64], banks[2 * pair + t][:, 0:64], ACT.Sigmoid)
            last.then_inc(free["a", pair], 1)

            def moe_exp(e, t):
                act.wait_ge(s_gu, 2 * e + t + 1)
                nc.scalar.activation(ge[t], banks[t][:, 0:FF], ACT.Sigmoid).then_inc(s_ge, 1)

            def moe_evac(e, t):
                act.wait_ge(s_gat, 2 * e + t + 1)
                nc.scalar.activation(ma2[t][0], banks[2 + t][:, 0:FF], ACT.Copy).then_inc(s_ah, 1)

            dn_high(0, 16)
            moe_exp(0, 0)
            moe_exp(0, 1)
            act.wait_ge(s_moe, 1)
            pairs = act.value_load(todo[0:1, 64:65], min_val=TOPK // 2, max_val=EXPERTS // 2)
            gu_high(1, 0, 32)
            gu_high(1, 1, 32)
            with act.Fori(0, pairs) as it:
                for j in range(MOE_SLOTS):
                    g = it * 2 + j
                    moe_evac(g, 0)
                    moe_exp(g + 1, 0)
                    gu_high(j, 0, 32 * it + 64)
                    moe_evac(g, 1)
                    gu_high(j, 1, 32 * it + 64)
                    dn_high(1 - j, 16 * it + (16 if j == 0 else 32))
                    moe_exp(g + 1, 1)
            moe_evac(pairs * 2, 0)
            moe_evac(pairs * 2, 1)

        @block.gpsimd
        def _(pool):
            c, me = Count(), Own(pool, pch)
            me.link(nc.gpsimd.memset(ident[:, :], 0.0))
            nc.gpsimd.affine_select(out=ident[:, :], in_=ident[:, :], compare_op=ALU.not_equal, fill=1.0, base=0,
                                    pattern=[[-1, P]], channel_multiplier=1).then_inc(s_id, 1)
            nc.gpsimd.memset(ones[:, :], 1.0).then_inc(s_id, 1)
            pool.wait_ge(s_const, 48)

            def alibi(sl, pattern):
                for i, x in enumerate(sl):
                    last = nc.gpsimd.tensor_scalar(bias[:, i, :], dist[:, pattern[i], :], -x, None, ALU.mult)
                last.then_inc(s_bias, 1)

            alibi(slopes(16), [0] * 16)
            pool.wait_ge(s_x, 1)
            for v, n in enumerate(("posk", "posv")):
                for l in range(16):
                    last = nc.gpsimd.tensor_scalar(Xp[:, v, l, :].rearrange("p (g n) -> p g n", g=4),
                                                   Xc[:, v, :, 2 * l:2 * l + 225:16], pc(n, l), None, ALU.add)
            last.then_inc(s_xp, 1)
            pool.wait_ge(s_attn, 1)
            alibi([x for x in slopes(8) for _ in range(2)], [0] * 16)
            pool.wait_ge(s_attn, 2)
            alibi(slopes(12), [1 + i // 4 for i in range(12)])
            for i in range(16):
                pair = (acc_before_D + i) % 2
                pool.wait_ge(free["a", pair], c.up(pair))
                x = am[i % 2][:, 0:256].rearrange("p (a b) -> p a b", a=2)
                nc.gpsimd.affine_select(out=x, in_=x, compare_op=ALU.is_ge, fill=0.0, base=-1,
                                        pattern=[[0, 2], [1, P]], channel_multiplier=-1).then_inc(s_am, 1)
            pool.wait_ge(s_rpb, 32 * 16)
            nc.gpsimd.tensor_tensor(bias[:, :, :], bias[:, :, :], mid_bc(cc("win"), 16), ALU.add).then_inc(s_bias, 1)
            for half in range(2):
                pool.wait_ge(s_gh, half + 1)
                x = slice(4 * half, 4 * half + 4)
                nc.gpsimd.tensor_tensor(gu_[0][1][:, x, :], guv[0][:, x, :], gu_[0][0][:, x, :], ALU.subtract).then_inc(s_gl, 1)
            pool.wait_ge(s_uh, 1)
            nc.gpsimd.tensor_tensor(uT2[1], uT[:, :, :], uT2[0], ALU.subtract).then_inc(s_ul, 1)

        @block.vector
        def _(dve):
            c, me = Count(), Own(dve, dch)
            v = nc.vector
            tick, own, link = me.tick, me.own, me.link

            def acc_in():
                i = c.acc % 2
                c.acc += 1
                dve.wait_ge(acc_done, c.acc)
                c.up(("d", i))
                return banks[2 * i], banks[2 * i + 1], free["d", i]

            def own_acc():
                i = (c.acc - 1) % 2
                dve.wait_ge(free["d", i], c.n["d", i])

            def act_does():
                dve.wait_ge(s_rstd, c.up("rstd"))

            def tr_in(dst, n, gains):
                for k in range(0, n, 2):
                    dve.wait_ge(tr_done, c.tr + 1)
                    b = banks[4 + c.tr % 2]
                    for j in range(min(2, n - k)):
                        w, s1, s2, op = gains(k + j)
                        last = v.tensor_scalar(dst[0:w, k + j, :], b[0:w, 256 * j:256 * j + 256], s1, s2, ALU.mult, op) \
                            if s2 is not None else v.tensor_scalar(dst[0:w, k + j, :], b[0:w, 256 * j:256 * j + 256], s1, None, ALU.mult)
                    last.then_inc(free["td", c.tr % 2], 1)
                    c.up(("td", c.tr % 2))
                    c.tr += 1

            def tr_own():
                i = (c.tr - 1) % 2
                dve.wait_ge(free["td", i], c.n["td", i])

            def uT_ready():
                tr_own()
                dve.sem_inc(s_uT, 1)

            def tile_in(dst, t, gains=None):
                for k in range(0, DC, 4):
                    dve.wait_ge(tr_done, c.tr + 1)
                    b = banks[4 + c.tr % 2]
                    if gains is None:
                        last = v.tensor_copy(dst[:, k:k + 4, 128 * t:128 * t + 128], b.rearrange("p (j s) -> p j s", j=4))
                    else:
                        for j in range(4):
                            _w, s1, s2, op = gains(k + j)
                            x, y = dst[:, k + j, 128 * t:128 * t + 128], b[:, 128 * j:128 * j + 128]
                            last = v.tensor_scalar(x, y, s1, s2, ALU.mult, op) if s2 is not None else \
                                v.tensor_scalar(x, y, s1, None, ALU.mult)
                    last.then_inc(free["td", c.tr % 2], 1)
                    c.up(("td", c.tr % 2))
                    c.tr += 1
                uT_ready()

            def plain(k):
                return P, 1.0, None, None

            def norm_in(gains, between=None):
                for t in range(T):
                    act_does()
                    v.tensor_scalar(u[:, t, :], h[:, t, :], rstd[:, t:t + 1], None, ALU.mult).then_inc(s_u, 1)
                if between is not None:
                    between()
                for t in range(T):
                    tile_in(uT, t, gains)

            def evac(dst0, dst1, n=512, scale=None):
                a, b, f = acc_in()
                for dst, x in ((dst0, a), (dst1, b)):
                    last = v.tensor_copy(dst, x[:, 0:n]) if scale is None else \
                        v.tensor_scalar(dst, x[:, 0:n], scale, None, ALU.mult)
                last.then_inc(f, 1)

            def flat(ap):
                return ap.rearrange("p a b -> p (a b)")

            def silu_z():
                own_acc()
                dve.sem_inc(s_sq, 1)

            def silu_end():
                act_does()
                link(v.tensor_tensor(z_[:, :], z_[:, :], u_[:, :], ALU.mult))

            def attention(units, blocks, dv, njobs, qkv=True):
                o = o_view(njobs, dv)
                nb = 128 * len(blocks)
                nk0 = 128 if blocks is CAUSAL else 256
                if qkv:
                    dve.sem_inc(s_qkv, 1)

                def soft(n, un):
                    a, b, f = acc_in()
                    if c.tr > 0:
                        dve.wait_ge(tr_done, c.tr)
                    job, bi = un[0]["job"], un[0]["b"]
                    d1 = probs[:, n % 2, 1, :, :]
                    d0 = probs[:, n % 2, 0, :, 0:nk0]
                    pair = psum[:, 1024 * ((c.acc - 1) % 2):1024 * ((c.acc - 1) % 2) + 1024].rearrange("p (i k) -> p i k", i=2)
                    a_, b_ = pair[:, :, 0:256], pair[:, :, 256:256 + nk0]
                    if bi is None:
                        v.tensor_copy(d1, a_)
                        v.tensor_copy(d0, b_).then_inc(f, 1)
                    else:
                        if blocks is CAUSAL:
                            v.tensor_tensor(d1, a_, bias[:, bi:bi + 2, :], ALU.add)
                            v.tensor_tensor(d0, b_, bias[:, bi:bi + 2, 128:256], ALU.add).then_inc(f, 1)
                        else:
                            for x, y, k in ((d1, a_, 8 + bi), (d0, b_, bi)):
                                for i in range(2):
                                    r3 = bias[:, k + i, :].rearrange("p (r c) -> p r c", c=64)
                                    rev = bass.AP(r3.tensor, r3.offset + 63, [r3.ap[0], [64, 4], [-1, 64]])
                                    last = v.tensor_tensor(x[:, i, :].rearrange("p (r c) -> p r c", c=64),
                                                           y[:, i, :].rearrange("p (r c) -> p r c", c=64), rev, ALU.add)
                            last.then_inc(f, 1)
                    own_acc()
                    v.tensor_reduce(nm[:, 1, job:job + 2], d1, AX.X, ALU.max, negate=True)
                    v.tensor_reduce(nm[:, 0, job:job + 2], d0, AX.X, ALU.max, negate=True).then_inc(s_mx, 1)

                def values(n, un):
                    dve.wait_ge(tr_done, c.tr + 2)
                    if c.o - 2 > 0:
                        dve.wait_ge(o_done, c.o - 2)
                    i = (c.tr + 1) % 2
                    v.tensor_copy(probsT[:, 2 * (n % 2) + 1, 0:nb], banks[4 + i][:, 0:nb]).then_inc(free["td", i], 1)
                    c.up(("td", i))
                    c.tr += 2
                    for i in range(2):
                        dve.wait_ge(o_done, c.o + 1)
                        ob_in(o[:, :, un[i]["job"], :], dv)
                soft(0, units[0])
                for n in range(len(units)):
                    if n + 1 < len(units):
                        soft(n + 1, units[n + 1])
                    values(n, units[n])
                own_o()

            def ob_in(dst, dv):
                i = c.o % 2
                v.tensor_copy(dst, banks[6 + i][:, 0:2 * dv].rearrange("p (t d) -> p t d", t=2)).then_inc(free["o", i], 1)
                c.up(("o", i))
                c.o += 1

            def own_o():
                for i in range(2):
                    dve.wait_ge(free["o", i], c.n["o", i])

            def osum(o, t, j, n):
                return o[:, t, j:j + n, :].rearrange("p j d -> p (j d)")

            def scaled(o, t, n, dv):
                link(v.tensor_tensor(o[:, t, :, :], o[:, t, :, :], last_bc(cf[:, t, 0:n], dv), ALU.mult))

            def mods(n):
                for _ in range(n):
                    a, b, f = acc_in()
                    x = mod[:, 512 * c.n.get("mod", 0):512 * c.n.get("mod", 0) + 512]
                    v.tensor_tensor(x, x, a[:, :], ALU.add).then_inc(f, 1)
                    c.up("mod")

            def project_out(i, combine):
                combine(0)
                dve.sem_inc(s_u, 1)
                mods(1)
                tile_in(uT, 0)
                combine(1)
                dve.sem_inc(s_u, 1)
                dve.sem_inc(s_attn, 1)
                mods(1)
                tile_in(uT, 1)
                dve.wait_ge(s_gpost, 16 * (i + 1))
                for t in range(T):
                    act_does()
                    pair = c.acc % 2
                    a, b, f = acc_in()
                    v.scalar_tensor_tensor(u[:, t, :], psum[:, 1024 * pair:1024 * pair + 1024], rstd[:, t:t + 1],
                                           gpost[:, :], ALU.mult, ALU.mult).then_inc(f, 1)
                    own_acc()
                    v.tensor_tensor(h[:, t, :], h[:, t, :], u[:, t, :], ALU.add).then_inc(s_sq, 1)

            def head_norms(x, nh, width, tiles=range(T)):
                m = nh * width
                for t in tiles:
                    xt = x[:, t, 0:m]
                    link(v.tensor_tensor(TMP[:, 0:m], xt, xt, ALU.mult))
                    link(v.tensor_reduce(ssq[:, nh * t:nh * t + nh], TMP[:, 0:m].rearrange("p (a b) -> p a b", a=nh), AX.X, ALU.add))
                dve.sem_inc(s_sq, 1)
                act_does()
                for t in tiles:
                    xt = x[:, t, 0:m].rearrange("p (a b) -> p a b", a=nh)
                    tick(v.tensor_tensor(xt, xt, last_bc(rstd[:, nh * t:nh * t + nh], width), ALU.mult))
                own()

            for x, val in ((epsc, EPS), (onec, 1.0), (rs[:, :, 0:16], 1.0)):
                tick(v.memset(x, val))
            dve.wait_ge(s_const, 48)
            own()
            cpar = par[:, PC["c"][0]:PC["c"][1]]
            v.tensor_copy(siluc[:, 8:16], cpar).then_inc(s_sq, 1)
            act_does()
            link(v.tensor_tensor(siluc[:, 0:8], siluc[:, 0:8], cpar, ALU.mult))
            dve.sem_inc(s_u, 1)
            posf = lamc[:, 0:2]
            link(v.tensor_copy(posf, posn[:, :]))
            magic = 1.5 * 2.0 ** 23
            two_pi = 2.0 * math.pi
            c1 = float(np.float32(np.round(two_pi * 2 ** 7) / 2 ** 7))
            c2 = float(np.float32(np.round((two_pi - c1) * 2 ** 20) / 2 ** 20))
            c3 = float(np.float32(two_pi - c1 - c2))
            turn = gelu_x[:, 0:32]
            ang = gelu_x[:, 32:64]
            for t in range(T):
                tick(v.tensor_scalar(ang[:, 16 * t:16 * t + 16], cc("freq"), posf[:, t:t + 1], None, ALU.mult))
            own()
            for dst, shift in ((sinr, 0.0), (cosr, 0.25)):
                link(v.tensor_scalar(turn, ang, 1.0 / two_pi, shift, ALU.mult, ALU.add))
                link(v.tensor_scalar(turn, turn, magic, None, ALU.add))
                link(v.tensor_scalar(turn, turn, magic, None, ALU.subtract))
                link(v.scalar_tensor_tensor(dst, turn, -c1, ang, ALU.mult, ALU.add))
                link(v.scalar_tensor_tensor(dst, turn, -c2, dst, ALU.mult, ALU.add))
                link(v.scalar_tensor_tensor(dst, turn, -c3, dst, ALU.mult, ALU.add))
                if shift:
                    link(v.tensor_scalar(dst, dst, math.pi / 2, None, ALU.add))
                link(v.tensor_scalar(dst, dst, 3.1415925, -3.1415925, ALU.min, ALU.max))
            dve.sem_inc(s_sq, 1)
            act_does()
            dve.wait_ge(s_h, 16)
            for _ in range(T):
                dve.sem_inc(s_sq, 1)

            norm_in(lambda k: (P, pc("pre", k), None, None))
            for j in range(2):
                evac(flat(QK[:, 4 * j:4 * j + 2, :]), flat(QK[:, 4 * j + 2:4 * j + 4, :]), scale=0.125)
            a, b, f = acc_in()
            for vi, bk in ((0, a), (1, b)):
                y = bk[:, :].rearrange("p (f s) -> p f s", f=2)
                for r in range(2):
                    v.tensor_copy(Xc[0:64, vi, r:r + 3:2, :], y[64 * r:64 * r + 64, :, :])
                    last = v.tensor_copy(Xc[64:128, vi, r:r + 3:2, 0:255], y[64 * r:64 * r + 64, :, 1:256])
            last.then_inc(f, 1)
            own_acc()
            dve.sem_inc(s_x, 1)
            for br in range(2):
                a, b, f = acc_in()
                y = a[:, :].rearrange("p (f s) -> p f s", f=2)
                for r in range(2):
                    for r2 in range(2):
                        g0 = 8 + 4 * br + r
                        v.tensor_copy(QK[64 * r2:64 * r2 + 64, g0:g0 + 3:2, :], y[64 * r:64 * r + 64, :, :])
                v.tensor_copy(V[:, :, 256 * br:256 * br + 256], b[:, :].rearrange("p (t n) -> p t n", t=2)).then_inc(f, 1)
            for j in range(2):
                evac(z[:, 0, 512 * j:512 * j + 512], z[:, 1, 512 * j:512 * j + 512])
            silu_z()
            evac(gate[:, 0, 0:48], gate[:, 1, 0:48], n=48)
            own_acc()
            dve.sem_inc(s_sq, 1)
            silu_end()
            act_does()
            a, b, f = acc_in()
            for vi, bk in ((0, a), (1, b)):
                last = v.tensor_copy(hid[:, 2 * vi:2 * vi + 2, :], bk[:, 0:128].rearrange("p (f n) -> p f n", f=2)[:, :, 0:60])
            last.then_inc(f, 1)
            own_acc()
            link(v.tensor_tensor(gelu_t, gelu_x, gelu_x, ALU.mult))
            link(v.tensor_scalar(gelu_t, gelu_t, 0.044715, 1.0, ALU.mult, ALU.add))
            v.tensor_tensor(gelu_t, gelu_t, gelu_x, ALU.mult).then_inc(s_sq, 1)
            act_does()
            v.tensor_tensor(gelu_x, gelu_x, gelu_t, ALU.mult).then_inc(s_hid, 1)
            tick(v.memset(ob[:, 4096:5120], 0.0))
            tick(v.memset(pb_[:, 1024:2048], 0.0))
            own()
            a, b, f = acc_in()
            for r in range(2):
                v.tensor_copy(kcT[64 * r:64 * r + 64, 0:60], a[0:64, 0:60])
            for r in range(4):
                last = v.tensor_copy(vd[32 * r:32 * r + 15, :, 64 * r:64 * r + 64], b[0:15, 0:256].rearrange("p (g n) -> p g n", g=4))
            last.then_inc(f, 1)
            own_acc()
            dve.sem_inc(s_hid, 1)
            a, b, f = acc_in()
            cbias = cc("cbias").rearrange("p (t h n) -> p t h n", t=2, n=15)
            cmask = cc("cmask").rearrange("p (t n) -> p t n", t=2)
            for t in range(T):
                for r, bk in ((0, a), (1, b)):
                    last = v.tensor_tensor(pc_[:, t, r:16:2, 0:15],
                                           bk[:, 128 * t:128 * t + 128].rearrange("p (h n) -> p h n", n=16)[:, :, 0:15],
                                           cbias[:, t, r:16:2, :], ALU.add)
            last.then_inc(f, 1)
            own_acc()
            for t in range(T):
                link(v.tensor_reduce(ssq, pc_[:, t, :, 0:15], AX.X, ALU.max))
                v.tensor_tensor(pc_[:, t, :, 0:15], pc_[:, t, :, 0:15], last_bc(ssq, 15), ALU.subtract).then_inc(s_sq, 1)
                act_does()
                link(v.tensor_tensor(pc_[:, t, :, 0:15], pc_[:, t, :, 0:15], mid_bc(cmask[:, t, :], 16), ALU.mult))
                link(v.tensor_reduce(ssq, pc_[:, t, :, 0:15], AX.X, ALU.add))
                link(v.tensor_scalar(ssq, ssq, 1e-30, None, ALU.max))
                link(v.reciprocal(ssq, ssq))
                link(v.tensor_tensor(pc_[:, t, :, 0:15], pc_[:, t, :, 0:15], last_bc(ssq, 15), ALU.mult))
            dve.sem_inc(s_hid, 1)
            for _ in range(2):
                dve.wait_ge(tr_done, c.tr + 1)
                i = c.tr % 2
                v.tensor_copy(flat(pcT[:, 4 * (c.tr % 2 if False else _):4 * _ + 4, :]), banks[4 + i][:, :]).then_inc(free["td", i], 1)
                c.up(("td", i))
                c.tr += 1
            oA = o_view(48, 64)
            for g in range(4):
                dve.wait_ge(o_done, c.o + 1)
                i = c.o % 2
                v.tensor_copy(oA[:, :, 4 * g:4 * g + 4, :], banks[6 + i][:, :].rearrange("p (t j d) -> p t j d", t=2, j=4))\
                    .then_inc(free["o", i], 1)
                c.up(("o", i))
                c.o += 1
            dve.wait_ge(s_bias, 1)
            attention(UA, CAUSAL, 64, 48)
            def combine_A(t):
                link(v.reciprocal(cf[:, t, 0:48], rs[:, t, 0:48]))
                link(v.tensor_tensor(cf[:, t, 0:48], cf[:, t, 0:48], gate[:, t, 0:48], ALU.mult))
                scaled(oA, t, 48, 64)
                link(v.tensor_tensor(u[:, t, :], osum(oA, t, 0, 16), osum(oA, t, 16, 16), ALU.add))
                link(v.tensor_tensor(u[:, t, :], u[:, t, :], osum(oA, t, 32, 16), ALU.add))
                link(v.tensor_tensor(u[:, t, :], u[:, t, :], z[:, t, :], ALU.mult))

            dve.wait_ge(s_row, 16)
            project_out(0, combine_A)

            def qkv(nq, nk):
                for j in range(nq + nk):
                    a, b, f = acc_in()
                    for x, t0 in ((a, 4 * j), (b, 4 * j + 2)):
                        for y in range(2):
                            last = v.tensor_scalar(QK[:, t0 + y, :], x[:, 256 * y:256 * y + 256],
                                                   0.125 if t0 + y < 2 * (nq + nk) else 1.0, None, ALU.mult)
                    last.then_inc(f, 1)
                for dst in (V, z):
                    for j in range(2):
                        evac(dst[:, 0, 512 * j:512 * j + 512], dst[:, 1, 512 * j:512 * j + 512])
                silu_z()
                silu_end()

            norm_in(lambda k: (P, pc("pre", DC + k), None, None), lambda: mods(1))
            qkv(2, 2)
            lam_init = 0.8 - 0.6 * math.exp(-0.3 * 1)
            dve.wait_ge(s_lam, 32)
            l4 = lamb.rearrange("p (a b) -> p a b", b=64)
            link(v.tensor_tensor(TMP[:, 0:128].rearrange("p (a b) -> p a b", a=2), l4[:, 0:3:2, :], l4[:, 1:4:2, :], ALU.mult))
            link(v.tensor_reduce(lamc[:, 0:2], TMP[:, 0:128].rearrange("p (a b) -> p a b", a=2), AX.X, ALU.add))
            dve.sem_inc(s_sq, 1)
            act_does()
            link(v.tensor_tensor(lamc[:, 2:3], lamc[:, 1:2], lamc[:, 0:1], ALU.subtract))
            link(v.tensor_scalar(lamc[:, 2:3], lamc[:, 2:3], -lam_init, None, ALU.add))
            dve.wait_ge(s_bias, 2)
            attention(UB, CAUSAL, 128, 16)
            oB = o_view(16, 128)

            def combine_B(t):
                link(v.reciprocal(cf[:, t, 0:16], rs[:, t, 0:16]))
                odd = cf[:, t, 1:16:2]
                link(v.tensor_scalar(odd, odd, lamc[:, 2:3], None, ALU.mult))
                scaled(oB, t, 16, 128)
                pairs = oB[:, t, :, :].rearrange("p (a m) d -> p m a d", m=2)
                ut = u[:, t, :].rearrange("p (a d) -> p a d", d=128)
                link(v.tensor_tensor(ut, pairs[:, 0, :, :], pairs[:, 1, :, :], ALU.add))
                head_norms(u, 8, 128, [t])
                link(v.scalar_tensor_tensor(ut, ut, 1.0 - lam_init, mid_bc(subg, 8), ALU.mult, ALU.mult))
                link(v.tensor_tensor(u[:, t, :], u[:, t, :], z[:, t, :], ALU.mult))

            project_out(1, combine_B)

            norm_in(lambda k: (P, pc("pre", 2 * DC + k), None, None), lambda: mods(1))
            qkv(1, 2)
            dve.wait_ge(s_bias, 3)
            attention(UC, CAUSAL, 256, 12)
            M4 = ssq[:, 0:8].rearrange("p (t h) -> p t h", t=2)
            link(v.tensor_tensor(M4, nm[:, :, 0:4], nm[:, :, 4:8], ALU.min))
            link(v.tensor_tensor(M4, M4, nm[:, :, 8:12], ALU.min))
            for g in range(3):
                tick(v.tensor_tensor(cf[:, :, 4 * g:4 * g + 4], M4, nm[:, :, 4 * g:4 * g + 4], ALU.subtract))
            own()
            dve.sem_inc(s_sq, 1)
            act_does()
            link(v.tensor_tensor(rs[:, :, 0:12], rs[:, :, 0:12], cf[:, :, 0:12], ALU.mult))
            link(v.tensor_tensor(M4, rs[:, :, 0:4], rs[:, :, 4:8], ALU.add))
            link(v.tensor_tensor(M4, M4, rs[:, :, 8:12], ALU.add))
            link(v.reciprocal(M4, M4))
            for g in range(3):
                tick(v.tensor_tensor(cf[:, :, 4 * g:4 * g + 4], cf[:, :, 4 * g:4 * g + 4], M4, ALU.mult))
            own()
            oC = o_view(12, 256)

            def combine_C(t):
                scaled(oC, t, 12, 256)
                link(v.tensor_tensor(u[:, t, :], osum(oC, t, 0, 4), osum(oC, t, 4, 4), ALU.add))
                link(v.tensor_tensor(u[:, t, :], u[:, t, :], osum(oC, t, 8, 4), ALU.add))
                link(v.tensor_tensor(u[:, t, :], u[:, t, :], z[:, t, :], ALU.mult))

            project_out(2, combine_C)

            norm_in(lambda k: (P, pc("pre", 3 * DC + k), None, None), lambda: mods(1))
            qkv(2, 2)
            dve.sem_inc(s_qkv, 1)
            oD = o_view(16, 64)
            for i in range(17):
                if i < 16:
                    bk = banks[2 * ((acc_before_D + i) % 2)]
                    dve.wait_ge(s_abs, i + 1)
                    link(v.scalar_tensor_tensor(lom[i % 2], bk[:, 0:384], 0.0, sp_[i % 2], ALU.max, ALU.add))
                    v.tensor_tensor(lom[i % 2][:, 0:256], lom[i % 2][:, 0:256], cc("strict"), ALU.mult)
                    v.tensor_scalar(lom[i % 2][:, 256:384], lom[i % 2][:, 256:384], -1.0, None, ALU.mult).then_inc(s_lom, 1)
                if i >= 1:
                    dve.wait_ge(o_done, c.o + 1)
                    ob_in(oD[:, :, i - 1, :], 64)
            own_o()
            c.acc += 16

            def combine_D(t):
                link(v.tensor_tensor(u[:, t, :], osum(oD, t, 0, 16), z[:, t, :], ALU.mult))

            project_out(3, combine_D)

            def modulation_columns():
                mods(1)
                a, b, f = acc_in()
                v.tensor_copy(modc, a[:, 0:32]).then_inc(f, 1)
                own_acc()
                for k, n in ((0, "g1"), (1, "g2")):
                    link(v.tensor_scalar(gs[:, 8 * k:8 * k + 8], modc[:, 16 * k + 8:16 * k + 16], 1.0, None, ALU.add))
                    link(v.tensor_tensor(gs[:, 8 * k:8 * k + 8], gs[:, 8 * k:8 * k + 8], par[:, PC[n][0]:PC[n][1]], ALU.mult))

            norm_in(lambda k: (P, gs[:, k:k + 1], modc[:, k:k + 1], ALU.add), modulation_columns)
            for dst in (NQ, NK):
                evac(dst[:, 0, :], dst[:, 1, :])
            evac(V[:, 0, 0:512], V[:, 1, 0:512])
            evac(LAT[:, 0, :], LAT[:, 1, :], n=416)
            for dst in (z, u):
                for j in range(2):
                    evac(dst[:, 0, 512 * j:512 * j + 512], dst[:, 1, 512 * j:512 * j + 512])
            own_acc()
            for _ in range(2):
                dve.sem_inc(s_sq, 1)
            act_does()
            act_does()
            head_norms(NQ, 8, 64)
            head_norms(NK, 8, 64)
            for a, n, at in ((0, 256, 0), (256, 128, 2)):
                for t in range(T):
                    x = LAT[:, t, a:a + n]
                    link(v.tensor_tensor(TMP[:, 0:n], x, x, ALU.mult))
                    link(v.tensor_reduce(ssq[:, at + t:at + t + 1], TMP[:, 0:n], AX.X, ALU.add))
            dve.sem_inc(s_sq, 1)
            act_does()
            for a, n, at in ((0, 256, 0), (256, 128, 2)):
                for t in range(T):
                    tick(v.tensor_scalar(LAT[:, t, a:a + n], LAT[:, t, a:a + n], rstd[:, at + t:at + t + 1], None, ALU.mult))
            own()
            dve.sem_inc(s_u, 1)
            tr_in(QK[:, 0:4, :], 4, lambda k: (P, pc("naq"), 0.125, ALU.mult))
            tr_in(QK[:, 4:8, :], 4, lambda k: (P, pc("nak"), None, None))
            tr_in(uT, 3, lambda k: (P, pc("qlat", k) if k < 2 else pc("kvlat"), None, None))
            uT_ready()
            cos2 = cosr.rearrange("p (t n) -> p t n", t=2)
            sin2 = sinr.rearrange("p (t n) -> p t n", t=2)

            def rope(dst, x, nh):
                for t in range(T):
                    x1, x2 = x[t][:, :, 0:16], x[t][:, :, 16:32]
                    co, si = mid_bc(cos2[:, t, :], nh), mid_bc(sin2[:, t, :], nh)
                    y = [TMP[:, 128 * k:128 * k + 16 * nh].rearrange("p (h n) -> p h n", h=nh) for k in range(4)]
                    for d, p_, q_ in ((0, x1, co), (1, x2, si), (2, x2, co), (3, x1, si)):
                        tick(v.tensor_tensor(y[d], p_, q_, ALU.mult))
                    own()
                    tick(v.tensor_tensor(dst[t][:, :, 0:16], y[0], y[1], ALU.subtract))
                    tick(v.tensor_tensor(dst[t][:, :, 16:32], y[2], y[3], ALU.add))
                    own()
            rope([KR[:, t:t + 1, :] for t in range(T)],
                 [LAT[:, t, 384:416].rearrange("p (h n) -> p h n", h=1) for t in range(T)], 1)
            for t in range(T):
                evac(MQ[:, t, 0:384], MQ[:, t, 384:768], n=384)
            for t in range(T):
                a, b, f = acc_in()
                for j, bk in ((0, a), (1, b)):
                    y = bk[:, :].rearrange("p (h n) -> p h n", n=128)
                    v.tensor_copy(MK[:, t, 384 * j:384 * j + 384].rearrange("p (h n) -> p h n", n=96)[:, :, 0:64], y[:, :, 0:64])
                    last = v.tensor_copy(V[:, t, 512 + 256 * j:768 + 256 * j].rearrange("p (h n) -> p h n", n=64), y[:, :, 64:128])
                last.then_inc(f, 1)
            own_acc()
            for t in range(T):
                tick(v.tensor_copy(MK[:, t, :].rearrange("p (h n) -> p h n", n=96)[:, :, 64:96], mid_bc(KR[:, t, :], 8)))
            qr = [MQ[:, t, :].rearrange("p (h n) -> p h n", n=96)[:, :, 64:96] for t in range(T)]
            rope(qr, qr, 8)
            head_norms(MQ, 8, 96)
            head_norms(MK, 8, 96)
            dve.sem_inc(s_u, 1)
            tr_in(QK[:, 8:16, :], 8, lambda k: (96, pc("mlaq", 0, 96), 96 ** -0.5, ALU.mult))
            tr_in(uT, 8, lambda k: (96, pc("mlak", 0, 96), None, None))
            tr_own()
            dve.wait_ge(s_bias, 4)
            attention(UN, FULL, 64, 16)
            attention(UM, FULL, 64, 16)
            oN = o_view(16, 64)
            for t in range(T):
                link(v.reciprocal(cf[:, t, 0:16], rs[:, t, 0:16]))
                link(v.tensor_tensor(ym[:, t, :].rearrange("p (j d) -> p j d", d=64), oN[:, t, :, :], last_bc(cf[:, t, 0:16], 64), ALU.mult))
                dve.sem_inc(s_u, 1)
            dve.sem_inc(s_attn, 1)
            for t in range(T):
                tile_in(uT, t)
            for t in range(T):
                a, b, f = acc_in()
                v.tensor_tensor(MG[:, t, 0:512], a[:, :], z[:, t, 0:512], ALU.mult)
                v.tensor_tensor(MG[:, t, 512:1024], b[:, :], z[:, t, 512:1024], ALU.mult).then_inc(f, 1)
            for t in range(T):
                a, b, f = acc_in()
                v.tensor_tensor(MG2[:, t, 0:512], a[:, :], u[:, t, 0:512], ALU.mult)
                v.tensor_tensor(MG2[:, t, 512:1024], b[:, :], u[:, t, 512:1024], ALU.mult).then_inc(f, 1)
                own_acc()
                v.tensor_tensor(MG[:, t, :], MG[:, t, :], MG2[:, t, :], ALU.add).then_inc(s_u, 1)
            for t in range(T):
                tile_in(uT, t)
            for t in range(T):
                pair = c.acc % 2
                a, b, f = acc_in()
                v.tensor_tensor(u[:, t, :], psum[:, 1024 * pair:1024 * pair + 1024], mod[:, 2 * D:3 * D], ALU.mult).then_inc(f, 1)
                own_acc()
                v.tensor_tensor(h[:, t, :], h[:, t, :], u[:, t, :], ALU.add).then_inc(s_sq, 1)
            norm_in(lambda k: (P, gs[:, 8 + k:9 + k], modc[:, 16 + k:17 + k], ALU.add))
            dve.sem_inc(s_sq, 1)

            pair = acc_router % 2
            dve.wait_ge(free["a", pair], 8 + 1)
            sc = gate[:, :, 0:64]
            sel, rep, m8, tmp = rt[0], rt[1], rt[2], rt[3]
            for t in range(T):
                tick(v.tensor_tensor(sel[:, 64 * t:64 * t + 64], sc[:, t, :], ebias, ALU.add))
            own()
            for g in range(16):
                tick(v.max(m8[:, 8 * g:8 * g + 8], sel[:, 8 * g:8 * g + 8]))
            own()
            m83 = m8.rearrange("p (g k) -> p g k", k=8)
            gsc, rk, wsum = rt[4][:, 0:16], rt[4][:, 16:32], rt[4][:, 32:34]
            link(v.tensor_tensor(gsc, m83[:, :, 0], m83[:, :, 1], ALU.add))
            for t in range(T):
                gi = last_bc(gsc[:, 8 * t:8 * t + 8], 8)
                gj = mid_bc(gsc[:, 8 * t:8 * t + 8], 8)
                x, y = rank[:, 0:64].rearrange("p (i j) -> p i j", i=8), rank[:, 64:128].rearrange("p (i j) -> p i j", i=8)
                tick(v.tensor_tensor(x, gj, gi, ALU.is_gt))
                link(v.tensor_tensor(y, gj, gi, ALU.is_equal))
                link(v.tensor_tensor(y, y, cc("lower").rearrange("p (i j) -> p i j", i=8), ALU.mult))
                link(v.tensor_tensor(x, x, y, ALU.add))
                link(v.tensor_reduce(rk[:, 8 * t:8 * t + 8], x, AX.X, ALU.add))
            link(v.tensor_scalar(rk, rk, 3.5, None, ALU.is_lt))
            s3 = sel.rearrange("p (g k) -> p g k", k=8)
            link(v.tensor_tensor(s3, s3, last_bc(rk, 8), ALU.mult))
            link(v.tensor_scalar(rk, rk, 1.0, BIG, ALU.subtract, ALU.mult))
            link(v.tensor_tensor(s3, s3, last_bc(rk, 8), ALU.add))
            for t in range(T):
                link(v.max(m8[:, 8 * t:8 * t + 8], sel[:, 64 * t:64 * t + 64]))
                link(v.match_replace(rep[:, 64 * t:64 * t + 64], m8[:, 8 * t:8 * t + 8], sel[:, 64 * t:64 * t + 64], -2 * BIG))
            link(v.tensor_scalar(rep, rep, -1.5 * BIG, None, ALU.is_lt))
            for t in range(T):
                link(v.tensor_tensor(sc[:, t, :], sc[:, t, :], rep[:, 64 * t:64 * t + 64], ALU.mult))
                link(v.tensor_reduce(wsum[:, t:t + 1], sc[:, t, :], AX.X, ALU.add))
            link(v.reciprocal(wsum, wsum))
            for t in range(T):
                link(v.tensor_scalar(sc[:, t, :], sc[:, t, :], wsum[:, t:t + 1], ROUTED_SCALE, ALU.mult, ALU.mult))
            dve.sem_inc(s_r1, 1)
            dve.wait_ge(s_aux, 1)
            link(v.tensor_scalar(active, banks[2][0:64, 0:1], 0.5, None, ALU.is_gt))
            link(v.tensor_copy(gT, banks[3][0:64, 0:256]))
            dve.sem_inc(s_r2, 1)
            dve.wait_ge(s_aux, 2)
            link(v.tensor_copy(rankc, banks[2][0:64, 1:2]))
            link(v.tensor_scalar(order, cc("negiota")[0:64, :], rankc, active, ALU.is_equal, ALU.mult))
            link(v.tensor_scalar(todo[0:1, 64:65], banks[2][0:1, 2:3], 0.5, 0.25, ALU.mult, ALU.add))
            dve.sem_inc(s_r2, 1)
            dve.wait_ge(s_aux, 3)
            tick(v.tensor_copy(todo[0:1, 0:64], banks[2][0:1, 8:72]))
            tick(v.tensor_copy(gate[:, :, 1:65], banks[3][:, 0:128].rearrange("p (t n) -> p t n", t=2)))
            tick(v.memset(zeros_, 0.0))
            own()
            tick(v.memset(gate[:, :, 0:1], 1.0))
            own()
            dve.sem_inc(s_moe, 1)

            def gu_low(g, j, half):
                dve.wait_ge(s_gh, 2 * g + half + 1)
                x = slice(4 * half, 4 * half + 4)
                v.tensor_tensor(gu_[j][1][:, x, :], guv[j][:, x, :], gu_[j][0][:, x, :], ALU.subtract).then_inc(s_gl, 1)

            def dn_low(g, j):
                dve.wait_ge(s_dh, g + 1)
                v.tensor_tensor(dn_[j][1], dnv[j], dn_[j][0], ALU.subtract).then_inc(s_dl, 1)

            def act_low(g, t):
                dve.wait_ge(s_ah, 2 * g + t + 1)
                v.tensor_tensor(ma2[t][1], banks[2 + t][:, 0:FF], ma2[t][0], ALU.subtract).then_inc(s_al, 1)

            for t in range(T):
                dve.wait_ge(s_ge, t + 1)
                link(v.tensor_tensor(ge[t], ge[t], banks[t][:, 0:FF], ALU.mult))
                v.scalar_tensor_tensor(ma[t], ge[t], gate[:, t, 0:1], banks[t][:, FF:2 * FF], ALU.mult, ALU.mult).then_inc(s_ga, 1)
            pairs = dve.value_load(todo[0:1, 64:65], min_val=TOPK // 2, max_val=EXPERTS // 2)
            dn_low(0, 0)
            gu_low(1, 1, 0)
            gu_low(1, 1, 1)
            with dve.Fori(0, pairs) as it:
                dve.wait_ge(s_ga, 4 * it + 2)
                v.tensor_copy(gcur[:, :, 0:2], gate[:, :, bass.ds(it * 2 + 1, 2)]).then_inc(s_gc, 1)
                dve.wait_ge(s_gc, it + 1)
                for j in range(MOE_SLOTS):
                    g = it * 2 + j

                    def gated(t):
                        n0 = it * 4 + 2 * j + t
                        dve.wait_ge(s_ge, n0 + 3)
                        v.tensor_tensor(ge[t], ge[t], banks[t][:, 0:FF], ALU.mult).then_inc(s_mc, 1)
                        dve.wait_ge(s_mc, n0 + 1)
                        dve.wait_ge(s_gat, n0 + 1)
                        v.scalar_tensor_tensor(ma[t], ge[t], gcur[:, t, j:j + 1], banks[t][:, FF:2 * FF],
                                               ALU.mult, ALU.mult).then_inc(s_ga, 1)

                    act_low(g, 0)
                    gated(0)
                    gu_low(g + 2, j, 0)
                    act_low(g, 1)
                    gu_low(g + 2, j, 1)
                    dn_low(g + 1, 1 - j)
                    gated(1)
            act_low(pairs * 2, 0)
            act_low(pairs * 2, 1)
            dve.wait_ge(s_all, 1)
            for t in range(T):
                for n in range(2):
                    tick(v.tensor_tensor(u[:, t, 512 * n:512 * n + 512], banks[4 + 2 * t + n][:, :],
                                         mod[:, 5 * D + 512 * n:5 * D + 512 * n + 512], ALU.mult))
            own()
            v.tensor_tensor(u_[:, :], u_[:, :], h_[:, :], ALU.add).then_inc(s_fin, 1)


_WEIGHTS = ["x", "norm_post", "a_w_in", "a_w_out", "a_cmp_w1_k", "a_cmp_w2_k", "a_cmp_w1_v", "a_cmp_w2_v", "b_w_in",
            "b_w_out", "b_lambda", "b_sub_gain", "c_w_in", "c_w_out", "d_w_in", "d_w_out", "w_ada_2", "b_ada_2",
            "w_in_2", "na_rpb_2", "w_uq_2", "w_ukv_2", "w_proj_na_2", "w_proj_mla_2", "w_out_2", "w_router_2",
            "e_bias_2", "w_exp_gate_2", "w_exp_up_2", "w_exp_down_2", "w_sh_gate_2", "w_sh_up_2", "w_sh_down_2"]


def kernel(**inputs):
    import concourse.bacc as _bacc
    from concourse import mybir as _mybir
    from concourse.bass_utils import run_bass_kernel_spmd as _run

    def cols(a, k):
        return np.asarray(a).reshape(k, P).T

    f = {k: np.asarray(x) for k, x in inputs.items()}
    par = np.zeros((P, PC_N), np.float32)

    def put(name, a):
        par[0:a.shape[0], PC[name][0]:PC[name][1]] = a
    put("pre", cols(f["norm_pre"].reshape(-1), 4 * DC))
    put("g1", cols(f["g_norm1_2"], DC))
    put("g2", cols(f["g_norm2_2"], DC))
    put("c", cols(f["c_2"], DC))
    put("naq", np.concatenate([f["g_na_q_2"][0]] * 2)[:, None])
    put("nak", np.concatenate([f["g_na_k_2"][0]] * 2)[:, None])
    put("qlat", cols(f["g_q_lat_2"], 2))
    put("kvlat", cols(f["g_kv_lat_2"], 1))
    put("mlaq", f["g_mla_q_2"][0][:, None])
    put("mlak", f["g_mla_k_2"][0][:, None])
    put("posk", cols(f["a_cmp_pos_k"], 16))
    put("posv", cols(f["a_cmp_pos_v"], 16))
    nc = _bacc.Bacc("TRN2", target_bir_lowering=False, num_devices=1)
    given = {n: f[n] for n in _WEIGHTS}
    given["params"] = par
    given["shape_consts"] = shape_constants()
    given["na_rpb_2"] = f["na_rpb_2"][..., ::-1]
    given["pos_cols"] = f["positions_2"].reshape(T, P).T
    arrays, aps = {}, {}
    for n, a in given.items():
        a = np.ascontiguousarray(a)
        arrays[f"in_{n}"] = a
        aps[n] = nc.dram_tensor(f"in_{n}", a.shape, _mybir.dt.from_np(a.dtype), kind="ExternalInput").ap()
    out = nc.dram_tensor("out_x", (1, S, D), _mybir.dt.float32, kind="ExternalOutput").ap()
    build(nc, aps, out)
    r = _run(nc, [arrays], core_ids=[0])
    return r.results[0]["out_x"]
```

```python
import math
import numpy as np
import concourse.bass as bass
from concourse import mybir
from contextlib import ExitStack

S, D, P, T = 256, 1024, 128, 2
DC = D // P
HD = 64
RING = 3
SLOT = 4096
N_CMP, CMP_L, CMP_ST = 15, 32, 16
A_COLS = dict(q=0, kc=1024, vc=1280, ks=1536, vs=1792, kw=2048, vw=2304, gl=2560, z=2608)
EXPERTS, FF, TOPK, GROUPS = 64, 256, 8, 8
ROUTED_SCALE = 2.5
EPS = 1e-6
BIG = 1e30
MOE_SLOTS = 2

PC = {}
_at = 0
for _n, _w in (("pre", 4 * DC), ("g1", DC), ("g2", DC), ("c", DC), ("naq", 1), ("nak", 1), ("qlat", 2),
               ("kvlat", 1), ("mlaq", 1), ("mlak", 1), ("posk", 16), ("posv", 16)):
    PC[_n] = (_at, _at + _w)
    _at += _w
PC_N = _at

CC = {}
_at = 0
for _n, _w in (("dist", 4 * 256), ("win", 256), ("cbias", 480), ("cmask", 30), ("strict", 256),
               ("tri", 128), ("lower", 64), ("freq", 16), ("negiota", 64), ("row", 1)):
    CC[_n] = (_at, _at + _w)
    _at += _w
CC_N = _at


def slopes(n):
    return [2.0 ** (-8.0 * (i + 1) / n) for i in range(n)]


def shape_constants():
    a = np.zeros((P, CC_N), np.float32)
    p = np.arange(P)[:, None]
    dist = P + p - np.arange(2 * P)[None, :]
    ok = dist >= 0
    pats = [ok, ok & (dist <= 128), ok & (dist % 4 == 0), ok & (dist % 16 == 0)]
    a[:, CC["dist"][0]:CC["dist"][1]] = np.stack([np.where(m, dist, BIG) for m in pats], 1).reshape(P, -1)
    col = p % 64
    kcol = 63 - np.arange(256)[None, :] % 64
    start = np.clip(col - 8, 0, 48)
    a[:, CC["win"][0]:CC["win"][1]] = np.where((kcol >= start) & (kcol < start + 16), 0.0, -BIG)
    end = CMP_ST * np.arange(N_CMP) + CMP_L - 1
    tok = np.arange(2)[None, :, None] * P + np.arange(P)[:, None, None]
    cd = tok - end[None, None, :]
    sl = np.array(slopes(16), np.float32)
    cb = np.where(cd[:, :, None, :] >= 0, -sl[None, None, :, None] * cd[:, :, None, :].astype(np.float32), -BIG)
    a[:, CC["cbias"][0]:CC["cbias"][1]] = cb.reshape(P, -1)
    a[:, CC["cmask"][0]:CC["cmask"][1]] = (cd >= 0).reshape(P, -1)
    q = np.arange(P)[None, :]
    neg = -(p < q).astype(np.float32)
    a[:, CC["strict"][0]:CC["strict"][1]] = np.concatenate([neg, neg], 1)
    a[:, CC["tri"][0]:CC["tri"][1]] = (p >= q)
    i, j = np.arange(8)[:, None], np.arange(8)[None, :]
    a[:, CC["lower"][0]:CC["lower"][1]] = (j < i).reshape(1, 64)
    a[:, CC["freq"][0]:CC["freq"][1]] = (np.float32(10000.0) ** (-np.arange(16, dtype=np.float32) / np.float32(16)))[None, :]
    a[:, CC["negiota"][0]:CC["negiota"][1]] = -np.arange(64)[None, :]
    a[:, CC["row"][0]:CC["row"][1]] = p
    return a


def build(nc, A, out):
    f32 = mybir.dt.float32
    f32r = mybir.dt.float32r
    i32 = mybir.dt.int32
    ALU = mybir.AluOpType
    ACT = mybir.ActivationFunctionType
    AX = mybir.AxisListType
    ctx = ExitStack()
    with ctx:
        def sb(name, *shape, dt=f32, stack=ctx):
            return stack.enter_context(nc.sbuf_tensor(name, [shape[0], int(np.prod(shape[1:]))], dt))

        def sem(name):
            return ctx.enter_context(nc.semaphore(name))

        ident = sb("ident", P, 128)
        cst = sb("shape_consts", P, CC_N)
        par = sb("params", P, PC_N)
        h_ = sb("h", P, T * D)
        u_ = sb("u", P, T * D)
        V_ = sb("V", P, T * D)
        mod = sb("mod", P, 6 * D)
        w2_ = sb("w2", P, 4 * 64)
        kcT = sb("kcmpT", P, 64)
        ones = sb("ones", P, 128)
        lam_ = sb("lambda_subgain", P, 384)
        sm = sb("small", P, 1120)
        posn = sb("positions", P, 2, dt=i32)
        todo = sb("expert_list", 1, 66, dt=i32)

        with ExitStack() as layers:
            uT_ = sb("uT", P, DC * S, stack=layers)
            pT_ = sb("probsT", P, 4 * 512, stack=layers)
            ring = [sb(f"ring{i}", P, SLOT, stack=layers) for i in range(RING)]
            QK_ = sb("QK", P, 16 * S, stack=layers)
            pb_ = sb("probs", P, 2 * 1024, stack=layers)
            ob = sb("oraw", P, 6144, stack=layers)
            bias_ = sb("bias", P, 16 * 256, stack=layers)
            z_ = sb("z", P, T * D, stack=layers)
            gpost = sb("gpost", P, D, stack=layers)
        with ExitStack() as projections:
            uTl_ = sb("input_low", P, DC * S, dt=f32r, stack=projections)
            uTh_ = sb("input_high", P, DC * S, dt=f32r, stack=projections)
            w_lo = [sb(f"weights_low{i}", P, SLOT, dt=f32r, stack=projections) for i in range(RING)]
            sb("over_QK", P, 16 * S, stack=projections)
            w_hi = [sb(f"weights_high{i}", P, SLOT, dt=f32r, stack=projections) for i in range(2)]
        sb("over_uT_probsT", P, 2 * DC * S)
        gu_lo = [sb(f"gate_up_low{j}", P, SLOT, dt=f32r) for j in range(MOE_SLOTS)]
        dn_lo = sb("down_low", P, SLOT, dt=f32r)
        gu_hi0 = sb("gate_up_high0", P, SLOT, dt=f32r)
        sb("over_probs", P, 2 * 1024)
        gu_hi = [gu_hi0, sb("gate_up_high1", P, SLOT, dt=f32r)]
        dn_hi = sb("down_high", P, SLOT, dt=f32r)
        uT_hi = sb("uT_high", P, DC * S, dt=f32r)
        uT_lo = sb("uT_low", P, DC * S, dt=f32r)
        ma_hi = sb("act_high", P, 2 * 256, dt=f32r)
        ma_lo = sb("act_low", P, 2 * 256, dt=f32r)

        h = h_[:, :].rearrange("p (t n) -> p t n", t=T)
        u = u_[:, :].rearrange("p (t n) -> p t n", t=T)
        uT = uT_[:, :].rearrange("p (c s) -> p c s", s=S)
        QK = QK_[:, :].rearrange("p (c s) -> p c s", s=S)
        V = V_[:, :].rearrange("p (t n) -> p t n", t=T)
        z = z_[:, :].rearrange("p (t n) -> p t n", t=T)
        bias = bias_[:, :].rearrange("p (h k) -> p h k", k=256)
        probs = pb_[:, :].rearrange("p (u t i k) -> p u t i k", u=2, t=2, i=2)
        probsT = pT_[:, :].rearrange("p (b n) -> p b n", n=512)
        w2 = w2_[:, :].rearrange("p (v c n) -> p v c n", v=2, c=2)

        def small(a, n):
            return sm[:, a:a + n]
        ssq, lnv, rstd = small(0, 16), small(16, 16), small(32, 16)
        rs = small(64, 96).rearrange("p (t j) -> p t j", t=2)
        nm = small(160, 96).rearrange("p (t j) -> p t j", t=2)
        cf = small(256, 96).rearrange("p (t j) -> p t j", t=2)
        gate = small(352, 132).rearrange("p (t j) -> p t j", t=2)
        epsc, onec, zeroc = small(484, 1), small(485, 1), small(486, 1)
        lamc = small(488, 8)
        gcur = small(496, 8).rearrange("p (t j) -> p t j", t=2)
        cosr = small(512, 32)
        sinr = small(544, 32)
        modc = small(576, 32)
        gs = small(608, 16)
        siluc = small(624, 16)
        gelu_x, gelu_t = small(640, 240), small(880, 240)
        rank = small(640, 256)

        psum = ctx.enter_context(nc.psum_tensor("psum", [P, 8 * 512], f32))
        banks = [psum[:, 512 * i:512 * i + 512] for i in range(8)]

        s_const, s_h, s_gpost, s_small = sem("consts_in"), sem("h_in"), sem("gpost_in"), sem("smalls_in")
        s_rpb, s_lam, s_row, s_rt, s_out = sem("rpb_in"), sem("lambda_in"), sem("b_ada_in"), sem("router_in"), sem("out_done")
        w_in = [sem(f"weights_in{i}") for i in range(RING)]
        acc_done = sem("acc_done")
        free = {("d", 0): sem("acc0_free_dve"), ("d", 1): sem("acc1_free_dve"),
                ("a", 0): sem("acc0_free_act"), ("a", 1): sem("acc1_free_act"),
                ("td", 0): sem("tr0_free_dve"), ("td", 1): sem("tr1_free_dve"),
                ("ta", 0): sem("tr0_free_act"), ("ta", 1): sem("tr1_free_act"),
                ("o", 0): sem("o0_free"), ("o", 1): sem("o1_free")}
        tr_done = sem("transposes_done")
        o_done = sem("o_done")
        dch, ach, pch, pech = sem("dve_chain"), sem("act_chain"), sem("pool_chain"), sem("pe_chain")
        s_sq = sem("ready_for_rstd")
        s_rstd = sem("act_result")
        s_u = sem("u_ready")
        s_uT = sem("uT_ready")
        s_qkv = sem("qkv_ready")
        s_mx = sem("max_ready")
        s_p = sem("probs_ready")
        s_bias = sem("bias_ready")
        s_attn = sem("attn_done")
        s_x = sem("cmp_in_ready")
        s_xp = sem("cmp_windows_ready")
        s_hid = sem("cmp_hidden_ready")
        s_cum = sem("cumsum_done")
        s_lom = sem("log_om_ready")
        s_abs = sem("softplus_parts_ready")
        s_am = sem("stick_weights_ready")
        s_id = sem("ident_ready")
        gu_in = [sem(f"gate_up_in{i}") for i in range(MOE_SLOTS)]
        dn_in = [sem(f"down_in{i}") for i in range(MOE_SLOTS)]
        s_gu, s_dn = sem("gate_up_done"), sem("down_done")
        s_ge, s_ga, s_gat = sem("moe_exp"), sem("moe_act"), sem("moe_act_transposed")
        s_ah, s_al = sem("moe_actT_high"), sem("moe_actT_low")
        s_gh, s_gl = sem("gate_up_high_ready"), sem("gate_up_low_ready")
        s_dh, s_dl = sem("down_high_ready"), sem("down_low_ready")
        s_uh, s_ul = sem("uT_high_ready"), sem("uT_low_ready")
        s_wh, s_wl = sem("weights_high_ready"), sem("weights_low_ready")
        s_wf = sem("first_weights_low_ready")
        s_moe = sem("moe_gates_ready")
        s_fin = sem("final_ready")
        s_r1, s_r2, s_aux = sem("expert_masks_ready"), sem("expert_ranks_ready"), sem("expert_sums_done")
        s_all = sem("experts_done")
        s_gc, s_mc = sem("moe_weights_copied"), sem("moe_chain")

        guv = [ring[j][:, :].rearrange("p (c n) -> p c n", n=2 * FF) for j in range(MOE_SLOTS)]
        dnv = [ring[2][:, 2048 * j:2048 * j + 2048].rearrange("p (c n) -> p c n", n=D) for j in range(MOE_SLOTS)]
        gu_ = [[x[j][:, :].rearrange("p (c n) -> p c n", n=2 * FF) for x in (gu_hi, gu_lo)] for j in range(MOE_SLOTS)]
        dn_ = [[x[:, 2048 * j:2048 * j + 2048].rearrange("p (c n) -> p c n", n=D) for x in (dn_hi, dn_lo)] for j in range(MOE_SLOTS)]
        in2 = [x[:, :].rearrange("p (c s) -> p c s", s=S) for x in (uTh_, uTl_)]
        uT2 = [x[:, :].rearrange("p (c s) -> p c s", s=S) for x in (uT_hi, uT_lo)]
        ma2 = [[x[:, 256 * t:256 * t + 256] for x in (ma_hi, ma_lo)] for t in range(T)]
        PARTS = ((0, 0), (0, 1), (1, 0))

        class Count:
            def __init__(self):
                self.acc = self.tr = self.o = self.w = 0
                self.win = [0] * RING
                self.n = {}

            def up(self, name, by=1):
                self.n[name] = self.n.get(name, 0) + by
                return self.n[name]

        class Own:
            def __init__(self, eng, s):
                self.eng, self.s, self.n = eng, s, 0

            def tick(self, ins):
                self.n += 1
                ins.then_inc(self.s, 1)

            def own(self):
                self.eng.wait_ge(self.s, self.n)

            def link(self, ins):
                self.tick(ins)
                self.own()

        def pc(name, i=0, p=P):
            a = PC[name][0] + i
            return par[0:p, a:a + 1]

        def cc(name):
            return cst[:, CC[name][0]:CC[name][1]]

        dist = cc("dist").rearrange("p (m k) -> p m k", k=256)
        tri = cc("tri")

        def last_bc(ap, n):
            return bass.AP(ap.tensor, ap.offset, [*ap.ap, [0, n]])

        def mid_bc(ap, n):
            return bass.AP(ap.tensor, ap.offset, [ap.ap[0], [0, n], *ap.ap[1:]])

        def row_bc(ap, n):
            return bass.AP(ap.tensor, ap.offset, [[0, P], [1, n]])

        def head(q, k, job, v, bidx):
            return dict(q=q, k=k, job=job, v=v, b=bidx)

        def o_view(n, dv):
            return ob[:, 0:2 * n * dv].rearrange("p (t j d) -> p t j d", t=2, j=n)

        UA, UB, UC, UN, UM = [], [], [], [], []
        for br in range(2):
            for hp in range(8):
                UA.append([head(QK[64 * i:64 * i + 64, hp, :], QK[64 * i:64 * i + 64, 8 + 4 * br + hp // 2, :],
                                16 + 16 * br + 2 * hp + i, (256 * br + 64 * (hp // 2), 64), 2 * hp + i) for i in range(2)])
        for hh in range(8):
            UB.append([head(QK[64 * i:64 * i + 64, hh, :], QK[64 * i:64 * i + 64, 8 + hh, :],
                            2 * hh + i, (128 * hh, 128), 2 * hh + i) for i in range(2)])
        for x in range(6):
            UC.append([head(QK[64 * i:64 * i + 64, x, :], QK[64 * i:64 * i + 64, 6 + x, :],
                            2 * x + i, (256 * ((2 * x + i) % 4), 256), 2 * x + i) for i in range(2)])
        for x in range(4):
            UN.append([head(QK[64 * i:64 * i + 64, x, :], QK[64 * i:64 * i + 64, 4 + x, :],
                            2 * x + i, (64 * (2 * x + i), 64), 2 * x + i) for i in range(2)])
            UM.append([head(QK[0:96, 8 + 2 * x + i, :], uT[0:96, 2 * x + i, :],
                            8 + 2 * x + i, (512 + 64 * (2 * x + i), 64), None) for i in range(2)])
        CAUSAL, FULL = [(1, 0), (1, 1), (0, 0)], [(1, 0), (1, 1), (0, 0), (0, 1)]
        LAYERS = ((UA, CAUSAL, 48, 64), (UB, CAUSAL, 16, 128), (UC, CAUSAL, 12, 256))

        Xc = bias_[:, 0:2048].rearrange("p (v g s) -> p v g s", v=2, g=4)
        Xp = bias_[:, 2048:2048 + 1920].rearrange("p (v l n) -> p v l n", v=2, l=16)
        hid = gelu_x.rearrange("p (f n) -> p f n", n=60)
        vd = mod[:, 1024:2048].rearrange("p (g n) -> p g n", g=4)
        pc_ = mod[:, 0:1024].rearrange("p (t h n) -> p t h n", t=2, n=32)
        pcT = u_[:, 0:1024].rearrange("p (b q) -> p b q", q=128)
        sp_ = [bias_[:, 768 * i:768 * i + 768].rearrange("p (i k) -> p i k", i=2) for i in range(2)]
        lom = [bias_[:, 1536 + 768 * i:2304 + 768 * i].rearrange("p (i k) -> p i k", i=2) for i in range(2)]
        am = [pb_[:, 768 * i:768 * i + 768].rearrange("p (i k) -> p i k", i=2) for i in range(2)]

        def stick_pair(i):
            a = 1024 * ((acc_before_D + i) % 2)
            return psum[:, a:a + 1024].rearrange("p (i k) -> p i k", i=2)[:, :, 0:384]
        SH = [(QK[64 * (i % 2):64 * (i % 2) + 64, i // 2, :], QK[64 * (i % 2):64 * (i % 2) + 64, 8 + i // 2, :]) for i in range(16)]
        NQ = QK_[:, 2048:3072].rearrange("p (t n) -> p t n", t=2)
        NK = QK_[:, 3072:4096].rearrange("p (t n) -> p t n", t=2)
        LAT = gpost[:, 0:832].rearrange("p (t n) -> p t n", t=2)
        MQ = ob[:, 0:1536].rearrange("p (t n) -> p t n", t=2)
        MK = ob[:, 2880:4416].rearrange("p (t n) -> p t n", t=2)
        KR = ob[:, 4416:4480].rearrange("p (t n) -> p t n", t=2)
        TMP = pb_[:, 0:1536]
        MG = ob[:, 2048:4096].rearrange("p (t n) -> p t n", t=2)
        MG2 = ob[:, 4096:6144].rearrange("p (t n) -> p t n", t=2)
        ym = bias_[:, 0:2048].rearrange("p (t n) -> p t n", t=2)
        ge = [V_[:, 256 * t:256 * t + 256] for t in range(2)]
        ma = [V_[:, 512 + 256 * t:768 + 256 * t] for t in range(2)]
        wr = pT_[:, 1024:1536].rearrange("p (c n) -> p c n", n=64)
        ebias = pT_[:, 1536:1600]
        rt = [pb_[:, 128 * i:128 * i + 128] for i in range(8)]
        active, rankc = small(896, 1)[0:64, :], small(897, 1)[0:64, :]
        order, gT = pb_[0:64, 1024:1088], pb_[0:64, 1280:1536]
        zeros_ = pT_[:, 0:512]
        ones_, ones_row = ones[:, :], ones[0:1, :]
        lamb, subg = lam_[:, 0:256], lam_[:, 256:384]

        def cols(ap, a, n):
            return [(0, 8 * n, ap[:, a:a + n].rearrange("(c p) n -> p c n", p=P), n)]
        aw, bw, cw, dw, ew = A["a_w_in"][0], A["b_w_in"][0], A["c_w_in"][0], A["d_w_in"][0], A["w_in_2"][0]
        MOD = [cols(A["w_ada_2"][0], 512 * j, 512) for j in range(12)]
        LA = [cols(aw, c, 512) for c in (1024, 0, 512, 1536, 2048, 2608, 3120)] + [cols(aw, 2560, 48)]
        LA_CMP = [[(0, SLOT, A[n][0].rearrange("(c p) n -> p c n", p=P), 256)] for n in ("a_cmp_w1_k", "a_cmp_w1_v")]
        LB = [cols(bw, 512 * j, 512) for j in range(8)]
        LC = [cols(cw, 512 * j, 512) for j in range(7)]
        LD = [cols(dw, 512 * j, 512) for j in range(8)]
        LE = [cols(ew, 512 * j, 512) for j in range(3)] + [cols(ew, 1536, 416)] + [cols(ew, 1952 + 512 * j, 512) for j in range(4)]
        LE_UP = [[(0, 1536, A["w_uq_2"][0].rearrange("(c p) n -> p c n", p=P), 768),
                  (1536, 1024, A["w_ukv_2"][0].rearrange("(c p) n -> p c n", p=P), 1024)]]
        LE_PROJ = [[(0, SLOT, A[n][0].rearrange("(c p) n -> p c n", p=P), 1024)] for n in ("w_proj_na_2", "w_proj_mla_2")]

        def outw(ap):
            return [cols(ap, 512 * j, 512) for j in range(2)]

        def one(loads, fills=1):
            return [(w, fills, 0) for w in loads]

        def closing(w_out, mods, columns=0):
            a, b = outw(w_out)
            return one(MOD[mods:mods + 2]) + [(a, 0, 2), (b, 2, 0)] + [(None, columns, 0)] + one(MOD[mods + 2:mods + 3])

        STREAM = one(LA[0:3]) + [(LA_CMP[0], 0, 1), (LA_CMP[1], 1, 0)] + one(LA[3:4]) + [(None, 1, 0)]
        STREAM += one(LA[4:5]) + [(None, 1, 0)] + one(LA[5:]) + [(None, len(UA), 0)] + closing(A["a_w_out"][0], 0)
        STREAM += one(LB) + [(None, len(UB), 0)] + closing(A["b_w_out"][0], 3)
        STREAM += one(LC) + [(None, len(UC), 0)] + closing(A["c_w_out"][0], 6)
        STREAM += one(LD)
        acc_B = len(LA) + 3 + len(UA) + 5
        acc_C = acc_B + len(LB) + len(UB) + 5
        acc_before_D = sum(f for _, f, _ in STREAM)
        STREAM += [(None, 8, 0)] + closing(A["d_w_out"][0], 9, columns=1)
        STREAM += one(LE) + one(LE_UP, 4) + [(None, 8, 0)] + one(LE_PROJ, 2)
        a_, b_ = outw(A["w_out_2"][0])
        STREAM += [(a_, 0, 2), (b_, 2, 0)]
        acc_router = sum(f for _, f, _ in STREAM)
        assert sum(w is not None for w, _, _ in STREAM) % RING == 0

        SPLITS, at, fills, loaded = [], 0, 0, [0] * RING
        for loads, f, _ in STREAM:
            fills += f
            if loads is not None:
                loaded[at % RING] += 16 * len(loads)
                if any(loads is x for x in LA + LB + LC + LD + LE):
                    SPLITS.append((at % RING, loaded[at % RING], fills, loads[0][1]))
                at += 1
        FIRST = [sum(len(x) for x in (LA, LB, LC, LD)[:i]) for i in range(5)]

        block = ctx.enter_context(nc.Block())

        @block.sync
        def _(sp):
            sp.dma_start(h[:, :, :], A["x"][0].rearrange("(t p) n -> p t n", p=P)).then_inc(s_h, 16)
            sp.wait_ge(s_const, 48)
            sp.wait_ge(s_h, 16)
            n, fills, done_at = 0, 0, []
            for loads, f, ahead in STREAM:
                fills += f
                if loads is None:
                    continue
                if n >= RING:
                    sp.wait_ge(acc_done, done_at[n - RING])
                for off, size, src, width in loads:
                    dst = ring[n % RING][:, off:off + size].rearrange("p (c n) -> p c n", n=width)
                    sp.dma_start(dst, src).then_inc(w_in[n % RING], 16)
                done_at.append(fills + ahead)
                n += 1
            def gate_up(j, g, up):
                sp.dma_start(guv[j][:, :, 0:FF], g.rearrange("(c p) n -> p c n", p=P)).then_inc(gu_in[j], 16)
                sp.dma_start(guv[j][:, :, FF:2 * FF], up.rearrange("(c p) n -> p c n", p=P)).then_inc(gu_in[j], 16)

            def down(j, dn):
                sp.dma_start(dnv[j], dn.rearrange("(c p) n -> p c n", p=P)).then_inc(dn_in[j], 16)

            def chosen(name, e):
                return A[name][0][bass.ds(e, 1)].rearrange("e k n -> (e k) n")

            def expert_id(k):
                return sp.value_load(todo[0:1, bass.ds(k, 1)], min_val=0, max_val=EXPERTS - 1)

            sp.wait_ge(acc_done, done_at[n - RING])
            gate_up(0, A["w_sh_gate_2"][0], A["w_sh_up_2"][0])
            sp.wait_ge(acc_done, fills)
            down(0, A["w_sh_down_2"][0])
            sp.wait_ge(s_moe, 1)
            pairs = sp.value_load(todo[0:1, 64:65], min_val=TOPK // 2, max_val=EXPERTS // 2)

            def step(g, j, first=False):
                e2, e1 = expert_id(g + 1), expert_id(g)
                sp.wait_ge(s_gu, 2 * g + 2)
                gate_up(j, chosen("w_exp_gate_2", e2), chosen("w_exp_up_2", e2))
                if not first:
                    sp.wait_ge(s_dn, 2 * g)
                down(1 - j, chosen("w_exp_down_2", e1))

            e = expert_id(0)
            gate_up(1, chosen("w_exp_gate_2", e), chosen("w_exp_up_2", e))
            step(0, 0, first=True)
            step(1, 1)
            with sp.Fori(1, pairs) as it:
                for j in range(MOE_SLOTS):
                    step(it * 2 + j, j)
            sp.wait_ge(s_fin, 1)
            sp.dma_start(out[0].rearrange("(t p) n -> p t n", p=P), u[:, :, :]).then_inc(s_out, 16)
            sp.wait_ge(s_out, 16)


        @block.tensor
        def _(pe):
            c, me = Count(), Own(pe, pech)
            prev = {}

            def take(kind, i, releaser):
                if (kind, i) in prev:
                    pe.wait_ge(*prev[kind, i])
                prev[kind, i] = (free[releaser, i], c.up((releaser, i)))

            def acc(releaser):
                i = c.acc % 2
                take("acc", i, releaser)
                c.acc += 1
                return banks[2 * i], banks[2 * i + 1]

            def tr(releaser):
                i = c.tr % 2
                take("tr", i, releaser)
                c.tr += 1
                return banks[4 + i]

            def obank():
                i = c.o % 2
                take("o", i, "o")
                c.o += 1
                return banks[6 + i]

            def slot():
                i = c.w % RING
                c.w += 1
                c.win[i] += 16
                pe.wait_ge(w_in[i], c.win[i])
                return ring[i]

            def transposes(src, chunks, releaser="td"):
                for k in range(0, len(chunks), 2):
                    b = tr(releaser)
                    for j, (a, w) in enumerate(chunks[k:k + 2]):
                        for t in range(T):
                            last = nc.tensor.transpose(b[0:w, 256 * j + 128 * t:256 * j + 128 * t + 128],
                                                       src[:, t, a:a + w], ident[:, :])
                    last.then_inc(tr_done, 1)

            CH = [(128 * k, 128) for k in range(DC)]

            def tile_transposes(src, releaser="td"):
                for t in range(T):
                    pe.wait_ge(s_u, c.up("u"))
                    for k in range(0, DC, 4):
                        b = tr(releaser)
                        for j in range(4):
                            last = nc.tensor.transpose(b[:, 128 * j:128 * j + 128],
                                                       src[:, t, 128 * (k + j):128 * (k + j) + 128], ident[:, :])
                        last.then_inc(tr_done, 1)
                    yield t

            def mm_T(bank, w2_, col, n=256):
                for f in range(n // 128):
                    k = 0
                    for d in range(DC):
                        for y, x in PARTS:
                            last = nc.tensor.matmul(bank[:, 256 * f:256 * f + 256],
                                                    w2_[x][:, d, col + 128 * f:col + 128 * f + 128], in2[y][:, d, :],
                                                    start=(k == 0), stop=(k == 3 * DC - 1))
                            k += 1
                return last

            def mm_P(out_, w2_, t, col, n):
                k = 0
                for d in range(DC):
                    for x, y in PARTS:
                        last = nc.tensor.matmul(out_, in2[x][:, d, 128 * t:128 * t + 128], w2_[y][:, d, col:col + n],
                                                start=(k == 0), stop=(k == 3 * DC - 1))
                        k += 1
                return last

            def mm_R(out_, w, t, col, n, lhs=None, kc=DC):
                for d in range(kc):
                    last = nc.tensor.matmul(out_, uT[:, (lhs or 0) + d, 128 * t:128 * t + 128], w[:, d, col:col + n],
                                            start=(d == 0), stop=(d == kc - 1))
                return last

            def proj(kind, n=512):
                i = c.w % RING
                slot()
                m = c.up("split")
                w = [x[:, 0:8 * n].rearrange("p (c n) -> p c n", n=n) for x in (w_hi[(m - 1) % 2], w_lo[i])]
                if m - 1 in FIRST:
                    pe.wait_ge(s_wf, FIRST.index(m - 1) + 1)
                pe.wait_ge(s_wl, 2 * m - sum(x < m for x in FIRST))
                a, b = acc("d")
                if kind == "TT":
                    mm_T(a, w, 0)
                    last = mm_T(b, w, 256)
                elif kind == "TR":
                    mm_T(a, w, 0)
                    mm_P(b[:, 0:256], w, 0, 256, 256)
                    last = mm_P(b[:, 256:512], w, 1, 256, 256)
                else:
                    mm_P(a[:, 0:n], w, 0, 0, n)
                    last = mm_P(b[:, 0:n], w, 1, 0, n)
                last.then_inc(acc_done, 1)

            def norm_in():
                for t in tile_transposes(u):
                    pass
                pe.wait_ge(s_uT, c.up("uT", 2))

            def modulation():
                w = slot()[:, :].rearrange("p (c n) -> p c n", n=512)
                a, _b = acc("d")
                for d in range(DC):
                    last = nc.tensor.matmul(a[:, :], last_bc(siluc[:, d:d + 1], P)[:, 0, :], w[:, d, :],
                                            start=(d == 0), stop=(d == DC - 1))
                last.then_inc(acc_done, 1)

            def attention(units, blocks, dv):
                nk0 = 128 if blocks is CAUSAL else 256
                pe.wait_ge(s_qkv, c.up("qkv"))

                def scores(un):
                    a, b = acc("d")
                    for x, bk in ((un[0], a), (un[1], b)):
                        nc.tensor.matmul(bk[:, 0:256], x["q"][:, 128:256], x["k"][:, 0:256], start=True, stop=True)
                        last = nc.tensor.matmul(bk[:, 256:256 + nk0], x["q"][:, 0:128], x["k"][:, 0:nk0],
                                                start=True, stop=True)
                    last.then_inc(acc_done, 1)

                ready = {}

                def probs_T(n):
                    pe.wait_ge(s_p, c.up("p"))
                    for i in range(2):
                        rel = "ta" if i == 0 else "td"
                        at = c.tr % 2
                        b = tr(rel)
                        for k, (qt, kb) in enumerate(blocks):
                            last = nc.tensor.transpose(b[:, 128 * k:128 * k + 128],
                                                       probs[:, n % 2, qt, i, 128 * kb:128 * kb + 128], ident[:, :])
                        last.then_inc(tr_done, 1)
                        ready[n, i] = prev["tr", at]

                def values(n, un):
                    for i, x in enumerate(un):
                        ob_ = obank()
                        pe.wait_ge(*ready[n, i])
                        for qt in (1, 0):
                            ks = [(k, kb) for k, (q_, kb) in enumerate(blocks) if q_ == qt]
                            for j, (k, kb) in enumerate(ks):
                                last = nc.tensor.matmul(ob_[:, dv * qt:dv * qt + dv],
                                                        probsT[:, 2 * (n % 2) + i, 128 * k:128 * k + 128],
                                                        V[:, kb, x["v"][0]:x["v"][0] + dv],
                                                        start=(j == 0), stop=(j == len(ks) - 1))
                        last.then_inc(o_done, 1)

                scores(units[0])
                for n in range(len(units)):
                    if n + 1 < len(units):
                        scores(units[n + 1])
                    probs_T(n)
                    if n >= 1:
                        values(n - 1, units[n - 1])
                values(len(units) - 1, units[-1])

            def project_out(src, mods=True, between=None):
                if mods:
                    modulation()
                    modulation()
                w = [slot()[:, :].rearrange("p (c n) -> p c n", n=512) for _ in range(2)]
                for t in tile_transposes(src):
                    pe.wait_ge(s_uT, c.up("uT"))
                    a, b = acc("d")
                    mm_R(a[:, :], w[0], t, 0, 512)
                    mm_R(b[:, :], w[1], t, 0, 512).then_inc(acc_done, 1)
                if between is not None:
                    between()
                if mods:
                    modulation()

            def columns():
                a, _b = acc("d")
                for k, base in enumerate((0, D, 3 * D, 4 * D)):
                    for d in range(DC):
                        last = nc.tensor.matmul(a[:, 8 * k + d:8 * k + d + 1], mod[0:1, base + 128 * d:base + 128 * d + 128],
                                                ones_row[0:1, 0:1], start=True, stop=True)
                last.then_inc(acc_done, 1)

            pe.wait_ge(s_id, 2)
            norm_in()
            pe.wait_ge(s_u, c.up("u"))
            for _ in range(3):
                proj("TT")
            wk, wv = slot(), slot()
            a, b = acc("d")
            pe.wait_ge(s_xp, 1)
            for v, (w, bk) in enumerate(((wk, a), (wv, b))):
                w = w[:, :].rearrange("p (c n) -> p c n", n=256)
                for f in range(2):
                    for l in range(16):
                        last = nc.tensor.matmul(bk[:, 64 * f:64 * f + 60], w[:, l, 128 * f:128 * f + 128], Xp[:, v, l, :],
                                                start=(l == 0), stop=(l == 15))
            last.then_inc(acc_done, 1)
            proj("TR")
            pe.wait_ge(s_hid, 1)
            pe.wait_ge(s_small, 32)
            a, b = acc("d")
            for f in range(2):
                nc.tensor.matmul(a[0:64, 0:60], w2[:, 0, f, :], hid[:, f, :], start=(f == 0), stop=(f == 1))
            for g in range(4):
                for f in range(2):
                    last = nc.tensor.matmul(b[0:15, 64 * g:64 * g + 64], hid[:, 2 + f, 15 * g:15 * g + 15], w2[:, 1, f, :],
                                            start=(f == 0), stop=(f == 1))
            last.then_inc(acc_done, 1)
            proj("TR")
            pe.wait_ge(s_hid, 2)
            a, b = acc("d")
            for qt in range(2):
                for i in range(16):
                    r, bk = 64 * (i % 2), (a, b)[i % 2]
                    at = 128 * qt + 16 * (i // 2)
                    last = nc.tensor.matmul(bk[:, at:at + 15], QK[r:r + 64, i // 2, 128 * qt:128 * qt + 128],
                                            kcT[r:r + 64, 15 * (i // 4):15 * (i // 4) + 15], start=True, stop=True)
            last.then_inc(acc_done, 1)
            proj("RR")
            proj("RR")
            proj("RR", 48)
            pe.wait_ge(s_hid, 3)
            for g2 in range(2):
                bk = tr("td")
                for k in range(4):
                    g, qt = 2 * g2 + k // 2, k % 2
                    last = nc.tensor.transpose(bk[:, 128 * k:128 * k + 128],
                                               mod[:, 512 * qt + 128 * g:512 * qt + 128 * g + 128], ident[:, :])
                last.then_inc(tr_done, 1)
            for g in range(4):
                bk = obank()
                pe.wait_ge(free["td", (c.tr - 2 + g // 2) % 2], c.n["td", (c.tr - 2 + g // 2) % 2])
                for qt in range(2):
                    last = nc.tensor.matmul(bk[:, 256 * qt:256 * qt + 256], pcT[:, 2 * g + qt, :], vd[:, g, :],
                                            start=True, stop=True)
                last.then_inc(o_done, 1)
            attention(UA, CAUSAL, 64)
            project_out(u)
            norm_in()
            for kind in ("TT",) * 4 + ("RR",) * 4:
                proj(kind)
            attention(UB, CAUSAL, 128)
            project_out(u)
            norm_in()
            for kind in ("TT",) * 3 + ("RR",) * 4:
                proj(kind)
            attention(UC, CAUSAL, 256)
            project_out(u)
            norm_in()
            for kind in ("TT",) * 4 + ("RR",) * 4:
                proj(kind)
            pe.wait_ge(s_qkv, c.up("qkv"))
            bk = {}

            def stick_scores(i):
                bk[i] = acc("a")
                for j in range(2):
                    q, k = SH[2 * i + j]
                    nc.tensor.matmul(bk[i][j][:, 0:128], k[:, 128:256], q[:, 128:256], start=True, stop=False, skip_group_check=True)
                    last = nc.tensor.matmul(bk[i][j][:, 128:384], k[:, 0:128], q[:, 0:256], start=False, stop=False, skip_group_check=True)
                last.then_inc(acc_done, 1)

            def stick_values(i):
                b = obank()
                pe.wait_ge(s_am, i + 1)
                for j in range(2):
                    x = am[i % 2][:, j, :]
                    vs = slice(64 * (2 * i + j), 64 * (2 * i + j) + 64)
                    o0, o1 = b[:, 64 * j:64 * j + 64], b[:, 128 + 64 * j:192 + 64 * j]
                    nc.tensor.matmul(o1, x[:, 0:128], V[:, 1, vs], start=True, stop=False)
                    nc.tensor.matmul(o1, x[:, 256:384], V[:, 0, vs], start=False, stop=True)
                    last = nc.tensor.matmul(o0, x[:, 128:256], V[:, 0, vs], start=True, stop=True)
                last.then_inc(o_done, 1)

            stick_scores(0)
            stick_scores(1)
            for i in range(8):
                pe.wait_ge(s_lom, i + 1)
                for j in range(2):
                    l_, b = lom[i % 2][:, j, :], bk[i][j]
                    nc.tensor.matmul(b[:, 0:128], tri, l_[:, 0:128], start=False, stop=False, skip_group_check=True)
                    nc.tensor.matmul(b[:, 128:384], tri, l_[:, 128:384], start=False, stop=False, skip_group_check=True)
                    last = nc.tensor.matmul(b[:, 256:384], ones_, l_[:, 0:128], start=False, stop=True, skip_group_check=True)
                last.then_inc(s_cum, 1)
                if i >= 1:
                    stick_values(i - 1)
                if i + 2 < 8:
                    stick_scores(i + 2)
            stick_values(7)
            project_out(u, between=columns)

            norm_in()
            for n in (512, 512, 512, 416, 512, 512, 512, 512):
                proj("RR", n)
            pe.wait_ge(s_u, c.up("u"))
            transposes(NQ, CH[0:4])
            transposes(NK, CH[0:4])
            transposes(LAT, CH[0:3])
            pe.wait_ge(s_uT, c.up("uT"))
            s = slot()
            i = (c.w - 1) % RING
            c.win[i] += 16
            pe.wait_ge(w_in[i], c.win[i])
            wq = s[:, 0:1536].rearrange("p (c n) -> p c n", n=768)
            wkv = s[:, 1536:2560].rearrange("p (c n) -> p c n", n=1024)
            for t in range(T):
                a, b = acc("d")
                mm_R(a[:, 0:384], wq, t, 0, 384, kc=2)
                mm_R(b[:, 0:384], wq, t, 384, 384, kc=2).then_inc(acc_done, 1)
            for t in range(T):
                a, b = acc("d")
                mm_R(a[:, :], wkv, t, 0, 512, lhs=2, kc=1)
                mm_R(b[:, :], wkv, t, 512, 512, lhs=2, kc=1).then_inc(acc_done, 1)
            pe.wait_ge(s_u, c.up("u"))
            transposes(MQ, [(96 * k, 96) for k in range(8)])
            transposes(MK, [(96 * k, 96) for k in range(8)])
            attention(UN, FULL, 64)
            attention(UM, FULL, 64)
            for t in tile_transposes(ym):
                pass
            pe.wait_ge(s_uT, c.up("uT", 2))
            for k in range(2):
                w = slot()[:, :].rearrange("p (c n) -> p c n", n=1024)
                for t in range(T):
                    a, b = acc("d")
                    mm_R(a[:, :], w, t, 0, 512, lhs=4 * k, kc=4)
                    mm_R(b[:, :], w, t, 512, 512, lhs=4 * k, kc=4).then_inc(acc_done, 1)
            project_out(MG, mods=False)
            norm_in()
            a, b = acc("a")
            pe.wait_ge(s_rt, 32)
            mm_R(a[:, 0:64], wr, 0, 0, 64)
            mm_R(b[:, 0:64], wr, 1, 0, 64).then_inc(acc_done, 1)
            for k in ("tr", "o"):
                for i in range(2):
                    pe.wait_ge(*prev[k, i])
            pe.wait_ge(*prev["acc", 0])

            def gate_up(t, j):
                n = 0
                for d in range(DC):
                    for x, y in PARTS:
                        last = nc.tensor.matmul(banks[t][:, :], uT2[x][:, d, 128 * t:128 * t + 128], gu_[j][y][:, d, :],
                                                start=(n == 0), stop=(n == 3 * DC - 1))
                        n += 1
                last.then_inc(s_gu, 1)

            def act_T(e, t):
                pe.wait_ge(s_ga, 2 * e + t + 1)
                for f in range(2):
                    last = nc.tensor.transpose(banks[2 + t][:, 128 * f:128 * f + 128], ma[t][:, 128 * f:128 * f + 128], ident[:, :])
                last.then_inc(s_gat, 1)

            def down(e, t, j, stop=False, done=None):
                pe.wait_ge(s_al, 2 * e + t + 1)
                for f in range(2):
                    for k, (x, y) in enumerate(PARTS):
                        for n in range(2):
                            last = nc.tensor.matmul(banks[4 + 2 * t + n][:, :], ma2[t][x][:, 128 * f:128 * f + 128],
                                                    dn_[j][y][:, f, 512 * n:512 * n + 512], start=False,
                                                    stop=(stop and f == 1 and k == 2), skip_group_check=True)
                last.then_inc(done or s_dn, 1)

            pe.wait_ge(s_gl, 2)
            pe.wait_ge(s_ul, 1)
            gate_up(0, 0)
            gate_up(1, 0)
            pe.wait_ge(*prev["acc", 1])
            pe.wait_ge(s_r1, 1)
            for t in range(T):
                nc.tensor.matmul(banks[2][0:64, 0:1], rt[1][:, 64 * t:64 * t + 64], ones_[:, 0:1], start=(t == 0), stop=(t == 1))
            for t in range(T):
                last = nc.tensor.transpose(banks[3][0:64, 128 * t:128 * t + 128], gate[:, t, 0:64], ident[:, :])
            last.then_inc(s_aux, 1)
            pe.wait_ge(s_r2, 1)
            nc.tensor.matmul(banks[2][0:64, 1:2], cc("strict")[0:64, 0:64], active, start=True, stop=True)
            nc.tensor.matmul(banks[2][0:1, 2:3], active, ones_[0:64, 0:1], start=True, stop=True).then_inc(s_aux, 1)
            pe.wait_ge(s_r2, 2)
            nc.tensor.matmul(banks[2][0:1, 8:72], cc("row")[0:64, :], order, start=True, stop=True)
            for t in range(T):
                last = nc.tensor.matmul(banks[3][:, 64 * t:64 * t + 64], gT[:, 128 * t:128 * t + 128], order, start=True, stop=True)
            last.then_inc(s_aux, 1)
            pe.wait_ge(s_moe, 1)
            pairs = pe.value_load(todo[0:1, 64:65], min_val=TOPK // 2, max_val=EXPERTS // 2)
            for k in range(4):
                nc.tensor.matmul(banks[4 + k][:, :], zeros_[:, 0:128], zeros_[:, :], start=True, stop=False, skip_group_check=True)
            with pe.Fori(0, pairs) as it:
                for j in range(MOE_SLOTS):
                    g, nj = it * 2 + j, (j + 1) % 2
                    act_T(g, 0)
                    pe.wait_ge(s_gl, 2 * g + 4)
                    gate_up(0, nj)
                    pe.wait_ge(s_dl, g + 1)
                    down(g, 0, j)
                    act_T(g, 1)
                    gate_up(1, nj)
                    down(g, 1, j)
            g = pairs * 2
            act_T(g, 0)
            pe.wait_ge(s_dl, g + 1)
            down(g, 0, 0, stop=True)
            act_T(g, 1)
            down(g, 1, 0, stop=True, done=s_all)

        @block.scalar
        def _(act):
            c, me = Count(), Own(act, ach)
            act.dma_start(cst[:, :], A["shape_consts"]).then_inc(s_const, 16)
            act.dma_start(par[:, :], A["params"]).then_inc(s_const, 16)
            act.dma_start(posn[:, :], A["pos_cols"]).then_inc(s_const, 16)
            for v, n in enumerate(("a_cmp_w2_k", "a_cmp_w2_v")):
                act.dma_start(w2[:, v, :, :], A[n][0].rearrange("(c p) n -> p c n", p=P)).then_inc(s_small, 16)

            act.dma_start(lamb, row_bc(A["b_lambda"][0].rearrange("a b -> (a b)"), 256)).then_inc(s_lam, 16)
            act.dma_start(subg, row_bc(A["b_sub_gain"][0], 128)).then_inc(s_lam, 16)

            def gp(i):
                act.dma_start(gpost[:, :], row_bc(A["norm_post"][i], D)).then_inc(s_gpost, 16)

            def funcs(kind, *args):
                act.wait_ge(s_sq, c.up("sq"))
                kind(*args)

            def do_rstd(n, width, at=0):
                me.link(nc.scalar.activation(lnv[:, at:at + n], ssq[:, at:at + n], ACT.Ln, bias=epsc, scale=1.0 / width))
                nc.scalar.activation(rstd[:, at:at + n], lnv[:, at:at + n], ACT.Exp, scale=-0.5).then_inc(s_rstd, 1)

            def do_exp(dst, src, scale):
                nc.scalar.activation(dst, src, ACT.Exp, scale=scale).then_inc(s_rstd, 1)

            def do_sigmoid(dst, src, scale=1.0):
                nc.scalar.activation(dst, src, ACT.Sigmoid, scale=scale).then_inc(s_rstd, 1)

            def squares(src=h):
                for t in range(T):
                    act.wait_ge(s_sq, c.up("sq"))
                    tile_rstd(t, src[:, t, :])

            def tile_rstd(t, x):
                me.link(nc.scalar.activation(pT_[:, 0:D], x, ACT.Square, accum_out=ssq[:, t:t + 1]))
                me.link(nc.scalar.activation(lnv[:, t:t + 1], ssq[:, t:t + 1], ACT.Ln, bias=epsc, scale=1.0 / D))
                nc.scalar.activation(rstd[:, t:t + 1], lnv[:, t:t + 1], ACT.Exp, scale=-0.5).then_inc(s_rstd, 1)

            def input_high():
                for t in range(T):
                    act.wait_ge(s_sq, c.up("sq"))
                    nc.scalar.activation(in2[0][:, :, 128 * t:128 * t + 128], uT[:, :, 128 * t:128 * t + 128], ACT.Copy)\
                        .then_inc(s_rstd, 1)

            def w_high(n=1):
                for _ in range(n):
                    m = c.up("split") - 1
                    i, loads, _fill, size = SPLITS[m]
                    act.wait_ge(w_in[i], loads)
                    if m >= 2:
                        act.wait_ge(acc_done, SPLITS[m - 2][2])
                    for k in range(2):
                        x = slice(size // 2 * k, size // 2 * (k + 1))
                        nc.scalar.activation(w_hi[m % 2][:, x], ring[i][:, x], ACT.Copy).then_inc(s_wh, 1)

            def open_layer(n, after_input=None):
                squares()
                w_high()
                input_high()
                if after_input is not None:
                    after_input()
                w_high(n - 1)

            def closing_norm():
                c.acc += 2
                for t in range(T):
                    act.wait_ge(acc_done, c.acc + 1)
                    pair = c.acc % 2
                    tile_rstd(t, psum[:, 1024 * pair:1024 * pair + 1024])
                    c.acc += 1
                c.acc += 1

            def attention(units, blocks, dv, after_first=None):
                nb = 128 * len(blocks)

                def exps(n, un):
                    act.wait_ge(s_mx, c.up("mx"))
                    job = un[0]["job"]
                    for qt in (1, 0):
                        nk = 256 if (qt or blocks is FULL) else 128
                        for i in range(2):
                            x = probs[:, n % 2, qt, i, 0:nk]
                            last = nc.scalar.activation(x, x, ACT.Exp, bias=nm[:, qt, job + i:job + i + 1],
                                                        accum_out=rs[:, qt, job + i:job + i + 1])
                    last.then_inc(s_p, 1)

                def evac(n):
                    act.wait_ge(tr_done, c.tr + 1)
                    if c.o - 2 > 0:
                        act.wait_ge(o_done, c.o - 2)
                    nc.scalar.activation(probsT[:, 2 * (n % 2), 0:nb], banks[4 + c.tr % 2][:, 0:nb], ACT.Copy)\
                        .then_inc(free["ta", c.tr % 2], 1)
                    c.tr += 2
                    c.o += 2
                exps(0, units[0])
                if after_first is not None:
                    after_first()
                for n in range(len(units)):
                    evac(n)
                    if n + 1 < len(units):
                        exps(n + 1, units[n + 1])

            gp(0)
            def conditioning():
                funcs(do_sigmoid, siluc[:, 0:8], siluc[:, 8:16])
                act.wait_ge(s_sq, c.up("sq"))
                me.link(nc.scalar.activation(sinr, sinr, ACT.Sin))
                nc.scalar.activation(cosr, cosr, ACT.Sin).then_inc(s_rstd, 1)

            open_layer(5, conditioning)
            c.tr += 4
            funcs(do_sigmoid, gelu_t, gelu_t, 1.5957691216057308)
            w_high(2)
            for qt in range(2):
                funcs(do_exp, pc_[:, qt, :, 0:15], pc_[:, qt, :, 0:15], 1.0)
            w_high()
            funcs(do_sigmoid, u[:, :, :], z[:, :, :])
            funcs(do_sigmoid, gate[:, :, 0:48], gate[:, :, 0:48])
            c.tr += 2
            c.o += 4

            def load_mod():
                act.dma_start(mod[:, :], row_bc(A["b_ada_2"][0], 6 * D)).then_inc(s_row, 16)

            attention(UA, CAUSAL, 64, load_mod)
            c.acc = len(LA) + 3 + len(UA)
            closing_norm()
            c.tr += 4
            open_layer(len(LB))
            gp(1)
            c.tr += 4
            funcs(do_sigmoid, u[:, :, :], z[:, :, :])
            funcs(do_exp, lamc[:, 0:2], lamc[:, 0:2], 1.0)
            attention(UB, CAUSAL, 128)
            for t in range(T):
                funcs(do_rstd, 8, 128, 8 * t)
            c.acc = acc_B + len(LB) + len(UB)
            closing_norm()
            c.tr += 4
            open_layer(len(LC))
            gp(2)
            c.tr += 4
            funcs(do_sigmoid, u[:, :, :], z[:, :, :])
            attention(UC, CAUSAL, 256)
            funcs(do_exp, cf[:, :, 0:12], cf[:, :, 0:12], 1.0)
            c.acc = acc_C + len(LC) + len(UC)
            closing_norm()
            c.tr += 4
            open_layer(len(LD))
            gp(3)
            c.tr += 4
            c.acc = acc_before_D
            funcs(do_sigmoid, u[:, :, :], z[:, :, :])

            def softplus_parts(i):
                act.wait_ge(acc_done, acc_before_D + i + 1)
                me.link(nc.scalar.activation(sp_[i % 2], stick_pair(i), ACT.Abs))
                me.link(nc.scalar.activation(sp_[i % 2], sp_[i % 2], ACT.Exp, scale=-1.0))
                nc.scalar.activation(sp_[i % 2], sp_[i % 2], ACT.Ln, bias=onec).then_inc(s_abs, 1)

            softplus_parts(0)
            softplus_parts(1)
            for i in range(8):
                act.wait_ge(s_cum, i + 1)
                if i >= 2:
                    act.wait_ge(o_done, c.o + i - 1)
                nc.scalar.activation(am[i % 2], stick_pair(i), ACT.Exp).then_inc(free["a", (acc_before_D + i) % 2], 1)
                if i + 2 < 8:
                    softplus_parts(i + 2)
            c.o += 8
            c.acc = acc_before_D + 8
            closing_norm()
            c.tr += 4
            open_layer(6)
            c.tr += 4
            funcs(do_rstd, 16, 64)
            funcs(do_rstd, 16, 64)
            act.wait_ge(s_sq, c.up("sq"))
            for width, a in ((256, 0), (128, 2)):
                me.link(nc.scalar.activation(lnv[:, a:a + 2], ssq[:, a:a + 2], ACT.Ln, bias=epsc, scale=1.0 / width))
            nc.scalar.activation(rstd[:, 0:4], lnv[:, 0:4], ACT.Exp, scale=-0.5).then_inc(s_rstd, 1)
            w_high(2)
            act.wait_ge(s_attn, 4)
            rp = A["na_rpb_2"]
            for i in range(8):
                for r in range(4):
                    src = bass.AP(rp.tensor, rp.offset + 465 * i + 31 * (7 - r) - 48, [[1, 64], [31, 4], [1, 64]])
                    act.dma_start(bias[64 * (r % 2):64 * (r % 2) + 64, 8 * (r // 2) + i, :].rearrange("p (a b) -> p a b", a=4),
                                  src).then_inc(s_rpb, 16)
            funcs(do_sigmoid, z[:, :, :], z[:, :, :])
            funcs(do_sigmoid, u[:, :, :], u[:, :, :])
            c.tr += 6
            funcs(do_rstd, 16, 96)
            funcs(do_rstd, 16, 96)
            c.tr += 8
            attention(UN, FULL, 64)
            attention(UM, FULL, 64)
            act.wait_ge(s_attn, 5)
            act.dma_start(wr, A["w_router_2"][0].rearrange("(c p) n -> p c n", p=P)).then_inc(s_rt, 16)
            act.dma_start(ebias, row_bc(A["e_bias_2"][0], 64)).then_inc(s_rt, 16)
            c.tr += 8

            def gu_high(j, half, loads):
                act.wait_ge(gu_in[j], loads)
                nc.scalar.activation(gu_[j][0][:, 4 * half:4 * half + 4, :], guv[j][:, 4 * half:4 * half + 4, :], ACT.Copy)\
                    .then_inc(s_gh, 1)

            def dn_high(j, loads):
                act.wait_ge(dn_in[j], loads)
                nc.scalar.activation(dn_[j][0], dnv[j], ACT.Copy).then_inc(s_dh, 1)

            gu_high(0, 0, 32)
            gu_high(0, 1, 32)
            squares()
            act.wait_ge(s_sq, c.up("sq"))
            nc.scalar.activation(uT2[0], uT[:, :, :], ACT.Copy).then_inc(s_uh, 1)
            c.acc = acc_router
            act.wait_ge(acc_done, acc_router + 1)
            pair = acc_router % 2
            for t in range(T):
                last = nc.scalar.activation(gate[:, t, 0:64], banks[2 * pair + t][:, 0:64], ACT.Sigmoid)
            last.then_inc(free["a", pair], 1)

            def moe_exp(e, t):
                act.wait_ge(s_gu, 2 * e + t + 1)
                nc.scalar.activation(ge[t], banks[t][:, 0:FF], ACT.Sigmoid).then_inc(s_ge, 1)

            def moe_evac(e, t):
                act.wait_ge(s_gat, 2 * e + t + 1)
                nc.scalar.activation(ma2[t][0], banks[2 + t][:, 0:FF], ACT.Copy).then_inc(s_ah, 1)

            dn_high(0, 16)
            moe_exp(0, 0)
            moe_exp(0, 1)
            act.wait_ge(s_moe, 1)
            pairs = act.value_load(todo[0:1, 64:65], min_val=TOPK // 2, max_val=EXPERTS // 2)
            gu_high(1, 0, 32)
            gu_high(1, 1, 32)
            with act.Fori(0, pairs) as it:
                for j in range(MOE_SLOTS):
                    g = it * 2 + j
                    moe_evac(g, 0)
                    moe_exp(g + 1, 0)
                    gu_high(j, 0, 32 * it + 64)
                    moe_evac(g, 1)
                    gu_high(j, 1, 32 * it + 64)
                    dn_high(1 - j, 16 * it + (16 if j == 0 else 32))
                    moe_exp(g + 1, 1)
            moe_evac(pairs * 2, 0)
            moe_evac(pairs * 2, 1)

        @block.gpsimd
        def _(pool):
            c, me = Count(), Own(pool, pch)
            me.link(nc.gpsimd.memset(ident[:, :], 0.0))
            nc.gpsimd.affine_select(out=ident[:, :], in_=ident[:, :], compare_op=ALU.not_equal, fill=1.0, base=0,
                                    pattern=[[-1, P]], channel_multiplier=1).then_inc(s_id, 1)
            nc.gpsimd.memset(ones[:, :], 1.0).then_inc(s_id, 1)
            pool.wait_ge(s_const, 48)

            def alibi(sl, pattern):
                for i, x in enumerate(sl):
                    last = nc.gpsimd.tensor_scalar(bias[:, i, :], dist[:, pattern[i], :], -x, None, ALU.mult)
                last.then_inc(s_bias, 1)

            def first_low(i):
                m = FIRST[i]
                r, _loads, _fill, size = SPLITS[m]
                pool.wait_ge(s_wh, 2 * m + 1)
                x = slice(0, size // 2)
                nc.gpsimd.tensor_tensor(w_lo[r][:, x], ring[r][:, x], w_hi[m % 2][:, x], ALU.subtract).then_inc(s_wf, 1)

            first_low(0)
            pool.wait_ge(s_x, 1)
            for v, n in enumerate(("posk", "posv")):
                for l in range(16):
                    last = nc.gpsimd.tensor_scalar(Xp[:, v, l, :].rearrange("p (g n) -> p g n", g=4),
                                                   Xc[:, v, :, 2 * l:2 * l + 225:16], pc(n, l), None, ALU.add)
            last.then_inc(s_xp, 1)
            pool.wait_ge(acc_done, 4)
            alibi(slopes(16), [0] * 16)
            pool.wait_ge(s_attn, 1)
            alibi([x for x in slopes(8) for _ in range(2)], [0] * 16)
            first_low(1)
            pool.wait_ge(s_attn, 2)
            alibi(slopes(12), [1 + i // 4 for i in range(12)])
            first_low(2)
            first_low(3)
            for i in range(8):
                pair = (acc_before_D + i) % 2
                pool.wait_ge(free["a", pair], c.up(pair))
                for j in range(2):
                    x = am[i % 2][:, j, 0:256].rearrange("p (a b) -> p a b", a=2)
                    last = nc.gpsimd.affine_select(out=x, in_=x, compare_op=ALU.is_ge, fill=0.0, base=-1,
                                                   pattern=[[0, 2], [1, P]], channel_multiplier=-1)
                last.then_inc(s_am, 1)
            first_low(4)
            pool.wait_ge(s_rpb, 32 * 16)
            nc.gpsimd.tensor_tensor(bias[:, :, :], bias[:, :, :], mid_bc(cc("win"), 16), ALU.add).then_inc(s_bias, 1)
            for half in range(2):
                pool.wait_ge(s_gh, half + 1)
                x = slice(4 * half, 4 * half + 4)
                nc.gpsimd.tensor_tensor(gu_[0][1][:, x, :], guv[0][:, x, :], gu_[0][0][:, x, :], ALU.subtract).then_inc(s_gl, 1)
            pool.wait_ge(s_uh, 1)
            nc.gpsimd.tensor_tensor(uT2[1], uT[:, :, :], uT2[0], ALU.subtract).then_inc(s_ul, 1)

        @block.vector
        def _(dve):
            c, me = Count(), Own(dve, dch)
            v = nc.vector
            tick, own, link = me.tick, me.own, me.link

            def acc_in():
                i = c.acc % 2
                c.acc += 1
                dve.wait_ge(acc_done, c.acc)
                c.up(("d", i))
                return banks[2 * i], banks[2 * i + 1], free["d", i]

            def own_acc():
                i = (c.acc - 1) % 2
                dve.wait_ge(free["d", i], c.n["d", i])

            def act_does():
                dve.wait_ge(s_rstd, c.up("rstd"))

            def tr_in(dst, n, gains):
                for k in range(0, n, 2):
                    dve.wait_ge(tr_done, c.tr + 1)
                    b = banks[4 + c.tr % 2]
                    for j in range(min(2, n - k)):
                        w, s1, s2, op = gains(k + j)
                        last = v.tensor_scalar(dst[0:w, k + j, :], b[0:w, 256 * j:256 * j + 256], s1, s2, ALU.mult, op) \
                            if s2 is not None else v.tensor_scalar(dst[0:w, k + j, :], b[0:w, 256 * j:256 * j + 256], s1, None, ALU.mult)
                    last.then_inc(free["td", c.tr % 2], 1)
                    c.up(("td", c.tr % 2))
                    c.tr += 1

            def tr_own():
                i = (c.tr - 1) % 2
                dve.wait_ge(free["td", i], c.n["td", i])

            def uT_ready():
                tr_own()
                dve.sem_inc(s_uT, 1)

            def tile_in(dst, t, gains=None, ready=uT_ready):
                for k in range(0, DC, 4):
                    dve.wait_ge(tr_done, c.tr + 1)
                    b = banks[4 + c.tr % 2]
                    if gains is None:
                        last = v.tensor_copy(dst[:, k:k + 4, 128 * t:128 * t + 128], b.rearrange("p (j s) -> p j s", j=4))
                    else:
                        for j in range(4):
                            _w, s1, s2, op = gains(k + j)
                            x, y = dst[:, k + j, 128 * t:128 * t + 128], b[:, 128 * j:128 * j + 128]
                            last = v.tensor_scalar(x, y, s1, s2, ALU.mult, op) if s2 is not None else \
                                v.tensor_scalar(x, y, s1, None, ALU.mult)
                    last.then_inc(free["td", c.tr % 2], 1)
                    c.up(("td", c.tr % 2))
                    c.tr += 1
                ready()

            def uT_to_act():
                tr_own()
                dve.sem_inc(s_sq, 1)

            def w_low(n=1, half=None):
                for _ in range(n):
                    m = c.up("split") - 1
                    i, _loads, _fill, size = SPLITS[m]
                    for k in range(2) if half is None else [half]:
                        x = slice(size // 2 * k, size // 2 * (k + 1))
                        dve.wait_ge(s_wh, 2 * m + k + 1)
                        v.tensor_tensor(w_lo[i][:, x], ring[i][:, x], w_hi[m % 2][:, x], ALU.subtract).then_inc(s_wl, 1)

            def next_low():
                if c.n["split"] not in FIRST[1:] + [len(SPLITS)]:
                    w_low()

            def plain(k):
                return P, 1.0, None, None

            def norm_in(gains, between=None, parts=True, after_input=None):
                for t in range(T):
                    act_does()
                    v.tensor_scalar(u[:, t, :], h[:, t, :], rstd[:, t:t + 1], None, ALU.mult).then_inc(s_u, 1)
                if between is not None:
                    between()
                for t in range(T):
                    tile_in(uT, t, gains, uT_to_act if parts else uT_ready)
                if parts:
                    for t in range(T):
                        act_does()
                        x = slice(128 * t, 128 * t + 128)
                        v.tensor_tensor(in2[1][:, :, x], uT[:, :, x], in2[0][:, :, x], ALU.subtract).then_inc(s_uT, 1)
                    w_low(half=1)
                    if after_input is not None:
                        after_input()
                    w_low()

            def evac(dst0, dst1, n=512, scale=None):
                a, b, f = acc_in()
                for dst, x in ((dst0, a), (dst1, b)):
                    last = v.tensor_copy(dst, x[:, 0:n]) if scale is None else \
                        v.tensor_scalar(dst, x[:, 0:n], scale, None, ALU.mult)
                last.then_inc(f, 1)
                next_low()

            def flat(ap):
                return ap.rearrange("p a b -> p (a b)")

            def silu_z():
                own_acc()
                dve.sem_inc(s_sq, 1)

            def silu_end():
                act_does()
                link(v.tensor_tensor(z_[:, :], z_[:, :], u_[:, :], ALU.mult))

            def attention(units, blocks, dv, njobs, qkv=True):
                o = o_view(njobs, dv)
                nb = 128 * len(blocks)
                nk0 = 128 if blocks is CAUSAL else 256
                if qkv:
                    dve.sem_inc(s_qkv, 1)

                def soft(n, un):
                    a, b, f = acc_in()
                    if c.tr > 0:
                        dve.wait_ge(tr_done, c.tr)
                    job, bi = un[0]["job"], un[0]["b"]
                    d1 = probs[:, n % 2, 1, :, :]
                    d0 = probs[:, n % 2, 0, :, 0:nk0]
                    pair = psum[:, 1024 * ((c.acc - 1) % 2):1024 * ((c.acc - 1) % 2) + 1024].rearrange("p (i k) -> p i k", i=2)
                    a_, b_ = pair[:, :, 0:256], pair[:, :, 256:256 + nk0]
                    if bi is None:
                        v.tensor_copy(d1, a_)
                        v.tensor_copy(d0, b_).then_inc(f, 1)
                    else:
                        if blocks is CAUSAL:
                            v.tensor_tensor(d1, a_, bias[:, bi:bi + 2, :], ALU.add)
                            v.tensor_tensor(d0, b_, bias[:, bi:bi + 2, 128:256], ALU.add).then_inc(f, 1)
                        else:
                            for x, y, k in ((d1, a_, 8 + bi), (d0, b_, bi)):
                                for i in range(2):
                                    r3 = bias[:, k + i, :].rearrange("p (r c) -> p r c", c=64)
                                    rev = bass.AP(r3.tensor, r3.offset + 63, [r3.ap[0], [64, 4], [-1, 64]])
                                    last = v.tensor_tensor(x[:, i, :].rearrange("p (r c) -> p r c", c=64),
                                                           y[:, i, :].rearrange("p (r c) -> p r c", c=64), rev, ALU.add)
                            last.then_inc(f, 1)
                    own_acc()
                    v.tensor_reduce(nm[:, 1, job:job + 2], d1, AX.X, ALU.max, negate=True)
                    v.tensor_reduce(nm[:, 0, job:job + 2], d0, AX.X, ALU.max, negate=True).then_inc(s_mx, 1)

                def probs_T(n):
                    dve.wait_ge(tr_done, c.tr + 2)
                    i = (c.tr + 1) % 2
                    v.tensor_copy(probsT[:, 2 * (n % 2) + 1, 0:nb], banks[4 + i][:, 0:nb]).then_inc(free["td", i], 1)
                    c.up(("td", i))
                    c.tr += 2

                def values(un):
                    for i in range(2):
                        dve.wait_ge(o_done, c.o + 1)
                        ob_in(o[:, :, un[i]["job"], :], dv)
                soft(0, units[0])
                for n in range(len(units)):
                    if n + 1 < len(units):
                        soft(n + 1, units[n + 1])
                    probs_T(n)
                    if n >= 1:
                        values(units[n - 1])
                values(units[-1])
                own_o()

            def ob_in(dst, dv):
                i = c.o % 2
                v.tensor_copy(dst, banks[6 + i][:, 0:2 * dv].rearrange("p (t d) -> p t d", t=2)).then_inc(free["o", i], 1)
                c.up(("o", i))
                c.o += 1

            def own_o():
                for i in range(2):
                    dve.wait_ge(free["o", i], c.n["o", i])

            def osum(o, t, j, n):
                return o[:, t, j:j + n, :].rearrange("p j d -> p (j d)")

            def scaled(o, t, n, dv):
                link(v.tensor_tensor(o[:, t, :, :], o[:, t, :, :], last_bc(cf[:, t, 0:n], dv), ALU.mult))

            def mods(n):
                for _ in range(n):
                    a, b, f = acc_in()
                    x = mod[:, 512 * c.n.get("mod", 0):512 * c.n.get("mod", 0) + 512]
                    v.tensor_tensor(x, x, a[:, :], ALU.add).then_inc(f, 1)
                    c.up("mod")

            def project_out(i, combine):
                combine(0)
                dve.sem_inc(s_u, 1)
                mods(1)
                tile_in(uT, 0)
                combine(1)
                dve.sem_inc(s_u, 1)
                dve.sem_inc(s_attn, 1)
                mods(1)
                tile_in(uT, 1)
                dve.wait_ge(s_gpost, 16 * (i + 1))
                for t in range(T):
                    act_does()
                    pair = c.acc % 2
                    a, b, f = acc_in()
                    v.scalar_tensor_tensor(u[:, t, :], psum[:, 1024 * pair:1024 * pair + 1024], rstd[:, t:t + 1],
                                           gpost[:, :], ALU.mult, ALU.mult).then_inc(f, 1)
                    own_acc()
                    v.tensor_tensor(h[:, t, :], h[:, t, :], u[:, t, :], ALU.add).then_inc(s_sq, 1)

            def head_norms(x, nh, width, tiles=range(T), tmp=TMP):
                m = nh * width
                for t in tiles:
                    xt = x[:, t, 0:m]
                    link(v.tensor_tensor(tmp[:, 0:m], xt, xt, ALU.mult))
                    link(v.tensor_reduce(ssq[:, nh * t:nh * t + nh], tmp[:, 0:m].rearrange("p (a b) -> p a b", a=nh), AX.X, ALU.add))
                dve.sem_inc(s_sq, 1)
                act_does()
                for t in tiles:
                    xt = x[:, t, 0:m].rearrange("p (a b) -> p a b", a=nh)
                    tick(v.tensor_tensor(xt, xt, last_bc(rstd[:, nh * t:nh * t + nh], width), ALU.mult))
                own()

            for x, val in ((epsc, EPS), (onec, 1.0), (rs[:, :, 0:16], 1.0)):
                tick(v.memset(x, val))
            dve.wait_ge(s_const, 48)
            own()
            dve.wait_ge(s_h, 16)
            for _ in range(T):
                dve.sem_inc(s_sq, 1)

            def conditioning():
                cpar = par[:, PC["c"][0]:PC["c"][1]]
                v.tensor_copy(siluc[:, 8:16], cpar).then_inc(s_sq, 1)
                act_does()
                link(v.tensor_tensor(siluc[:, 0:8], siluc[:, 0:8], cpar, ALU.mult))
                dve.sem_inc(s_u, 1)
                posf = lamc[:, 0:2]
                link(v.tensor_copy(posf, posn[:, :]))
                magic = 1.5 * 2.0 ** 23
                two_pi = 2.0 * math.pi
                c1 = float(np.float32(np.round(two_pi * 2 ** 7) / 2 ** 7))
                c2 = float(np.float32(np.round((two_pi - c1) * 2 ** 20) / 2 ** 20))
                c3 = float(np.float32(two_pi - c1 - c2))
                turn = gelu_x[:, 0:32]
                ang = gelu_x[:, 32:64]
                for t in range(T):
                    tick(v.tensor_scalar(ang[:, 16 * t:16 * t + 16], cc("freq"), posf[:, t:t + 1], None, ALU.mult))
                own()
                for dst, shift in ((sinr, 0.0), (cosr, 0.25)):
                    link(v.tensor_scalar(turn, ang, 1.0 / two_pi, shift, ALU.mult, ALU.add))
                    link(v.tensor_scalar(turn, turn, magic, None, ALU.add))
                    link(v.tensor_scalar(turn, turn, magic, None, ALU.subtract))
                    link(v.scalar_tensor_tensor(dst, turn, -c1, ang, ALU.mult, ALU.add))
                    link(v.scalar_tensor_tensor(dst, turn, -c2, dst, ALU.mult, ALU.add))
                    link(v.scalar_tensor_tensor(dst, turn, -c3, dst, ALU.mult, ALU.add))
                    if shift:
                        link(v.tensor_scalar(dst, dst, math.pi / 2, None, ALU.add))
                    link(v.tensor_scalar(dst, dst, 3.1415925, -3.1415925, ALU.min, ALU.max))
                dve.sem_inc(s_sq, 1)
                act_does()

            norm_in(lambda k: (P, pc("pre", k), None, None), after_input=conditioning)
            def keys_values(br):
                a, b, f = acc_in()
                y = a[:, :].rearrange("p (f s) -> p f s", f=2)
                for r in range(2):
                    for r2 in range(2):
                        g0 = 8 + 4 * br + r
                        v.tensor_copy(QK[64 * r2:64 * r2 + 64, g0:g0 + 3:2, :], y[64 * r:64 * r + 64, :, :])
                v.tensor_copy(V[:, :, 256 * br:256 * br + 256], b[:, :].rearrange("p (t n) -> p t n", t=2)).then_inc(f, 1)
                next_low()

            a, b, f = acc_in()
            for vi, bk in ((0, a), (1, b)):
                y = bk[:, :].rearrange("p (f s) -> p f s", f=2)
                for r in range(2):
                    v.tensor_copy(Xc[0:64, vi, r:r + 3:2, :], y[64 * r:64 * r + 64, :, :])
                    last = v.tensor_copy(Xc[64:128, vi, r:r + 3:2, 0:255], y[64 * r:64 * r + 64, :, 1:256])
            last.then_inc(f, 1)
            own_acc()
            dve.sem_inc(s_x, 1)
            next_low()
            for j in range(2):
                evac(flat(QK[:, 4 * j:4 * j + 2, :]), flat(QK[:, 4 * j + 2:4 * j + 4, :]), scale=0.125)
            a, b, f = acc_in()
            for vi, bk in ((0, a), (1, b)):
                last = v.tensor_copy(hid[:, 2 * vi:2 * vi + 2, :], bk[:, 0:128].rearrange("p (f n) -> p f n", f=2)[:, :, 0:60])
            last.then_inc(f, 1)
            own_acc()
            link(v.tensor_tensor(gelu_t, gelu_x, gelu_x, ALU.mult))
            link(v.tensor_scalar(gelu_t, gelu_t, 0.044715, 1.0, ALU.mult, ALU.add))
            v.tensor_tensor(gelu_t, gelu_t, gelu_x, ALU.mult).then_inc(s_sq, 1)
            act_does()
            v.tensor_tensor(gelu_x, gelu_x, gelu_t, ALU.mult).then_inc(s_hid, 1)
            tick(v.memset(mod[:, 0:2048], 0.0))
            own()
            keys_values(0)
            a, b, f = acc_in()
            for r in range(2):
                v.tensor_copy(kcT[64 * r:64 * r + 64, 0:60], a[0:64, 0:60])
            for r in range(4):
                last = v.tensor_copy(vd[32 * r:32 * r + 15, :, 64 * r:64 * r + 64], b[0:15, 0:256].rearrange("p (g n) -> p g n", g=4))
            last.then_inc(f, 1)
            own_acc()
            dve.sem_inc(s_hid, 1)
            keys_values(1)
            a, b, f = acc_in()
            cbias = cc("cbias").rearrange("p (t h n) -> p t h n", t=2, n=15)
            cmask = cc("cmask").rearrange("p (t n) -> p t n", t=2)
            for t in range(T):
                for r, bk in ((0, a), (1, b)):
                    last = v.tensor_tensor(pc_[:, t, r:16:2, 0:15],
                                           bk[:, 128 * t:128 * t + 128].rearrange("p (h n) -> p h n", n=16)[:, :, 0:15],
                                           cbias[:, t, r:16:2, :], ALU.add)
            last.then_inc(f, 1)
            own_acc()
            for t in range(T):
                link(v.tensor_reduce(ssq, pc_[:, t, :, 0:15], AX.X, ALU.max))
                v.tensor_tensor(pc_[:, t, :, 0:15], pc_[:, t, :, 0:15], last_bc(ssq, 15), ALU.subtract).then_inc(s_sq, 1)
                act_does()
                link(v.tensor_tensor(pc_[:, t, :, 0:15], pc_[:, t, :, 0:15], mid_bc(cmask[:, t, :], 16), ALU.mult))
                link(v.tensor_reduce(ssq, pc_[:, t, :, 0:15], AX.X, ALU.add))
                link(v.tensor_scalar(ssq, ssq, 1e-30, None, ALU.max))
                link(v.reciprocal(ssq, ssq))
                link(v.tensor_tensor(pc_[:, t, :, 0:15], pc_[:, t, :, 0:15], last_bc(ssq, 15), ALU.mult))
            dve.sem_inc(s_hid, 1)
            for j in range(2):
                evac(z[:, 0, 512 * j:512 * j + 512], z[:, 1, 512 * j:512 * j + 512])
            silu_z()
            evac(gate[:, 0, 0:48], gate[:, 1, 0:48], n=48)
            own_acc()
            dve.sem_inc(s_sq, 1)
            silu_end()
            act_does()
            for k in range(2):
                dve.wait_ge(tr_done, c.tr + 1)
                i = c.tr % 2
                v.tensor_copy(flat(pcT[:, 4 * k:4 * k + 4, :]), banks[4 + i][:, :]).then_inc(free["td", i], 1)
                c.up(("td", i))
                c.tr += 1
            oA = o_view(48, 64)
            for g in range(4):
                dve.wait_ge(o_done, c.o + 1)
                i = c.o % 2
                v.tensor_copy(oA[:, :, 4 * g:4 * g + 4, :], banks[6 + i][:, :].rearrange("p (t j d) -> p t j d", t=2, j=4))\
                    .then_inc(free["o", i], 1)
                c.up(("o", i))
                c.o += 1
            dve.wait_ge(s_bias, 1)
            attention(UA, CAUSAL, 64, 48)
            def combine_A(t):
                link(v.reciprocal(cf[:, t, 0:48], rs[:, t, 0:48]))
                link(v.tensor_tensor(cf[:, t, 0:48], cf[:, t, 0:48], gate[:, t, 0:48], ALU.mult))
                scaled(oA, t, 48, 64)
                link(v.tensor_tensor(u[:, t, :], osum(oA, t, 0, 16), osum(oA, t, 16, 16), ALU.add))
                link(v.tensor_tensor(u[:, t, :], u[:, t, :], osum(oA, t, 32, 16), ALU.add))
                link(v.tensor_tensor(u[:, t, :], u[:, t, :], z[:, t, :], ALU.mult))

            dve.wait_ge(s_row, 16)
            project_out(0, combine_A)

            def qkv(nq, nk):
                for j in range(nq + nk):
                    a, b, f = acc_in()
                    for x, t0 in ((a, 4 * j), (b, 4 * j + 2)):
                        for y in range(2):
                            last = v.tensor_scalar(QK[:, t0 + y, :], x[:, 256 * y:256 * y + 256],
                                                   0.125 if t0 + y < 2 * (nq + nk) else 1.0, None, ALU.mult)
                    last.then_inc(f, 1)
                    next_low()
                for dst in (V, z):
                    for j in range(2):
                        evac(dst[:, 0, 512 * j:512 * j + 512], dst[:, 1, 512 * j:512 * j + 512])
                silu_z()
                silu_end()

            norm_in(lambda k: (P, pc("pre", DC + k), None, None), lambda: mods(1))
            qkv(2, 2)
            lam_init = 0.8 - 0.6 * math.exp(-0.3 * 1)
            dve.wait_ge(s_lam, 32)
            l4 = lamb.rearrange("p (a b) -> p a b", b=64)
            link(v.tensor_tensor(TMP[:, 0:128].rearrange("p (a b) -> p a b", a=2), l4[:, 0:3:2, :], l4[:, 1:4:2, :], ALU.mult))
            link(v.tensor_reduce(lamc[:, 0:2], TMP[:, 0:128].rearrange("p (a b) -> p a b", a=2), AX.X, ALU.add))
            dve.sem_inc(s_sq, 1)
            act_does()
            link(v.tensor_tensor(lamc[:, 2:3], lamc[:, 1:2], lamc[:, 0:1], ALU.subtract))
            link(v.tensor_scalar(lamc[:, 2:3], lamc[:, 2:3], -lam_init, None, ALU.add))
            dve.wait_ge(s_bias, 2)
            attention(UB, CAUSAL, 128, 16)
            oB = o_view(16, 128)

            def combine_B(t):
                link(v.reciprocal(cf[:, t, 0:16], rs[:, t, 0:16]))
                odd = cf[:, t, 1:16:2]
                link(v.tensor_scalar(odd, odd, lamc[:, 2:3], None, ALU.mult))
                scaled(oB, t, 16, 128)
                pairs = oB[:, t, :, :].rearrange("p (a m) d -> p m a d", m=2)
                ut = u[:, t, :].rearrange("p (a d) -> p a d", d=128)
                link(v.tensor_tensor(ut, pairs[:, 0, :, :], pairs[:, 1, :, :], ALU.add))
                head_norms(u, 8, 128, [t])
                link(v.scalar_tensor_tensor(ut, ut, 1.0 - lam_init, mid_bc(subg, 8), ALU.mult, ALU.mult))
                link(v.tensor_tensor(u[:, t, :], u[:, t, :], z[:, t, :], ALU.mult))

            project_out(1, combine_B)

            norm_in(lambda k: (P, pc("pre", 2 * DC + k), None, None), lambda: mods(1))
            qkv(1, 2)
            dve.wait_ge(s_bias, 3)
            attention(UC, CAUSAL, 256, 12)
            M4 = ssq[:, 0:8].rearrange("p (t h) -> p t h", t=2)
            link(v.tensor_tensor(M4, nm[:, :, 0:4], nm[:, :, 4:8], ALU.min))
            link(v.tensor_tensor(M4, M4, nm[:, :, 8:12], ALU.min))
            for g in range(3):
                tick(v.tensor_tensor(cf[:, :, 4 * g:4 * g + 4], M4, nm[:, :, 4 * g:4 * g + 4], ALU.subtract))
            own()
            dve.sem_inc(s_sq, 1)
            act_does()
            link(v.tensor_tensor(rs[:, :, 0:12], rs[:, :, 0:12], cf[:, :, 0:12], ALU.mult))
            link(v.tensor_tensor(M4, rs[:, :, 0:4], rs[:, :, 4:8], ALU.add))
            link(v.tensor_tensor(M4, M4, rs[:, :, 8:12], ALU.add))
            link(v.reciprocal(M4, M4))
            for g in range(3):
                tick(v.tensor_tensor(cf[:, :, 4 * g:4 * g + 4], cf[:, :, 4 * g:4 * g + 4], M4, ALU.mult))
            own()
            oC = o_view(12, 256)

            def combine_C(t):
                scaled(oC, t, 12, 256)
                link(v.tensor_tensor(u[:, t, :], osum(oC, t, 0, 4), osum(oC, t, 4, 4), ALU.add))
                link(v.tensor_tensor(u[:, t, :], u[:, t, :], osum(oC, t, 8, 4), ALU.add))
                link(v.tensor_tensor(u[:, t, :], u[:, t, :], z[:, t, :], ALU.mult))

            project_out(2, combine_C)

            norm_in(lambda k: (P, pc("pre", 3 * DC + k), None, None), lambda: mods(1))
            qkv(2, 2)
            dve.sem_inc(s_qkv, 1)
            oD = o_view(16, 64)
            for i in range(9):
                if i < 8:
                    dve.wait_ge(s_abs, i + 1)
                    link(v.scalar_tensor_tensor(lom[i % 2], stick_pair(i), 0.0, sp_[i % 2], ALU.max, ALU.add))
                    v.tensor_tensor(lom[i % 2][:, :, 0:256], lom[i % 2][:, :, 0:256], mid_bc(cc("strict"), 2), ALU.mult)
                    v.tensor_scalar(lom[i % 2][:, :, 256:384], lom[i % 2][:, :, 256:384], -1.0, None, ALU.mult).then_inc(s_lom, 1)
                if i >= 1:
                    dve.wait_ge(o_done, c.o + 1)
                    k = c.o % 2
                    v.tensor_copy(oD[:, :, 2 * i - 2:2 * i, :],
                                  banks[6 + k][:, 0:256].rearrange("p (t j d) -> p t j d", t=2, j=2)).then_inc(free["o", k], 1)
                    c.up(("o", k))
                    c.o += 1
            own_o()
            c.acc += 8

            def combine_D(t):
                link(v.tensor_tensor(u[:, t, :], osum(oD, t, 0, 16), z[:, t, :], ALU.mult))

            project_out(3, combine_D)

            def modulation_columns():
                a, b, f = acc_in()
                v.tensor_copy(modc, a[:, 0:32]).then_inc(f, 1)
                own_acc()
                for k, n in ((0, "g1"), (1, "g2")):
                    link(v.tensor_scalar(gs[:, 8 * k:8 * k + 8], modc[:, 16 * k + 8:16 * k + 16], 1.0, None, ALU.add))
                    link(v.tensor_tensor(gs[:, 8 * k:8 * k + 8], gs[:, 8 * k:8 * k + 8], par[:, PC[n][0]:PC[n][1]], ALU.mult))
                mods(1)

            norm_in(lambda k: (P, gs[:, k:k + 1], modc[:, k:k + 1], ALU.add), modulation_columns)
            for dst in (NQ, NK):
                evac(dst[:, 0, :], dst[:, 1, :])
            evac(V[:, 0, 0:512], V[:, 1, 0:512])
            evac(LAT[:, 0, :], LAT[:, 1, :], n=416)
            own_acc()
            head_norms(NQ, 8, 64, tmp=QK_)
            head_norms(NK, 8, 64, tmp=QK_)
            for a, n, at in ((0, 256, 0), (256, 128, 2)):
                for t in range(T):
                    x = LAT[:, t, a:a + n]
                    link(v.tensor_tensor(QK_[:, 0:n], x, x, ALU.mult))
                    link(v.tensor_reduce(ssq[:, at + t:at + t + 1], QK_[:, 0:n], AX.X, ALU.add))
            dve.sem_inc(s_sq, 1)
            act_does()
            for a, n, at in ((0, 256, 0), (256, 128, 2)):
                for t in range(T):
                    tick(v.tensor_scalar(LAT[:, t, a:a + n], LAT[:, t, a:a + n], rstd[:, at + t:at + t + 1], None, ALU.mult))
            own()
            for dst in (z, u):
                for j in range(2):
                    evac(dst[:, 0, 512 * j:512 * j + 512], dst[:, 1, 512 * j:512 * j + 512])
            own_acc()
            for _ in range(2):
                dve.sem_inc(s_sq, 1)
            dve.sem_inc(s_u, 1)
            tr_in(QK[:, 0:4, :], 4, lambda k: (P, pc("naq"), 0.125, ALU.mult))
            tr_in(QK[:, 4:8, :], 4, lambda k: (P, pc("nak"), None, None))
            tr_in(uT, 3, lambda k: (P, pc("qlat", k) if k < 2 else pc("kvlat"), None, None))
            uT_ready()
            for _ in range(2):
                act_does()
            cos2 = cosr.rearrange("p (t n) -> p t n", t=2)
            sin2 = sinr.rearrange("p (t n) -> p t n", t=2)

            def rope(dst, x, nh):
                for t in range(T):
                    x1, x2 = x[t][:, :, 0:16], x[t][:, :, 16:32]
                    co, si = mid_bc(cos2[:, t, :], nh), mid_bc(sin2[:, t, :], nh)
                    y = [TMP[:, 128 * k:128 * k + 16 * nh].rearrange("p (h n) -> p h n", h=nh) for k in range(4)]
                    for d, p_, q_ in ((0, x1, co), (1, x2, si), (2, x2, co), (3, x1, si)):
                        tick(v.tensor_tensor(y[d], p_, q_, ALU.mult))
                    own()
                    tick(v.tensor_tensor(dst[t][:, :, 0:16], y[0], y[1], ALU.subtract))
                    tick(v.tensor_tensor(dst[t][:, :, 16:32], y[2], y[3], ALU.add))
                    own()
            rope([KR[:, t:t + 1, :] for t in range(T)],
                 [LAT[:, t, 384:416].rearrange("p (h n) -> p h n", h=1) for t in range(T)], 1)
            for t in range(T):
                evac(MQ[:, t, 0:384], MQ[:, t, 384:768], n=384)
            for t in range(T):
                a, b, f = acc_in()
                for j, bk in ((0, a), (1, b)):
                    y = bk[:, :].rearrange("p (h n) -> p h n", n=128)
                    v.tensor_copy(MK[:, t, 384 * j:384 * j + 384].rearrange("p (h n) -> p h n", n=96)[:, :, 0:64], y[:, :, 0:64])
                    last = v.tensor_copy(V[:, t, 512 + 256 * j:768 + 256 * j].rearrange("p (h n) -> p h n", n=64), y[:, :, 64:128])
                last.then_inc(f, 1)
            own_acc()
            for t in range(T):
                tick(v.tensor_copy(MK[:, t, :].rearrange("p (h n) -> p h n", n=96)[:, :, 64:96], mid_bc(KR[:, t, :], 8)))
            qr = [MQ[:, t, :].rearrange("p (h n) -> p h n", n=96)[:, :, 64:96] for t in range(T)]
            rope(qr, qr, 8)
            head_norms(MQ, 8, 96)
            head_norms(MK, 8, 96)
            dve.sem_inc(s_u, 1)
            tr_in(QK[:, 8:16, :], 8, lambda k: (96, pc("mlaq", 0, 96), 96 ** -0.5, ALU.mult))
            tr_in(uT, 8, lambda k: (96, pc("mlak", 0, 96), None, None))
            tr_own()
            dve.wait_ge(s_bias, 4)
            attention(UN, FULL, 64, 16)
            attention(UM, FULL, 64, 16)
            oN = o_view(16, 64)
            for t in range(T):
                link(v.reciprocal(cf[:, t, 0:16], rs[:, t, 0:16]))
                link(v.tensor_tensor(ym[:, t, :].rearrange("p (j d) -> p j d", d=64), oN[:, t, :, :], last_bc(cf[:, t, 0:16], 64), ALU.mult))
                dve.sem_inc(s_u, 1)
            dve.sem_inc(s_attn, 1)
            for t in range(T):
                tile_in(uT, t)
            for t in range(T):
                a, b, f = acc_in()
                v.tensor_tensor(MG[:, t, 0:512], a[:, :], z[:, t, 0:512], ALU.mult)
                v.tensor_tensor(MG[:, t, 512:1024], b[:, :], z[:, t, 512:1024], ALU.mult).then_inc(f, 1)
            for t in range(T):
                a, b, f = acc_in()
                v.tensor_tensor(MG2[:, t, 0:512], a[:, :], u[:, t, 0:512], ALU.mult)
                v.tensor_tensor(MG2[:, t, 512:1024], b[:, :], u[:, t, 512:1024], ALU.mult).then_inc(f, 1)
                own_acc()
                v.tensor_tensor(MG[:, t, :], MG[:, t, :], MG2[:, t, :], ALU.add).then_inc(s_u, 1)
            for t in range(T):
                tile_in(uT, t)
            for t in range(T):
                pair = c.acc % 2
                a, b, f = acc_in()
                v.tensor_tensor(u[:, t, :], psum[:, 1024 * pair:1024 * pair + 1024], mod[:, 2 * D:3 * D], ALU.mult).then_inc(f, 1)
                own_acc()
                v.tensor_tensor(h[:, t, :], h[:, t, :], u[:, t, :], ALU.add).then_inc(s_sq, 1)
            norm_in(lambda k: (P, gs[:, 8 + k:9 + k], modc[:, 16 + k:17 + k], ALU.add), parts=False)
            dve.sem_inc(s_sq, 1)

            pair = acc_router % 2
            dve.wait_ge(free["a", pair], 8 // 2 + 1)
            sc = gate[:, :, 0:64]
            sel, rep, m8, tmp = rt[0], rt[1], rt[2], rt[3]
            for t in range(T):
                tick(v.tensor_tensor(sel[:, 64 * t:64 * t + 64], sc[:, t, :], ebias, ALU.add))
            own()
            for g in range(16):
                tick(v.max(m8[:, 8 * g:8 * g + 8], sel[:, 8 * g:8 * g + 8]))
            own()
            m83 = m8.rearrange("p (g k) -> p g k", k=8)
            gsc, rk, wsum = rt[4][:, 0:16], rt[4][:, 16:32], rt[4][:, 32:34]
            link(v.tensor_tensor(gsc, m83[:, :, 0], m83[:, :, 1], ALU.add))
            for t in range(T):
                gi = last_bc(gsc[:, 8 * t:8 * t + 8], 8)
                gj = mid_bc(gsc[:, 8 * t:8 * t + 8], 8)
                x, y = rank[:, 0:64].rearrange("p (i j) -> p i j", i=8), rank[:, 64:128].rearrange("p (i j) -> p i j", i=8)
                tick(v.tensor_tensor(x, gj, gi, ALU.is_gt))
                link(v.tensor_tensor(y, gj, gi, ALU.is_equal))
                link(v.tensor_tensor(y, y, cc("lower").rearrange("p (i j) -> p i j", i=8), ALU.mult))
                link(v.tensor_tensor(x, x, y, ALU.add))
                link(v.tensor_reduce(rk[:, 8 * t:8 * t + 8], x, AX.X, ALU.add))
            link(v.tensor_scalar(rk, rk, 3.5, None, ALU.is_lt))
            s3 = sel.rearrange("p (g k) -> p g k", k=8)
            link(v.tensor_tensor(s3, s3, last_bc(rk, 8), ALU.mult))
            link(v.tensor_scalar(rk, rk, 1.0, BIG, ALU.subtract, ALU.mult))
            link(v.tensor_tensor(s3, s3, last_bc(rk, 8), ALU.add))
            for t in range(T):
                link(v.max(m8[:, 8 * t:8 * t + 8], sel[:, 64 * t:64 * t + 64]))
                link(v.match_replace(rep[:, 64 * t:64 * t + 64], m8[:, 8 * t:8 * t + 8], sel[:, 64 * t:64 * t + 64], -2 * BIG))
            link(v.tensor_scalar(rep, rep, -1.5 * BIG, None, ALU.is_lt))
            for t in range(T):
                link(v.tensor_tensor(sc[:, t, :], sc[:, t, :], rep[:, 64 * t:64 * t + 64], ALU.mult))
                link(v.tensor_reduce(wsum[:, t:t + 1], sc[:, t, :], AX.X, ALU.add))
            link(v.reciprocal(wsum, wsum))
            for t in range(T):
                link(v.tensor_scalar(sc[:, t, :], sc[:, t, :], wsum[:, t:t + 1], ROUTED_SCALE, ALU.mult, ALU.mult))
            dve.sem_inc(s_r1, 1)
            dve.wait_ge(s_aux, 1)
            link(v.tensor_scalar(active, banks[2][0:64, 0:1], 0.5, None, ALU.is_gt))
            link(v.tensor_copy(gT, banks[3][0:64, 0:256]))
            dve.sem_inc(s_r2, 1)
            dve.wait_ge(s_aux, 2)
            link(v.tensor_copy(rankc, banks[2][0:64, 1:2]))
            link(v.tensor_scalar(order, cc("negiota")[0:64, :], rankc, active, ALU.is_equal, ALU.mult))
            link(v.tensor_scalar(todo[0:1, 64:65], banks[2][0:1, 2:3], 0.5, 0.25, ALU.mult, ALU.add))
            dve.sem_inc(s_r2, 1)
            dve.wait_ge(s_aux, 3)
            tick(v.tensor_copy(todo[0:1, 0:64], banks[2][0:1, 8:72]))
            tick(v.tensor_copy(gate[:, :, 1:65], banks[3][:, 0:128].rearrange("p (t n) -> p t n", t=2)))
            tick(v.memset(zeros_, 0.0))
            own()
            tick(v.memset(gate[:, :, 0:1], 1.0))
            own()
            dve.sem_inc(s_moe, 1)

            def gu_low(g, j, half):
                dve.wait_ge(s_gh, 2 * g + half + 1)
                x = slice(4 * half, 4 * half + 4)
                v.tensor_tensor(gu_[j][1][:, x, :], guv[j][:, x, :], gu_[j][0][:, x, :], ALU.subtract).then_inc(s_gl, 1)

            def dn_low(g, j):
                dve.wait_ge(s_dh, g + 1)
                v.tensor_tensor(dn_[j][1], dnv[j], dn_[j][0], ALU.subtract).then_inc(s_dl, 1)

            def act_low(g, t):
                dve.wait_ge(s_ah, 2 * g + t + 1)
                v.tensor_tensor(ma2[t][1], banks[2 + t][:, 0:FF], ma2[t][0], ALU.subtract).then_inc(s_al, 1)

            for t in range(T):
                dve.wait_ge(s_ge, t + 1)
                link(v.tensor_tensor(ge[t], ge[t], banks[t][:, 0:FF], ALU.mult))
                v.scalar_tensor_tensor(ma[t], ge[t], gate[:, t, 0:1], banks[t][:, FF:2 * FF], ALU.mult, ALU.mult).then_inc(s_ga, 1)
            pairs = dve.value_load(todo[0:1, 64:65], min_val=TOPK // 2, max_val=EXPERTS // 2)
            dn_low(0, 0)
            gu_low(1, 1, 0)
            gu_low(1, 1, 1)
            with dve.Fori(0, pairs) as it:
                dve.wait_ge(s_ga, 4 * it + 2)
                v.tensor_copy(gcur[:, :, 0:2], gate[:, :, bass.ds(it * 2 + 1, 2)]).then_inc(s_gc, 1)
                dve.wait_ge(s_gc, it + 1)
                for j in range(MOE_SLOTS):
                    g = it * 2 + j

                    def gated(t):
                        n0 = it * 4 + 2 * j + t
                        dve.wait_ge(s_ge, n0 + 3)
                        v.tensor_tensor(ge[t], ge[t], banks[t][:, 0:FF], ALU.mult).then_inc(s_mc, 1)
                        dve.wait_ge(s_mc, n0 + 1)
                        dve.wait_ge(s_gat, n0 + 1)
                        v.scalar_tensor_tensor(ma[t], ge[t], gcur[:, t, j:j + 1], banks[t][:, FF:2 * FF],
                                               ALU.mult, ALU.mult).then_inc(s_ga, 1)

                    act_low(g, 0)
                    gated(0)
                    gu_low(g + 2, j, 0)
                    act_low(g, 1)
                    gu_low(g + 2, j, 1)
                    dn_low(g + 1, 1 - j)
                    gated(1)
            act_low(pairs * 2, 0)
            act_low(pairs * 2, 1)
            dve.wait_ge(s_all, 1)
            for t in range(T):
                for n in range(2):
                    tick(v.tensor_tensor(u[:, t, 512 * n:512 * n + 512], banks[4 + 2 * t + n][:, :],
                                         mod[:, 5 * D + 512 * n:5 * D + 512 * n + 512], ALU.mult))
            own()
            v.tensor_tensor(u_[:, :], u_[:, :], h_[:, :], ALU.add).then_inc(s_fin, 1)


_WEIGHTS = ["x", "norm_post", "a_w_in", "a_w_out", "a_cmp_w1_k", "a_cmp_w2_k", "a_cmp_w1_v", "a_cmp_w2_v", "b_w_in",
            "b_w_out", "b_lambda", "b_sub_gain", "c_w_in", "c_w_out", "d_w_in", "d_w_out", "w_ada_2", "b_ada_2",
            "w_in_2", "na_rpb_2", "w_uq_2", "w_ukv_2", "w_proj_na_2", "w_proj_mla_2", "w_out_2", "w_router_2",
            "e_bias_2", "w_exp_gate_2", "w_exp_up_2", "w_exp_down_2", "w_sh_gate_2", "w_sh_up_2", "w_sh_down_2"]


def kernel(**inputs):
    import concourse.bacc as _bacc
    from concourse import mybir as _mybir
    from concourse.bass_utils import run_bass_kernel_spmd as _run

    def cols(a, k):
        return np.asarray(a).reshape(k, P).T

    f = {k: np.asarray(x) for k, x in inputs.items()}
    par = np.zeros((P, PC_N), np.float32)

    def put(name, a):
        par[0:a.shape[0], PC[name][0]:PC[name][1]] = a
    put("pre", cols(f["norm_pre"].reshape(-1), 4 * DC))
    put("g1", cols(f["g_norm1_2"], DC))
    put("g2", cols(f["g_norm2_2"], DC))
    put("c", cols(f["c_2"], DC))
    put("naq", np.concatenate([f["g_na_q_2"][0]] * 2)[:, None])
    put("nak", np.concatenate([f["g_na_k_2"][0]] * 2)[:, None])
    put("qlat", cols(f["g_q_lat_2"], 2))
    put("kvlat", cols(f["g_kv_lat_2"], 1))
    put("mlaq", f["g_mla_q_2"][0][:, None])
    put("mlak", f["g_mla_k_2"][0][:, None])
    put("posk", cols(f["a_cmp_pos_k"], 16))
    put("posv", cols(f["a_cmp_pos_v"], 16))
    nc = _bacc.Bacc("TRN2", target_bir_lowering=False, num_devices=1)
    given = {n: f[n] for n in _WEIGHTS}
    given["params"] = par
    given["shape_consts"] = shape_constants()
    given["na_rpb_2"] = f["na_rpb_2"][..., ::-1]
    given["pos_cols"] = f["positions_2"].reshape(T, P).T
    arrays, aps = {}, {}
    for n, a in given.items():
        a = np.ascontiguousarray(a)
        arrays[f"in_{n}"] = a
        aps[n] = nc.dram_tensor(f"in_{n}", a.shape, _mybir.dt.from_np(a.dtype), kind="ExternalInput").ap()
    out = nc.dram_tensor("out_x", (1, S, D), _mybir.dt.float32, kind="ExternalOutput").ap()
    build(nc, aps, out)
    r = _run(nc, [arrays], core_ids=[0])
    return r.results[0]["out_x"]
```
